# Optimizing a Trainium2 kernel written in Bass

```python
import jax, jax.numpy as jnp
from jax import lax
import numpy as np

D_MODEL = 1024
BATCH = 1
SEQ = 512
DEPTH = 1

MEM_LEN = 256
DN_ALPHA = (2 * DEPTH) ** 0.25
DN_BETA = (8 * DEPTH) ** -0.25
LN_EPS = 1e-5
NEG = -1e30
FORCE = 1e9

RET_HEADS = 4
RET_DIM = D_MODEL // 2 // RET_HEADS
RET_CHUNK = 128
RET_ROPE_BASE = 10000.0

NSA_HEADS = 8
NSA_KV_GROUPS = 2
NSA_HPG = NSA_HEADS // NSA_KV_GROUPS
NSA_DIM = D_MODEL // 2 // NSA_HEADS
CMP_LEN = 32
CMP_STRIDE = 16
CMP_HIDDEN = 256
SEL_LEN = 64
SEL_TOPK = 16
WIN = 512
Q_BLOCK = 128
ROPE_THETA = 500000.0
ROPE_DIMS = NSA_DIM // 4

RET_WIDTH = RET_HEADS * RET_DIM
NSA_WIDTH = NSA_HEADS * NSA_DIM
MIX_WIDTH = RET_WIDTH + NSA_WIDTH
KV_WIDTH = NSA_KV_GROUPS * NSA_DIM
IN_SIZES = [RET_WIDTH] * 4 + [NSA_WIDTH] + [KV_WIDTH] * 6 + [3 * NSA_HEADS]
IN_COLS = sum(IN_SIZES)

XATT_HEADS = 4
XATT_DIM = D_MODEL // XATT_HEADS

N_EXPERTS = 64
TOP_K = 8
N_GROUPS = 8
TOPK_GROUPS = 4
EXPERT_FF = 256
SHARED_FF = 256
ROUTED_SCALE = 2.5
MOE_BLOCK = 128

kernel_name = 'hymba_retnet_nsa_deepnorm_moe'

def layer_norm(x, g, b):
    xf = x.astype(jnp.float32)
    mu = xf.mean(-1, keepdims=True)
    var = jnp.square(xf - mu).mean(-1, keepdims=True)
    return ((xf - mu) * lax.rsqrt(var + LN_EPS) * g + b).astype(x.dtype)

def rotary(x, pos, n_rot, base):
    half = n_rot // 2
    inv = base ** (-jnp.arange(half, dtype=jnp.float32) / half)
    ang = pos.astype(jnp.float32)[..., None] * inv
    cos = jnp.cos(ang)[:, :, None, :]
    sin = jnp.sin(ang)[:, :, None, :]
    x1 = x[..., :half].astype(jnp.float32)
    x2 = x[..., half:n_rot].astype(jnp.float32)
    out = jnp.concatenate([x1 * cos - x2 * sin, x2 * cos + x1 * sin,
                           x[..., n_rot:].astype(jnp.float32)], axis=-1)
    return out.astype(x.dtype)

def retention(q, k, v, pos):
    B, T, H, dh = q.shape
    C = RET_CHUNK
    nc = T // C
    q = rotary(q, pos, dh, RET_ROPE_BASE)
    k = rotary(k, pos, dh, RET_ROPE_BASE) * (dh ** -0.5)

    def chunks(a):
        return a.reshape(B, nc, C, H, dh).transpose(0, 3, 1, 2, 4)

    qc, kc, vc = chunks(q), chunks(k), chunks(v)
    log_g = jnp.log(1.0 - 2.0 ** (-5.0 - jnp.arange(H, dtype=jnp.float32)))
    idx = jnp.arange(C, dtype=jnp.float32)
    rel = idx[:, None] - idx[None, :]
    dmask = jnp.where(rel >= 0, jnp.exp(log_g[:, None, None] * jnp.maximum(rel, 0.0)), 0.0)
    scores = jnp.einsum('bhncd,bhnmd->bhncm', qc, kc) * dmask[:, None]
    inner = jnp.einsum('bhncm,bhnme->bhnce', scores, vc)
    zeta = jnp.exp(log_g[:, None] * (C - 1.0 - idx))
    xi = jnp.exp(log_g[:, None] * (idx + 1.0))
    chunk_decay = jnp.exp(log_g * C)[:, None, None]
    kv = jnp.einsum('bhncd,bhnce->nbhde', kc * zeta[:, None, :, None], vc).astype(jnp.float32)

    def step(state, kv_n):
        return state * chunk_decay + kv_n, state

    _, prev = lax.scan(step, jnp.zeros(kv.shape[1:], jnp.float32), kv)
    cross = jnp.einsum('bhncd,nbhde->bhnce', qc, prev) * xi[:, None, :, None]
    o = (inner + cross).astype(jnp.float32).transpose(0, 2, 3, 1, 4).reshape(B, T, H, dh)
    mu = o.mean(-1, keepdims=True)
    var = jnp.square(o - mu).mean(-1, keepdims=True)
    o = (o - mu) * lax.rsqrt(var + LN_EPS)
    return o.reshape(B, T, H * dh)

def native_sparse_attention(q, kc, vc, ks, vs, kw, vw, gates, pos,
                            cmp_pe_k, cmp_pe_v, cmp_w1_k, cmp_w2_k, cmp_w1_v, cmp_w2_v):
    B, T, H, dh = q.shape
    G, hpg = NSA_KV_GROUPS, NSA_HPG
    scale = dh ** -0.5
    q_rot = rotary(q, pos, ROPE_DIMS, ROPE_THETA)
    ks = rotary(ks, pos, ROPE_DIMS, ROPE_THETA)
    kw = rotary(kw, pos, ROPE_DIMS, ROPE_THETA)

    n_cmp = (T - CMP_LEN) // CMP_STRIDE + 1
    blk = jnp.arange(n_cmp)[:, None] * CMP_STRIDE + jnp.arange(CMP_LEN)[None, :]

    def compress(a, pe, w1, w2):
        ab = a[:, blk] + pe[None, None, :, None, :]
        ab = ab.transpose(0, 1, 3, 2, 4).reshape(B, n_cmp, G, CMP_LEN * dh)
        return jax.nn.silu(ab @ w1) @ w2

    k_cmp = compress(kc, cmp_pe_k, cmp_w1_k, cmp_w2_k)
    v_cmp = compress(vc, cmp_pe_v, cmp_w1_v, cmp_w2_v)
    cmp_start = jnp.arange(n_cmp) * CMP_STRIDE
    cmp_last = cmp_start + CMP_LEN - 1

    n_sel = T // SEL_LEN
    n_top = min(SEL_TOPK, n_sel)
    ks_b = ks.reshape(B, n_sel, SEL_LEN, G, dh).transpose(0, 3, 1, 2, 4)
    vs_b = vs.reshape(B, n_sel, SEL_LEN, G, dh).transpose(0, 3, 1, 2, 4)
    sel_start = jnp.arange(n_sel) * SEL_LEN
    overlap = ((cmp_start[:, None] < sel_start[None, :] + SEL_LEN)
               & (cmp_start[:, None] + CMP_LEN > sel_start[None, :])).astype(jnp.float32)
    gather = jax.vmap(jax.vmap(lambda tab, ix: tab[ix]))

    kw_p = jnp.pad(kw, ((0, 0), (WIN, 0), (0, 0), (0, 0)))
    vw_p = jnp.pad(vw, ((0, 0), (WIN, 0), (0, 0), (0, 0)))

    nqb = T // Q_BLOCK

    def to_blocks(a):
        return a.reshape((B, nqb, Q_BLOCK) + a.shape[2:]).swapaxes(0, 1)

    q_g = q.reshape(B, T, G, hpg, dh)
    qr_g = q_rot.reshape(B, T, G, hpg, dh)
    g_g = jax.nn.sigmoid(gates).reshape(B, T, G, hpg, 3)
    j_sel = jnp.arange(n_sel)

    def block_fn(args):
        i, qb, qrb, gb = args
        t = i * Q_BLOCK + jnp.arange(Q_BLOCK)
        s_c = jnp.einsum('bqghd,bcgd->bghqc', qb, k_cmp).astype(jnp.float32) * scale
        valid_c = cmp_last[None, :] <= t[:, None]
        p_c = jnp.where(valid_c, jax.nn.softmax(jnp.where(valid_c, s_c, NEG), axis=-1), 0.0)
        o_c = jnp.einsum('bghqc,bcgd->bqghd', p_c, v_cmp)
        imp = jnp.einsum('bghqc,cs->bgqs', p_c, overlap)
        cur = t // SEL_LEN
        forced = (j_sel[None] == 0) | (j_sel[None] == cur[:, None]) | (j_sel[None] == cur[:, None] - 1)
        imp = jnp.where(forced, FORCE, imp)
        imp = jnp.where(j_sel[None] <= cur[:, None], imp, NEG)
        _, sel = lax.top_k(imp, n_top)
        k_sel = gather(ks_b, sel)
        v_sel = gather(vs_b, sel)
        kpos = sel[..., None] * SEL_LEN + jnp.arange(SEL_LEN)
        m_s = (kpos <= t[:, None, None])[:, :, None]
        s_s = jnp.einsum('bqghd,bgqnld->bghqnl', qrb, k_sel).astype(jnp.float32) * scale
        s_s = jnp.where(m_s, s_s, NEG)
        p_s = jax.nn.softmax(s_s.reshape(B, G, hpg, Q_BLOCK, n_top * SEL_LEN), axis=-1)
        p_s = p_s.reshape(B, G, hpg, Q_BLOCK, n_top, SEL_LEN)
        o_s = jnp.einsum('bghqnl,bgqnld->bqghd', p_s, v_sel)
        start = i * Q_BLOCK
        k_win = lax.dynamic_slice_in_dim(kw_p, start, WIN + Q_BLOCK, axis=1)
        v_win = lax.dynamic_slice_in_dim(vw_p, start, WIN + Q_BLOCK, axis=1)
        wpos = start - WIN + jnp.arange(WIN + Q_BLOCK)
        diff = t[:, None] - wpos[None, :]
        m_w = (wpos[None, :] >= 0) & (diff >= 0) & (diff < WIN)
        s_w = jnp.einsum('bqghd,bkgd->bghqk', qrb, k_win).astype(jnp.float32) * scale
        p_w = jax.nn.softmax(jnp.where(m_w, s_w, NEG), axis=-1)
        o_w = jnp.einsum('bghqk,bkgd->bqghd', p_w, v_win)
        o = gb[..., 0:1] * o_c + gb[..., 1:2] * o_s + gb[..., 2:3] * o_w
        return o.reshape(B, Q_BLOCK, H * dh)

    out = lax.map(block_fn, (jnp.arange(nqb), to_blocks(q_g), to_blocks(qr_g), to_blocks(g_g)))
    return out.swapaxes(0, 1).reshape(B, T, H * dh)

def memory_cross_attention(x, mem, w_xq, w_xkv, w_xo):
    B, T, D = x.shape
    q = (x @ w_xq).reshape(B, T, XATT_HEADS, XATT_DIM)
    k, v = jnp.split(mem @ w_xkv, 2, axis=-1)
    k = k.reshape(B, -1, XATT_HEADS, XATT_DIM)
    v = v.reshape(B, -1, XATT_HEADS, XATT_DIM)
    s = jnp.einsum('bthd,bmhd->bhtm', q, k).astype(jnp.float32) * (XATT_DIM ** -0.5)
    p = jax.nn.softmax(s, axis=-1)
    o = jnp.einsum('bhtm,bmhd->bthd', p, v).reshape(B, T, D)
    return o @ w_xo

def moe(x, w_router, router_bias, w_gate, w_up, w_down, ws_gate, ws_up, ws_down):
    B, T, D = x.shape
    xf = x.reshape(-1, D)
    N = xf.shape[0]
    E = N_EXPERTS
    scores = jax.nn.sigmoid((xf @ w_router).astype(jnp.float32))
    biased = scores + router_bias.astype(jnp.float32)
    group_score = lax.top_k(biased.reshape(N, N_GROUPS, E // N_GROUPS), 2)[0].sum(-1)
    kth = lax.top_k(group_score, TOPK_GROUPS)[0][:, -1:]
    expert_ok = jnp.repeat(group_score >= kth, E // N_GROUPS, axis=1)
    _, top_e = lax.top_k(jnp.where(expert_ok, biased, NEG), TOP_K)
    w = jnp.take_along_axis(scores, top_e, axis=-1)
    w = w / w.sum(-1, keepdims=True) * ROUTED_SCALE
    flat_e = top_e.reshape(-1)
    flat_tok = jnp.repeat(jnp.arange(N, dtype=jnp.int32), TOP_K)
    flat_w = w.reshape(-1)
    order = jnp.argsort(flat_e)
    e_sorted = flat_e[order]
    counts = jnp.bincount(flat_e, length=E)
    starts = jnp.cumsum(counts) - counts
    padded = (counts + MOE_BLOCK - 1) // MOE_BLOCK * MOE_BLOCK
    pad_ends = jnp.cumsum(padded)
    pad_starts = pad_ends - padded
    dest = pad_starts[e_sorted] + (jnp.arange(N * TOP_K) - starts[e_sorted])
    cap = N * TOP_K + E * MOE_BLOCK
    n_blocks = cap // MOE_BLOCK
    slot_tok = jnp.zeros((cap,), jnp.int32).at[dest].set(flat_tok[order])
    slot_w = jnp.zeros((cap,), jnp.float32).at[dest].set(flat_w[order])
    block_e = jnp.minimum(jnp.searchsorted(pad_ends, jnp.arange(n_blocks) * MOE_BLOCK, side='right'), E - 1)

    def body(acc, blk):
        tok, wt, e = blk
        h = xf[tok]
        y = (jax.nn.silu(h @ w_gate[e]) * (h @ w_up[e])) @ w_down[e]
        return acc.at[tok].add(y.astype(jnp.float32) * wt[:, None]), None

    routed, _ = lax.scan(body, jnp.zeros((N, D), jnp.float32),
                         (slot_tok.reshape(n_blocks, MOE_BLOCK), slot_w.reshape(n_blocks, MOE_BLOCK), block_e))
    shared = (jax.nn.silu(xf @ ws_gate) * (xf @ ws_up)) @ ws_down
    return (routed + shared).reshape(B, T, D)

def hybrid_layer(x, mem, positions, w_in, cmp_pe_k, cmp_pe_v, cmp_w1_k, cmp_w2_k, cmp_w1_v, cmp_w2_v,
                 w_out, ln1_g, ln1_b, w_xq, w_xkv, w_xo, ln2_g, ln2_b, w_router, router_bias,
                 w_gate, w_up, w_down, ws_gate, ws_up, ws_down, ln3_g, ln3_b):
    B, T, _ = x.shape
    h = x @ w_in
    (rq, rk, rv, rg, nq, nkc, nvc, nks, nvs, nkw, nvw, ngate) = jnp.split(
        h, list(np.cumsum(IN_SIZES)[:-1]), axis=-1)
    o_ret = retention(rq.reshape(B, T, RET_HEADS, RET_DIM), rk.reshape(B, T, RET_HEADS, RET_DIM),
                      rv.reshape(B, T, RET_HEADS, RET_DIM), positions)
    o_ret = jax.nn.silu(rg) * o_ret
    kvs = lambda a: a.reshape(B, T, NSA_KV_GROUPS, NSA_DIM)
    o_nsa = native_sparse_attention(nq.reshape(B, T, NSA_HEADS, NSA_DIM), kvs(nkc), kvs(nvc), kvs(nks),
                                    kvs(nvs), kvs(nkw), kvs(nvw), ngate, positions,
                                    cmp_pe_k, cmp_pe_v, cmp_w1_k, cmp_w2_k, cmp_w1_v, cmp_w2_v)
    mix = jnp.concatenate([o_ret.astype(x.dtype), o_nsa.astype(x.dtype)], axis=-1) @ w_out
    x = layer_norm(DN_ALPHA * x + mix, ln1_g, ln1_b)
    x = layer_norm(DN_ALPHA * x + memory_cross_attention(x, mem, w_xq, w_xkv, w_xo), ln2_g, ln2_b)
    y = moe(x, w_router, router_bias, w_gate, w_up, w_down, ws_gate, ws_up, ws_down)
    x = layer_norm(DN_ALPHA * x + y.astype(x.dtype), ln3_g, ln3_b)
    return x

def setup_inputs(seed: int = 0) -> dict:
    key = jax.random.key(seed)
    ks = jax.random.split(key, 32)
    L, D = DEPTH, D_MODEL
    nrm = lambda k, shape, s: jax.random.normal(k, shape, jnp.float32) * s
    return {
        'x': nrm(ks[0], (BATCH, SEQ, D), 1.0),
        'mem': nrm(ks[1], (BATCH, MEM_LEN, D), 1.0),
        'positions': (jnp.arange(SEQ, dtype=jnp.int32)[None, :]
                      + jax.random.randint(ks[2], (BATCH, 1), 0, 1024, dtype=jnp.int32)),
        'w_in': nrm(ks[3], (L, D, IN_COLS), D ** -0.5),
        'cmp_pe_k': nrm(ks[4], (L, CMP_LEN, NSA_DIM), 0.1),
        'cmp_pe_v': nrm(ks[5], (L, CMP_LEN, NSA_DIM), 0.1),
        'cmp_w1_k': nrm(ks[6], (L, CMP_LEN * NSA_DIM, CMP_HIDDEN), (CMP_LEN * NSA_DIM) ** -0.5),
        'cmp_w2_k': nrm(ks[7], (L, CMP_HIDDEN, NSA_DIM), CMP_HIDDEN ** -0.5),
        'cmp_w1_v': nrm(ks[8], (L, CMP_LEN * NSA_DIM, CMP_HIDDEN), (CMP_LEN * NSA_DIM) ** -0.5),
        'cmp_w2_v': nrm(ks[9], (L, CMP_HIDDEN, NSA_DIM), CMP_HIDDEN ** -0.5),
        'w_out': nrm(ks[10], (L, MIX_WIDTH, D), DN_BETA * MIX_WIDTH ** -0.5),
        'ln1_g': 1.0 + nrm(ks[11], (L, D), 0.02),
        'ln1_b': nrm(ks[12], (L, D), 0.02),
        'w_xq': nrm(ks[13], (L, D, D), D ** -0.5),
        'w_xkv': nrm(ks[14], (L, D, 2 * D), D ** -0.5),
        'w_xo': nrm(ks[15], (L, D, D), DN_BETA * D ** -0.5),
        'ln2_g': 1.0 + nrm(ks[16], (L, D), 0.02),
        'ln2_b': nrm(ks[17], (L, D), 0.02),
        'w_router': nrm(ks[18], (L, D, N_EXPERTS), D ** -0.5),
        'router_bias': nrm(ks[19], (L, N_EXPERTS), 0.01),
        'w_gate': nrm(ks[20], (L, N_EXPERTS, D, EXPERT_FF), D ** -0.5),
        'w_up': nrm(ks[21], (L, N_EXPERTS, D, EXPERT_FF), D ** -0.5),
        'w_down': nrm(ks[22], (L, N_EXPERTS, EXPERT_FF, D), DN_BETA * EXPERT_FF ** -0.5),
        'ws_gate': nrm(ks[23], (L, D, SHARED_FF), D ** -0.5),
        'ws_up': nrm(ks[24], (L, D, SHARED_FF), D ** -0.5),
        'ws_down': nrm(ks[25], (L, SHARED_FF, D), DN_BETA * SHARED_FF ** -0.5),
        'ln3_g': 1.0 + nrm(ks[26], (L, D), 0.02),
        'ln3_b': nrm(ks[27], (L, D), 0.02),
    }

def reference(x, mem, positions, w_in, cmp_pe_k, cmp_pe_v, cmp_w1_k, cmp_w2_k, cmp_w1_v, cmp_w2_v,
              w_out, ln1_g, ln1_b, w_xq, w_xkv, w_xo, ln2_g, ln2_b, w_router, router_bias,
              w_gate, w_up, w_down, ws_gate, ws_up, ws_down, ln3_g, ln3_b):
    for l in range(DEPTH):
        x = hybrid_layer(x, mem, positions, w_in[l], cmp_pe_k[l], cmp_pe_v[l], cmp_w1_k[l], cmp_w2_k[l],
                         cmp_w1_v[l], cmp_w2_v[l], w_out[l], ln1_g[l], ln1_b[l], w_xq[l], w_xkv[l],
                         w_xo[l], ln2_g[l], ln2_b[l], w_router[l], router_bias[l], w_gate[l], w_up[l],
                         w_down[l], ws_gate[l], ws_up[l], ws_down[l], ln3_g[l], ln3_b[l])
    return x


_drawn_inputs = setup_inputs


def setup_inputs(seed=0):
    import zlib

    import numpy as np

    out = dict(_drawn_inputs(seed))
    spreads = {}
    factors = {'cmp_pe_k': 8.0, 'ln3_g': 2.806, 'ln3_b': 3.118}
    for name, (base, spread) in spreads.items():
        noise = np.random.default_rng([zlib.crc32(name.encode()), seed]).standard_normal(out[name].shape)
        drawn = base * np.exp(spread * noise) if base else spread * noise
        out[name] = __import__('jax').numpy.asarray(drawn.astype(out[name].dtype))
    for name, factor in factors.items():
        out[name] = (out[name] * factor).astype(out[name].dtype)
    return out
```

```python
from contextlib import ExitStack

import numpy as np

import concourse.bass as bass
from concourse import mybir

F32 = mybir.dt.float32
BF16 = mybir.dt.bfloat16
I32 = mybir.dt.int32
U32 = mybir.dt.uint32
ALU = mybir.AluOpType
ACT = mybir.ActivationFunctionType
AX = mybir.AxisListType
DS = bass.DynSlice

P = 128
T = 512
D = 1024
TT = T // P
KD = D // P
MEM = 256
ALPHA = 2.0 ** 0.25
EPS = 1e-5
NEG = -1e30

RH, RD = 4, 128
NH, NG, ND = 8, 2, 64
HPG = NH // NG
NCMP, CMP_LEN, CMP_STRIDE, CMP_HID = 31, 32, 16, 256
RROT, NROT = RD // 2, 8
NFREQ = RROT + NROT
XH = 4

NE, TOPK, GROUPS, TOPG, FF = 64, 8, 8, 4, 256
EPG = NE // GROUPS
SCALE_W = 2.5
BLK = 128
MAX_EXTRA = T * TOPK // BLK - 1
EXTRA = 40
ITEMS = NE + EXTRA
FAR = 1.0e6
OOB = 8192.0

C_ID, C_CAUS, C_INV, C_EPS = 0, 128, 256, 256 + NFREQ
NC_A = C_EPS + 4
NC_B = TT * NCMP * 2
R_TRI, R_ONE, R_IOTA, R_TRI64, R_TOK = 0, 128, 256, 384, 448
NC_R = R_TOK + 2 * TT


def constants():
    p = np.arange(P)
    a = np.zeros((P, NC_A), np.float32)
    a[:, C_ID:C_ID + P] = np.eye(P)
    a[:, C_CAUS:C_CAUS + P] = np.where(p[None, :] <= p[:, None], 0.0, NEG)
    inv_r = 10000.0 ** (-np.arange(RROT) / RROT)
    inv_n = 500000.0 ** (-np.arange(NROT) / NROT)
    a[:, C_INV:C_INV + NFREQ] = np.concatenate([inv_r, inv_n])[None, :]
    a[:, C_EPS] = EPS
    t = np.arange(TT)[None, :, None] * P + p[:, None, None]
    ok = CMP_STRIDE * np.arange(NCMP)[None, None, :] + CMP_LEN - 1 <= t
    b = np.stack([ok.astype(np.float32), np.where(ok, 0.0, NEG)], 1).reshape(P, -1).astype(np.float32)
    decay = np.zeros((P, RH, T), np.float64)
    rel = np.arange(T)[None, :] - p[:, None]
    for h in range(RH):
        decay[:, h] = np.where(rel >= 0, np.exp(np.log(1 - 2.0 ** (-5 - h)) * np.maximum(rel, 0)), 0) * RD ** -0.5
    r = np.zeros((P, NC_R), np.float32)
    r[:, R_TRI:R_TRI + P] = p[:, None] < p[None, :]
    r[:, R_ONE:R_ONE + P] = 1.0
    r[:, R_IOTA:R_IOTA + P] = p[None, :]
    e = np.arange(NE)
    r[:NE, R_TRI64:R_TRI64 + NE] = e[:, None] <= e[None, :]
    r[:, R_TOK:R_TOK + TT] = p[:, None]
    r[:, R_TOK + TT:R_TOK + 2 * TT] = np.arange(TT)[None, :] * P - OOB
    return {"c_first": a, "c_cmp": b, "c_decay": decay.reshape(P, -1).astype(np.float32), "c_route": r}


class Units:

    def __init__(self, names):
        self.at = {name: n for n, name in enumerate(names)}
        self.n = len(names)

    def no(self, *name):
        return self.at[name if len(name) > 1 else name[0]]


W_COLS = [512] * 6 + [280]
PROJ = Units([("in", c, t) for c in range(7) for t in range(TT)]
             + [("xk", d) for d in range(KD)] + [("xv", m, n) for n in range(2) for m in range(2)]
             + [("out", t, n) for t in range(TT) for n in range(2)]
             + [("xq", d) for d in range(KD)]
             + [("xo", t, n) for t in range(TT) for n in range(2)]
             + [("sgu", t) for t in range(TT)] + [("sdn", t, n) for t in range(TT) for n in range(2)])
ATT = [(pr, h, br, q) for pr in range(NH // 2) for h in (2 * pr, 2 * pr + 1) for br in range(2) for q in range(TT)]
TRAN = Units([("x", t, j) for t in range(TT) for j in range(2)]
             + [("ret", c, t) for c in range(2) for t in range(TT)]
             + [("oret", t) for t in range(TT)]
             + [("nq", t, j) for t in range(TT) for j in range(2)]
             + [("kv5", t, j) for t in range(TT) for j in range(2)]
             + [("kv6", t) for t in range(TT)]
             + [("hid", j) for j in range(2)]
             + [("mem", m, j) for m in range(2) for j in range(2)]
             + [("pc", t) for t in range(TT)]
             + [("pt", n) for n in range(len(ATT))]
             + [("x1", t, j) for t in range(TT) for j in range(2)]
             + [("px", h, t) for h in range(XH) for t in range(TT)]
             + [("x2", t, j) for t in range(TT) for j in range(2)]
             + [("sh", t) for t in range(TT)])
SCORE = Units([("ret", h, k) for h in range(RH) for k in range(TT)]
              + [("hid", j) for j in range(2)] + [("kvc", 0)]
              + [("sc", t, a) for t in range(TT) for a in range(2)]
              + [("att", n) for n in range(len(ATT))]
              + [("x", h, t) for h in range(XH) for t in range(TT)]
              + [("logit", 0), ("pos", 0), ("extra", 0), ("cum", 0), ("item", 0)])
OUTP = Units([("ret", h) for h in range(RH)] + [("nsa", pr) for pr in range(NH // 2)]
             + [("x", h, d) for h in range(XH) for d in range(2)])

CHUNKS = ([("in", c) for c in range(7)] + [("w1", 0), ("w1", 1)] + [("xkv", c) for c in range(4)]
          + [("out", 0), ("out", 1), ("xq", 0), ("xq", 1), ("xo", 0), ("xo", 1), ("sgu", 0), ("sdn", 0)])
SLOT = [n % 4 for n in range(len(CHUNKS))]
SLOT[-1] = 2
CHUNK_NO = {name: n for n, name in enumerate(CHUNKS)}


def loads_before(n):
    return sum(SLOT[m] == SLOT[n] for m in range(n + 1))


def last_in_slot(slot, before):
    found = [m for m in range(before) if SLOT[m] == slot]
    return found[-1] if found else None


def build(nc, io, out):
    ctx = ExitStack()
    base = (nc.sbuf_base + 31) // 32 * 32
    KB = 1024

    def at(name, shape, dt, offset):
        return nc.alloc_sbuf_tensor_at(name, shape, dt, offset=base + offset)

    def sem(name):
        return ctx.enter_context(nc.semaphore(name))

    O_RING, O_DOWN, O_X, O_A, O_B, O_C, O_D, O_E, O_F = (k * KB for k in (0, 64, 96, 112, 128, 144, 160, 176, 200))
    ring = [at(f"ring{s}", [P, 4096], F32, O_RING + s * 16 * KB) for s in range(4)]
    xres = at("xres", [P, TT, D], F32, O_X)
    xT = at("xT", [P, KD, T], F32, O_A)
    nqT = at("nqT", [P, NH // 2, T], F32, O_DOWN)
    nqrT = at("nqrT", [P, NH // 2, T], F32, O_DOWN + 8 * KB)
    kselT = at("kselT", [P, NG, T], F32, O_DOWN + 16 * KB)
    kwinT = at("kwinT", [P, NG, T], F32, O_DOWN + 20 * KB)
    mem_in = at("mem_in", [P, 2, D], F32, O_DOWN + 24 * KB)
    retT = [at(f"ret{n}T", [P, RH, T], F32, O_C + k * 8 * KB) for k, n in enumerate("qk")]
    rv = at("rv", [P, TT, RH * RD], F32, O_D)
    swish = at("swish", [P, TT, RH * RD], F32, O_D + 8 * KB)
    decay = at("decay", [P, RH, T], F32, O_E)
    retS = at("retS", [P, TT, T], F32, O_E + 8 * KB)
    oret = at("oret", [P, TT, RH * RD], F32, O_E + 16 * KB)
    mixT = at("mixT", [P, KD, T], F32, O_B)
    ang = at("ang", [P, TT, NFREQ], F32, O_B)
    turns = at("turns", [P, 2, TT, NFREQ], F32, O_B + 2 * KB)
    stage = [at(f"stage{b}", [P, D], F32, O_B + (8 + 4 * b) * KB) for b in range(2)]
    kvcT = at("kvcT", [P, 4, T], F32, O_D)
    ab = at("ab", [P, 2, 16, NG, NCMP], F32, O_D + 8 * KB)
    w2k = at("w2k", [P, 2, 2, ND], F32, O_C)
    w2v = at("w2v", [P, 2, ND], F32, O_C + 1024)
    hid = at("hid", [NG * NCMP, 2, CMP_HID], F32, O_C + 1536)
    hidkT = at("hidkT", [P, 2, NG * NCMP], F32, O_C + 3584)
    hidvT = at("hidvT", [P, 2, NG, HPG, 32], F32, O_C + 4096)
    pc = [at(f"pc{b}", [P, NH, 32], F32, O_C + 6144 + b * 1024) for b in range(2)]
    pcT = at("pcT", [P, NG, T], F32, O_C + 8 * KB)
    vsw = at("vsw", [P, 2, TT, NG * ND], F32, O_C + 12 * KB)
    PT = [at(f"PT{b}", [P, TT, T], F32, O_E + b * 8 * KB) for b in range(2)]
    prob = [at(f"prob{b}", [P, T], F32, O_E + (16 + 2 * b) * KB) for b in range(2)]
    memT = at("memT", [P, KD, MEM], F32, O_D)
    kxT = at("kxT", [P, KD, MEM], F32, O_A)
    vx = at("vx", [P, 2, D], F32, O_A + 8 * KB)
    x1T = at("x1T", [P, KD, T], F32, O_C)
    xqT = at("xqT", [P, KD, T], F32, O_B)
    xoT = at("xoT", [P, KD, T], F32, O_C)
    PX = [at(f"PX{b}", [P, 2, T], F32, O_E + b * 4 * KB) for b in range(2)]
    probx = [at(f"probx{b}", [P, MEM], F32, O_E + (8 + b) * KB) for b in range(2)]
    lng = at("lng", [P, 2, D], F32, O_D + 8 * KB)
    x2T = at("x2T", [P, KD, T], F32, O_B)
    sgate = at("sgate", [P, FF], F32, O_C)
    sact = at("sact", [P, TT, FF], F32, O_C + 1 * KB)
    sactT = at("sactT", [P, 2, T], F32, O_C + 5 * KB)
    wrt = at("wrt", [P, KD, NE], F32, O_C + 9 * KB)
    rcon = at("rcon", [P, NC_R], F32, O_C + 11 * KB)
    rbias = at("rbias", [P, NE], F32, O_C + 13 * KB)
    score = at("score", [P, TT, NE], F32, O_D)
    biased = at("biased", [P, TT, NE], F32, O_D + 1 * KB)
    tmpa = at("tmpa", [P, TT, NE], F32, O_D + 2 * KB)
    hot8 = at("hot8", [P, TOPK, NE], F32, O_D + 3 * KB)
    hot8w = at("hot8w", [P, TOPK, NE], F32, O_D + 5 * KB)
    maskt = at("maskt", [P, TT, NE], F32, O_A)
    gtop = at("gtop", [P, TT, GROUPS, 8], F32, O_A + 1 * KB)
    rsmall = at("rsmall", [P, 1024], F32, O_A + 2 * KB)
    wdown = [at(f"wdown{b}", [P, 2, D], F32, O_DOWN + b * 8 * KB) for b in range(2)]
    xg = [at(f"xg{b}", [P, D], F32, O_DOWN + (16 + 4 * b) * KB) for b in range(2)]
    ysb = [at(f"ysb{b}", [P, D], F32, O_DOWN + (24 + 4 * b) * KB) for b in range(2)]
    xgT = at("xgT", [P, KD, BLK], F32, O_E)
    egate = at("egate", [P, FF], F32, O_E + 4 * KB)
    eact = at("eact", [P, FF], F32, O_E + 5 * KB)
    eactT = at("eactT", [P, 2, BLK], F32, O_E + 6 * KB)
    onehot = at("onehot", [P, TT, BLK], BF16, O_E + 7 * KB)
    posm = at("posm", [P, TT, NE], F32, O_E + 8 * KB)
    krank = at("krank", [P, TT, NE], F32, O_E + 9 * KB)
    info = at("info", [P, TT, 4], BF16, O_E + 10 * KB)
    wtop = at("wtop", [P, TT, TOPK], F32, O_E + 10 * KB + 64)
    itab = at("itab", [P, ITEMS], F32, O_E + 10 * KB + 256)
    itabi = at("itabi", [P, ITEMS + 2], I32, O_E + 11 * KB)
    boff = at("boff", [P, ITEMS], F32, O_E + 11 * KB + 512)
    rel = at("rel", [P, TT], F32, O_E + 12 * KB)
    gidx = [at(f"gidx{b}", [P, 1], I32, O_E + 12 * KB + 64 + 32 * b) for b in range(2)]
    snext = [at(f"snext{b}", [P, 1], I32, O_E + 12 * KB + 128 + 32 * b) for b in range(2)]
    scur = [at(f"scur{b}", [P, 1], I32, O_E + 12 * KB + 192 + 32 * b) for b in range(2)]
    gfl = at("gfl", [P, 1], F32, O_E + 12 * KB + 256)
    mcon = at("mcon", [P, BLK], F32, O_E + 12 * KB + 512)
    lng3 = at("lng3", [P, 2, D], F32, O_E + 14 * KB)
    yb = [at(f"yb{b}", [P, TOPK, D], F32, O_A + 32 * KB * b) for b in range(2)]
    c1 = at("c1", [P, NC_A], F32, O_F)
    tab = at("tab", [P, 2, TT, NFREQ], F32, O_F + 1536)
    gate = at("gate", [P, TT, 3 * NH], F32, O_F + 3840)
    vcmp = at("vcmp", [P, NG, ND], F32, O_F + 4224)
    kcmpT = at("kcmpT", [P, NG * NCMP], F32, O_F + 4736)
    ccmp = at("ccmp", [P, 2, TT, NCMP], F32, O_F + 4992)
    posi = at("posi", [P, TT], I32, O_F + 6016)
    posf = at("posf", [P, TT], F32, O_F + 6048)
    stat = at("stat", [P, 4, 6], F32, O_F + 6080)
    mv = at("mv", [P, TT, 2], F32, O_F + 6208)
    std = at("std", [P, TT], F32, O_F + 6240)
    nmax = at("nmax", [P, 2, 8], F32, O_F + 6272)
    rsum = at("rsum", [P, 2, 8], F32, O_F + 6336)
    rinv = at("rinv", [P, 2, 8], F32, O_F + 6400)
    cmpm = at("cmpm", [P, NH], F32, O_F + 6496)
    pe2 = at("pe2", [P, 2, 16], F32, O_F + 6528)
    rott = at("rott", [P, 2, 512], F32, O_E + 16 * KB)
    rottn = at("rottn", [P, 2, 2 * NH * NROT], F32, O_F + 6656)

    ident = c1[:, C_ID:C_ID + P]
    causal = c1[:, C_CAUS:C_CAUS + P]
    eps = c1[:, C_EPS:C_EPS + 1]

    def pair(name):
        return [ctx.enter_context(nc.psum_tensor(f"{name}{b}", [P, 512], F32)) for b in range(2)]

    pp, tp, sp_, op = pair("proj"), pair("tran"), pair("score"), pair("outp")

    x2_dram = nc.dram_tensor("x2_rows", [T, D], F32, kind="Internal").ap()
    y_dram = nc.dram_tensor("y_rows", [T * TOPK, D], F32, kind="Internal").ap()

    x_in = [sem(f"x_in{t}") for t in range(TT)]
    const_in, decay_in, mem_loaded, cmp_in, ln_in = (sem(n) for n in ("const_in", "decay_in", "mem_loaded", "cmp_in", "ln_in"))
    pe_in, route_in = sem("pe_in"), sem("route_in")
    loaded = [sem(f"loaded{s}") for s in range(4)]
    proj_done, tran_done, score_done, outp_done = (sem(n) for n in ("proj_done", "tran_done", "score_done", "outp_done"))
    proj_free, tran_free, score_free, outp_free = ([sem(f"{n}_free{b}") for b in range(2)] for n in ("proj", "tran", "score", "outp"))
    dve_step, act_step = sem("dve_step"), sem("act_step")
    angles_ready, tables_ready = sem("angles_ready"), sem("tables_ready")
    staged, raw_staged = sem("staged"), sem("raw_staged")
    sig_read = sem("sig_read")
    gates_ready = sem("gates_ready")
    rets_ready, rstd_asked, rstd_ready, oret_ready = (sem(n) for n in ("rets_ready", "rstd_asked", "rstd_ready", "oret_ready"))
    zeros_ready, pv_done, scur_ready, loop_step = (sem(n) for n in ("zeros_ready", "pv_done", "scur_ready", "loop_step"))
    pool_turn = sem("pool_turn")
    ab_ready, hid_ready, kvcmp_ready = sem("ab_ready"), sem("hid_ready"), sem("kvcmp_ready")
    pc_asked, pc_exp, pc_ready = sem("pc_asked"), sem("pc_exp"), sem("pc_ready")
    max_ready, exp_ready, prob_ready = sem("max_ready"), sem("exp_ready"), sem("prob_ready")
    var_ready, std_ready = sem("var_ready"), sem("std_ready")
    ln_ready = sem("ln_ready")
    xmax_ready, xexp_ready, xprob_ready = sem("xmax_ready"), sem("xexp_ready"), sem("xprob_ready")
    sgate_ready, sact_ready = sem("sgate_ready"), sem("sact_ready")
    score_sig, mask_ready, extra_ready, item_ready = (sem(n) for n in ("score_sig", "mask_ready", "extra_ready", "item_ready"))
    x2_saved = sem("x2_saved")
    e_gu_in = [sem(f"e_gu_in{b}") for b in range(2)]
    e_dn_in = [sem(f"e_dn_in{b}") for b in range(2)]
    hot_ready, idx_done, idx_ready = sem("hot_ready"), sem("idx_done"), sem("idx_ready")
    gathered = [sem(f"gathered{b}") for b in range(2)]
    scattered = [sem(f"scattered{b}") for b in range(2)]
    xgT_done, xgT_a, xgT_d = sem("xgT_done"), sem("xgT_a"), sem("xgT_d")
    h_done, egate_ready, eact_ready, eT_done, eT_ready = (sem(n) for n in ("h_done", "egate_ready", "eact_ready", "eT_done", "eT_ready"))
    y_done, y_act, y_dve = sem("y_done"), sem("y_act"), sem("y_dve")
    list_ready, moe_set = sem("list_ready"), sem("moe_set")
    y_in = [sem(f"y_in{b}") for b in range(2)]
    sum_done, fin_ready, out_saved = sem("sum_done"), sem("fin_ready"), sem("out_saved")

    def wait_done(eng, units, done, *name):
        eng.wait_ge(done, units.no(*name) + 1)

    def chunk_view(slot, blocks, cols):
        return ring[slot][:, 0:blocks * cols].rearrange("p (k n) -> p k n", k=blocks)

    def chunk_parts(name):
        kind, c = name
        n = CHUNK_NO[name]
        kp = lambda w: w.rearrange("(k p) n -> p k n", p=P)
        if kind == "in":
            v = chunk_view(SLOT[n], KD, W_COLS[c])
            return v, [(v, kp(io["w_in"][:, 512 * c:512 * c + W_COLS[c]]))]
        if kind == "w1":
            v = chunk_view(SLOT[n], 16, CMP_HID)
            return v, [(v, kp(io["cmp_w1_k" if c == 0 else "cmp_w1_v"]))]
        if kind == "sgu":
            v = ring[SLOT[n]][:, :].rearrange("p (g k n) -> p g k n", g=2, k=KD)
            return v, [(v[:, 0], kp(io["ws_gate"])), (v[:, 1], kp(io["ws_up"]))]
        if kind == "sdn":
            v = chunk_view(SLOT[n], 2, D)
            return v, [(v, kp(io["ws_down"]))]
        w = {"xkv": "w_xkv", "out": "w_out", "xq": "w_xq", "xo": "w_xo"}[kind]
        v = chunk_view(SLOT[n], KD, 512)
        return v, [(v, kp(io[w][:, 512 * c:512 * c + 512]))]

    def chunk_loaded(name):
        n = CHUNK_NO[name]
        return loaded[SLOT[n]], 16 * sum(len(chunk_parts(CHUNKS[m])[1]) for m in range(n + 1) if SLOT[m] == SLOT[n])

    def chunk_used(name):
        kind, c = name
        if kind == "w1":
            return score_done, SCORE.no("hid", c) + 1
        last = {"in": ("in", c, TT - 1), "xkv": ("xk", 4 * c + 3) if c < 2 else ("xv", 1, c - 2),
                "out": ("out", TT - 1, 1), "xq": ("xq", 4 * c + 3), "xo": ("xo", TT - 1, 1),
                "sgu": ("sgu", TT - 1), "sdn": ("sdn", TT - 1, 1)}[kind]
        return proj_done, PROJ.no(*last) + 1

    def pv_done_at(group):
        pr, g = divmod(group, 4)
        return (outp_done, OUTP.no("nsa", pr) + 1) if g == 3 else (pv_done, 3 * pr + g + 1)

    block = ctx.enter_context(nc.Block())

    @block.sync
    def _(sp):
        for t in range(TT):
            sp.dma_start(xres[:, t, :], io["x"][t * P:(t + 1) * P, :]).then_inc(x_in[t], 16)
        for n, name in enumerate(CHUNKS):
            before = last_in_slot(SLOT[n], n)
            if before is not None:
                sp.wait_ge(*chunk_used(CHUNKS[before]))
            for dst, src in chunk_parts(name)[1]:
                sp.dma_start(dst, src).then_inc(loaded[SLOT[n]], 16)

        gu = [ring[b][:, :].rearrange("p (g k n) -> p g k n", g=2, k=KD) for b in range(2)]

        def load_expert(b, e):
            for g, w in enumerate(("w_gate", "w_up")):
                sp.dma_start(gu[b][:, g], io[w][DS(e, 1), :, :].rearrange("o (p k) n -> p (o k) n", k=KD))\
                  .then_inc(e_gu_in[b], 16)

        def load_down(b, e):
            sp.dma_start(wdown[b][:, :, :], io["w_down"][DS(e, 1), :, :].rearrange("o (p k) n -> p (o k) n", k=2))\
              .then_inc(e_dn_in[b], 16)

        for b in range(2):
            sp.wait_ge(*chunk_used(CHUNKS[last_in_slot(b, len(CHUNKS))]))
            load_expert(b, b)
        sp.wait_ge(outp_done, OUTP.no("nsa", NH // 2 - 1) + 1)
        for b in range(2):
            load_down(b, b)
        sp.wait_ge(list_ready, 1)
        pairs = sp.value_load(itabi[0:1, ITEMS:ITEMS + 1], min_val=NE // 2, max_val=(NE + MAX_EXTRA + 1) // 2)
        with sp.Fori(1, pairs) as j:
            for b in range(2):
                e = sp.value_load(itabi[0:1, DS(j * 2 + b, 1)], min_val=0, max_val=NE - 1)
                sp.wait_ge(h_done, j * 2 + (b - 1))
                load_expert(b, e)
                sp.wait_ge(y_done, j * 2 + (b - 1))
                load_down(b, e)
        for b in range(2):
            sp.wait_ge(scattered[b], pairs * 16 + 16)
        for t in range(TT):
            if t >= 2:
                sp.wait_ge(sum_done, t - 1)
            sp.dma_start(yb[t % 2][:, :, :],
                         y_dram[t * P * TOPK:(t + 1) * P * TOPK, :].rearrange("(p k) n -> p k n", k=TOPK))\
              .then_inc(y_in[t % 2], 16)
        for t in range(TT):
            sp.wait_ge(fin_ready, t + 1)
            sp.dma_start(out[t * P:(t + 1) * P, :], xres[:, t, :]).then_inc(out_saved, 16)
        sp.wait_ge(out_saved, 16 * TT)

    @block.gpsimd
    def _(pool):
        with nc.allow_non_contiguous_dma(reason="a few small rows"):
            pool.dma_start(c1[:, :], io["c_first"]).then_inc(const_in, 16)
            pool.dma_start(posi[:, :], io["positions"].rearrange("(t p) -> p t", p=P)).then_inc(const_in, 16)
            pool.dma_start(decay[:, :, :], io["c_decay"].rearrange("p (h t) -> p h t", h=RH)).then_inc(decay_in, 16)
            pool.dma_start(mem_in[:, :, :], io["mem"].rearrange("(m p) n -> p m n", p=P)).then_inc(mem_loaded, 16)
            for j, w in enumerate(("cmp_pe_k", "cmp_pe_v")):
                pool.dma_start(pe2[:, j, :], io[w].rearrange("(l h) d -> (h d) l", h=2)).then_inc(pe_in, 16)
            pool.dma_start(ccmp[:, :, :, :], io["c_cmp"].rearrange("p (a t c) -> p a t c", a=2, t=TT)).then_inc(pe_in, 16)
            pool.wait_ge(outp_done, OUTP.no("ret", RH - 1) + 1)
            for j in range(2):
                pool.dma_start(w2k[:, :, j, :], io["cmp_w2_k"].rearrange("(k p) d -> p k d", p=P)).then_inc(cmp_in, 16)
            pool.dma_start(w2v[:, :, :], io["cmp_w2_v"].rearrange("(k p) d -> p k d", p=P)).then_inc(cmp_in, 16)

            def load_norm(dst, n):
                for j, w in enumerate(("g", "b")):
                    src = io[f"ln{n}_{w}"].rearrange("(o n) -> o n", o=1).to_broadcast([P, D])
                    pool.dma_start(dst[:, j, :], src).then_inc(ln_in, 16)

            pool.wait_ge(score_done, SCORE.no("hid", 1) + 1)
            load_norm(lng, 1)
            pool.wait_ge(ln_ready, TT)
            load_norm(lng, 2)
            pool.wait_ge(ln_ready, 2 * TT)
            pool.dma_start(wrt[:, :, :], io["w_router"].rearrange("(k p) n -> p k n", p=P)).then_inc(route_in, 16)
            pool.dma_start(rcon[:, :], io["c_route"]).then_inc(route_in, 16)
            pool.dma_start(mcon[:, :], io["c_route"][:, R_IOTA:R_IOTA + BLK]).then_inc(route_in, 16)
            pool.dma_start(rbias[:, :], io["router_bias"].rearrange("(o n) -> o n", o=1).to_broadcast([P, NE]))\
                .then_inc(route_in, 16)
            load_norm(lng3, 3)
        for t in range(TT):
            pool.dma_start(x2_dram[t * P:(t + 1) * P, :], xres[:, t, :]).then_inc(x2_saved, 16)
        pool.wait_ge(x2_saved, 16 * TT)

        def gather(b):
            pool.indirect_dma_start(out=xg[b][:, :], out_offset=None, in_=x2_dram[:, :],
                                    in_offset=bass.IndirectOffsetOnAxis(ap=gidx[b][:, 0:1], axis=0),
                                    bounds_check=T - 1, oob_is_err=False).then_inc(gathered[b], 16)

        def scatter(b):
            pool.indirect_dma_start(out=y_dram[:, :],
                                    out_offset=bass.IndirectOffsetOnAxis(ap=scur[b][:, 0:1], axis=0),
                                    in_=ysb[b][:, :], in_offset=None,
                                    bounds_check=T * TOPK - 1, oob_is_err=False).then_inc(scattered[b], 16)

        pool.wait_ge(moe_set, 6)
        for b in range(2):
            scatter(b)
        for b in range(2):
            pool.wait_ge(idx_ready, b + 1)
            gather(b)
        pool.wait_ge(list_ready, 1)
        pairs = pool.value_load(itabi[0:1, ITEMS:ITEMS + 1], min_val=NE // 2, max_val=(NE + MAX_EXTRA + 1) // 2)
        with pool.Fori(0, pairs) as j:
            for b in range(2):
                pool.wait_ge(xgT_done, j * 2 + (b + 1))
                pool.wait_ge(idx_ready, j * 2 + (b + 3))
                pool.sem_inc(pool_turn, 1)
                gather(b)
                pool.wait_ge(y_act, j * 2 + (b + 2))
                pool.wait_ge(y_dve, j * 2 + (b + 2))
                pool.sem_inc(pool_turn, 1)
                scatter(b)
        for b in range(2):
            pool.wait_ge(gathered[b], pairs * 16 + 16)

    @block.tensor
    def _(pe):
        mm, count = nc.tensor.matmul, {"p": 0, "t": 0, "s": 0, "o": 0}

        def take(key, units, free, name):
            n = units.no(*name)
            assert n == count[key], (name, n, count[key])
            count[key] += 1
            if n >= 2:
                pe.wait_ge(free[n % 2], n // 2)
            return n % 2

        def transposes(name, parts):
            b = take("t", TRAN, tran_free, name)
            for src, dst in parts:
                rows = src.shape[0]
                last = nc.tensor.transpose(dst(tp[b]), src, ident[0:rows, 0:rows])
            last.then_inc(tran_done, 1)

        def four(src, blocks):
            return [(src[:, k * P:(k + 1) * P], lambda bank, j=j: bank[:, j * P:(j + 1) * P])
                    for j, k in enumerate(blocks)]

        pe.wait_ge(const_in, 32)
        for t in range(TT):
            pe.wait_ge(x_in[t], 16)
            for j in range(2):
                transposes(("x", t, j), four(xres[:, t, :], range(4 * j, 4 * j + 4)))

        def proj_chunk(c, after=None):
            w = chunk_parts(("in", c))[0]
            pe.wait_ge(*chunk_loaded(("in", c)))
            for t in range(TT):
                if c == 0:
                    for b in range(2):
                        pe.wait_ge(tran_free[b], t + 1)
                b = take("p", PROJ, proj_free, ("in", c, t))
                for k in range(KD):
                    last = mm(pp[b][:, 0:W_COLS[c]], xT[:, k, t * P:(t + 1) * P], w[:, k, :],
                              start=(k == 0), stop=(k == KD - 1))
                last.then_inc(proj_done, 1)
                if after is not None and t >= 1:
                    after(t - 1)
            if after is not None:
                after(TT - 1)

        def stage_no(c, t):
            return [0, 1, 4, 5, 6].index(c) * TT + t

        def ret_T(c):
            def go(t):
                n = stage_no(c, t)
                pe.wait_ge(staged, n + 1)
                transposes(("ret", c, t), four(stage[n % 2][:, :], range(RH)))
            return go

        def nq_T(t):
            n = stage_no(4, t)
            pe.wait_ge(staged, n + 1)
            for j in range(2):
                transposes(("nq", t, j), four(stage[n % 2][:, :], range(4 * j, 4 * j + 4)))

        def kv5_T(t):
            n = stage_no(5, t)
            pe.wait_ge(staged, n + 1)
            transposes(("kv5", t, 0), four(stage[n % 2][:, :], range(0, 4)))
            transposes(("kv5", t, 1), four(stage[n % 2][:, :], range(4, 6)))

        def kv6_T(t):
            n = stage_no(6, t)
            pe.wait_ge(staged, n + 1)
            transposes(("kv6", t), four(stage[n % 2][:, :], range(0, 2)))

        proj_chunk(0, ret_T(0))
        proj_chunk(1, ret_T(1))
        proj_chunk(2)
        proj_chunk(3)

        last_ret = TRAN.no("ret", 1, TT - 1)
        for b in range(2):
            pe.wait_ge(tran_free[b], (last_ret + 1) // 2)
        def ret_scores(h):
            for k in range(TT):
                b = take("s", SCORE, score_free, ("ret", h, k))
                n = T - k * P
                mm(sp_[b][:, 0:n], retT[1][:, h, k * P:(k + 1) * P], retT[0][:, h, k * P:T],
                   start=True, stop=True).then_inc(score_done, 1)

        for h in range(RH):
            ret_scores(h)
            pe.wait_ge(rets_ready, TT * (h + 1))
            if h == 0:
                pe.wait_ge(proj_free[0], 8)
                pe.wait_ge(proj_free[1], 8)
            b = take("o", OUTP, outp_free, ("ret", h))
            for q in range(TT):
                for k in range(q + 1):
                    last = mm(op[b][:, q * P:(q + 1) * P], retS[:, k, (q - k) * P:(q - k + 1) * P],
                              rv[:, k, h * RD:(h + 1) * RD], start=(k == 0), stop=(k == q))
            last.then_inc(outp_done, 1)

        pe.wait_ge(oret_ready, RH)
        for t in range(TT):
            transposes(("oret", t), four(oret[:, t, :], range(RH)))

        proj_chunk(4, nq_T)
        proj_chunk(5, kv5_T)
        proj_chunk(6, kv6_T)

        for j in range(2):
            w = chunk_parts(("w1", j))[0]
            pe.wait_ge(*chunk_loaded(("w1", j)))
            pe.wait_ge(ab_ready, j + 1)
            b = take("s", SCORE, score_free, ("hid", j))
            for l in range(16):
                last = mm(sp_[b][0:NG * NCMP, 0:CMP_HID], ab[:, j, l, :, :].rearrange("p g c -> p (g c)"), w[:, l, :],
                          start=(l == 0), stop=(l == 15))
            last.then_inc(score_done, 1)
        for j in range(2):
            pe.wait_ge(hid_ready, j + 1)
            transposes(("hid", j), [(hid[:, j, k * P:(k + 1) * P], lambda bank, k=k: bank[:, k * P:k * P + NG * NCMP])
                                    for k in range(2)])
        pe.wait_ge(cmp_in, 48)
        for j in range(2):
            n = TRAN.no("hid", j)
            pe.wait_ge(tran_free[n % 2], n // 2 + 1)
        b = take("s", SCORE, score_free, ("kvc", 0))
        for k in range(2):
            mm(sp_[b][:, 0:NG * NCMP], w2k[:, k, :, :].rearrange("p a d -> p (a d)"), hidkT[:, k, :],
               start=(k == 0), stop=(k == 1))
        for g in range(NG):
            for k in range(2):
                last = mm(sp_[b][:, 128 + g * ND:128 + (g + 1) * ND],
                          hidvT[:, k, g, :, :].rearrange("p a c -> p (a c)"), w2v[:, k, :],
                          start=(k == 0), stop=(k == 1))
        last.then_inc(score_done, 1)

        pe.wait_ge(mem_loaded, 16)
        for m in range(2):
            for j in range(2):
                transposes(("mem", m, j), four(mem_in[:, m, :], range(4 * j, 4 * j + 4)))
        last_mem = TRAN.no("mem", 1, 1)
        for b in range(2):
            pe.wait_ge(tran_free[b], (last_mem + 1) // 2 if b == 1 else (last_mem + 2) // 2)
        for c in range(2):
            w = chunk_parts(("xkv", c))[0]
            pe.wait_ge(*chunk_loaded(("xkv", c)))
            for d in range(4):
                b = take("p", PROJ, proj_free, ("xk", 4 * c + d))
                for k in range(KD):
                    last = mm(pp[b][:, 0:MEM], w[:, k, d * P:(d + 1) * P], memT[:, k, :],
                              start=(k == 0), stop=(k == KD - 1))
                last.then_inc(proj_done, 1)
        for c in range(2):
            w = chunk_parts(("xkv", 2 + c))[0]
            pe.wait_ge(*chunk_loaded(("xkv", 2 + c)))
            for m in range(2):
                b = take("p", PROJ, proj_free, ("xv", m, c))
                for k in range(KD):
                    last = mm(pp[b][:, :], memT[:, k, m * P:(m + 1) * P], w[:, k, :],
                              start=(k == 0), stop=(k == KD - 1))
                last.then_inc(proj_done, 1)

        pe.wait_ge(kvcmp_ready, 1)
        for t in range(TT):
            for a in range(2):
                b = take("s", SCORE, score_free, ("sc", t, a))
                for i in range(NH // 2):
                    g = (2 * i + a) // HPG
                    last = mm(sp_[b][:, i * 32:i * 32 + NCMP], nqT[a * ND:(a + 1) * ND, i, t * P:(t + 1) * P],
                              kcmpT[a * ND:(a + 1) * ND, g * NCMP:(g + 1) * NCMP], start=True, stop=True)
                last.then_inc(score_done, 1)
            if t >= 1:
                pe.wait_ge(pc_ready, t)
                transposes(("pc", t - 1), four(pc[(t - 1) % 2][:, :, :].rearrange("p h c -> p (h c)"), range(NG)))
        pe.wait_ge(pc_ready, TT)
        transposes(("pc", TT - 1), four(pc[(TT - 1) % 2][:, :, :].rearrange("p h c -> p (h c)"), range(NG)))

        kT, LAG = (kselT, kwinT), 2

        def att_scores(n):
            _, h, br, q = ATT[n]
            lo, g = ND * (h % 2), h // HPG
            b = take("s", SCORE, score_free, ("att", n))
            mm(sp_[b][:, 0:(q + 1) * P], nqrT[lo:lo + ND, h // 2, q * P:(q + 1) * P],
               kT[br][lo:lo + ND, g, 0:(q + 1) * P], start=True, stop=True).then_inc(score_done, 1)

        def att_T(n):
            pe.wait_ge(prob_ready, n + 1)
            transposes(("pt", n), four(prob[n % 2][:, :], range(ATT[n][3] + 1)))

        def att_pv(n):
            pr, h, br, q = ATT[n]
            lo, g = ND * (h % 2), h // HPG
            o = op[OUTP.no("nsa", pr) % 2]
            if h % 2 == 0 and br == 0:
                take("o", OUTP, outp_free, ("nsa", pr))
            if n == TT - 1:
                for t in range(TT):
                    m = TRAN.no("pc", t)
                    pe.wait_ge(tran_free[m % 2], m // 2 + 1)
            if br == 0:
                r = 32 * (h % HPG)
                mm(o[lo:lo + ND, :], vcmp[r:r + 32, g, :], pcT[r:r + 32, g, :], start=True, stop=False)
            for i in range(2):
                m = TRAN.no("pt", n - i)
                pe.wait_ge(tran_free[m % 2], m // 2 + 1)
            for k in range(TT):
                last = mm(o[lo:lo + ND, k * P:T], vsw[:, br, k, g * ND:(g + 1) * ND],
                          PT[(n // TT) % 2][:, k, k * P:T], start=False, stop=(br == 1 and k == TT - 1))
            if h % 2 == 1 and br == 1:
                last.then_inc(outp_done, 1)
            else:
                last.then_inc(pv_done, 1)

        for n in range(len(ATT) + LAG + 2):
            if n < len(ATT):
                att_scores(n)
            if LAG <= n < len(ATT) + LAG:
                att_T(n - LAG)
            if n >= LAG + 2 and (n - LAG - 2) % TT == TT - 1:
                att_pv(n - LAG - 2)

        w = [chunk_parts(("out", n))[0] for n in range(2)]
        for n in range(2):
            pe.wait_ge(*chunk_loaded(("out", n)))
        for b in range(2):
            pe.wait_ge(outp_free[b], (RH + NH // 2) // 2)
        for t in range(TT):
            for n in range(2):
                b = take("p", PROJ, proj_free, ("out", t, n))
                for k in range(KD):
                    last = mm(pp[b][:, :], mixT[:, k, t * P:(t + 1) * P], w[n][:, k, :], start=(k == 0), stop=(k == KD - 1))
                last.then_inc(proj_done, 1)

        def norm_T(which, kind):
            for t in range(TT):
                pe.wait_ge(ln_ready, TT * which + t + 1)
                for j in range(2):
                    transposes((kind, t, j), four(xres[:, t, :], range(4 * j, 4 * j + 4)))
            for j in range(2):
                m = TRAN.no(kind, TT - 1, j)
                pe.wait_ge(tran_free[m % 2], m // 2 + 1)

        norm_T(0, "x1")
        for c in range(2):
            w = chunk_parts(("xq", c))[0]
            pe.wait_ge(*chunk_loaded(("xq", c)))
            for d in range(4):
                b = take("p", PROJ, proj_free, ("xq", 4 * c + d))
                for k in range(KD):
                    last = mm(pp[b][:, :], w[:, k, d * P:(d + 1) * P], x1T[:, k, :], start=(k == 0), stop=(k == KD - 1))
                last.then_inc(proj_done, 1)
        for d in range(KD - 2, KD):
            m = PROJ.no("xq", d)
            pe.wait_ge(proj_free[m % 2], m // 2 + 1)

        XU = [(h, t) for h in range(XH) for t in range(TT)]

        def x_pv(h):
            for i in range(2):
                m = TRAN.no("px", h, TT - 1 - i)
                pe.wait_ge(tran_free[m % 2], m // 2 + 1)
            for d in range(2):
                b = take("o", OUTP, outp_free, ("x", h, d))
                for m in range(2):
                    last = mm(op[b][:, :], vx[:, m, (2 * h + d) * P:(2 * h + d + 1) * P], PX[h % 2][:, m, :],
                              start=(m == 0), stop=(m == 1))
                last.then_inc(outp_done, 1)

        for n in range(len(XU) + LAG + 1):
            if n < len(XU):
                h, t = XU[n]
                b = take("s", SCORE, score_free, ("x", h, t))
                for d in range(2):
                    last = mm(sp_[b][:, 0:MEM], xqT[:, 2 * h + d, t * P:(t + 1) * P], kxT[:, 2 * h + d, :],
                              start=(d == 0), stop=(d == 1))
                last.then_inc(score_done, 1)
            if LAG <= n < len(XU) + LAG:
                h, t = XU[n - LAG]
                pe.wait_ge(xprob_ready, n - LAG + 1)
                transposes(("px", h, t), four(probx[(n - LAG) % 2][:, :], range(2)))
            if n >= LAG + 1 and (n - LAG - 1) % TT == TT - 1:
                x_pv((n - LAG - 1) // TT)

        w = [chunk_parts(("xo", n))[0] for n in range(2)]
        for n in range(2):
            pe.wait_ge(*chunk_loaded(("xo", n)))
        for b in range(2):
            pe.wait_ge(outp_free[b], OUTP.n // 2)
        for t in range(TT):
            for n in range(2):
                b = take("p", PROJ, proj_free, ("xo", t, n))
                for k in range(KD):
                    last = mm(pp[b][:, :], xoT[:, k, t * P:(t + 1) * P], w[n][:, k, :], start=(k == 0), stop=(k == KD - 1))
                last.then_inc(proj_done, 1)

        norm_T(1, "x2")
        pe.wait_ge(route_in, 64)
        b = take("s", SCORE, score_free, ("logit", 0))
        for t in range(TT):
            for k in range(KD):
                last = mm(sp_[b][:, t * NE:(t + 1) * NE], x2T[:, k, t * P:(t + 1) * P], wrt[:, k, :],
                          start=(k == 0), stop=(k == KD - 1))
        last.then_inc(score_done, 1)
        w = chunk_parts(("sgu", 0))[0]
        pe.wait_ge(*chunk_loaded(("sgu", 0)))
        wd = chunk_parts(("sdn", 0))[0]
        for t in range(TT):
            b = take("p", PROJ, proj_free, ("sgu", t))
            for k in range(KD):
                last = mm(pp[b][:, :], x2T[:, k, t * P:(t + 1) * P], w[:, :, k, :], start=(k == 0), stop=(k == KD - 1))
            last.then_inc(proj_done, 1)
        for t in range(TT):
            pe.wait_ge(sact_ready, t + 1)
            transposes(("sh", t), four(sact[:, t, :], range(2)))
        pe.wait_ge(*chunk_loaded(("sdn", 0)))
        for t in range(TT):
            m = TRAN.no("sh", t)
            pe.wait_ge(tran_free[m % 2], m // 2 + 1)
            for n in range(2):
                b = take("p", PROJ, proj_free, ("sdn", t, n))
                for k in range(2):
                    last = mm(pp[b][:, :], sactT[:, k, t * P:(t + 1) * P], wd[:, k, n * 512:(n + 1) * 512],
                              start=(k == 0), stop=(k == 1))
                last.then_inc(proj_done, 1)

        tri, one = rcon[:, R_TRI:R_TRI + P], rcon[:, R_ONE:R_ONE + P]
        pe.wait_ge(mask_ready, 1)
        b = take("s", SCORE, score_free, ("pos", 0))
        for t in range(TT):
            for u in range(t + 1):
                mm(sp_[b][:, t * NE:(t + 1) * NE], tri if u == t else one, maskt[:, u, :], start=(u == 0), stop=(u == t))
        for u in range(TT):
            last = mm(sp_[b][0:NE, 384:385], maskt[:, u, :], one[:, 0:1], start=(u == 0), stop=(u == TT - 1))
        last.then_inc(score_done, 1)
        pe.wait_ge(extra_ready, 1)
        b = take("s", SCORE, score_free, ("extra", 0))
        ecol = rsmall[0:NE, 512:513]
        mm(sp_[b][0:NE, 0:1], rcon[0:NE, R_TRI64:R_TRI64 + NE], ecol, start=True, stop=True)
        mm(sp_[b][:, 1:2], rcon[0:NE, R_ONE:R_ONE + P], ecol, start=True, stop=True).then_inc(score_done, 1)
        pe.wait_ge(extra_ready, 2)
        b = take("s", SCORE, score_free, ("cum", 0))
        ended = rsmall[0:NE, 640:640 + EXTRA]
        mm(sp_[b][:, 0:EXTRA], rcon[0:NE, R_ONE:R_ONE + P], ended, start=True, stop=True)
        mm(sp_[b][:, 64:64 + EXTRA], rsmall[0:NE, 768:768 + P], ended, start=True, stop=True).then_inc(score_done, 1)

        gu = [ring[b][:, :].rearrange("p (g k n) -> p g k n", g=2, k=KD) for b in range(2)]
        hps, ips, yps = pp[0], pp[1], op
        eTps = sp_[0]
        idx_ps = pp[1]

        def number_rows():
            for t in range(TT):
                last = mm(idx_ps[:, 0:4], onehot[:, t, :], info[:, t, :], start=(t == 0), stop=(t == TT - 1))
            return last

        def rows_T(b):
            for k in range(KD):
                last = nc.tensor.transpose(tp[k // 4][:, (k % 4) * P:(k % 4 + 1) * P], xg[b][:, k:D:KD], ident)
            return last

        for b in range(2):
            pe.wait_ge(hot_ready, b + 1)
            if b == 1:
                pe.wait_ge(idx_ready, 1)
            else:
                pe.wait_ge(proj_free[0], PROJ.n // 2)
                pe.wait_ge(proj_free[1], PROJ.n // 2)
            number_rows().then_inc(idx_done, 1)
        pe.wait_ge(gathered[0], 16)
        rows_T(0).then_inc(xgT_done, 1)
        pe.wait_ge(list_ready, 1)
        pairs = pe.value_load(itabi[0:1, ITEMS:ITEMS + 1], min_val=NE // 2, max_val=(NE + MAX_EXTRA + 1) // 2)
        with pe.Fori(0, pairs) as j:
            for b in range(2):
                pe.wait_ge(e_gu_in[b], j * 32 + 32)
                pe.wait_ge(xgT_a, j * 2 + (b + 1))
                pe.wait_ge(xgT_d, j * 2 + (b + 1))
                for k in range(KD):
                    last = mm(hps[:, :], xgT[:, k, :], gu[b][:, :, k, :], start=(k == 0), stop=(k == KD - 1))
                last.then_inc(h_done, 1)
                pe.wait_ge(hot_ready, j * 2 + (b + 3))
                number_rows().then_inc(idx_done, 1)
                pe.wait_ge(gathered[1 - b], j * 16 + 16 * (b + 1))
                rows_T(1 - b).then_inc(xgT_done, 1)
                pe.wait_ge(eact_ready, j * 2 + (b + 1))
                for k in range(2):
                    last = nc.tensor.transpose(eTps[:, k * P:(k + 1) * P], eact[:, k:FF:2], ident)
                last.then_inc(eT_done, 1)
                pe.wait_ge(eT_ready, j * 2 + (b + 1))
                pe.wait_ge(e_dn_in[b], j * 16 + 16)
                pe.wait_ge(y_act, j * 2 + (b + 1))
                pe.wait_ge(y_dve, j * 2 + (b + 1))
                for n in range(2):
                    for k in range(2):
                        last = mm(yps[n][:, :], eactT[:, k, :], wdown[b][:, k, n * 512:(n + 1) * 512],
                                  start=(k == 0), stop=(k == 1))
                last.then_inc(y_done, 1)

    @block.scalar
    def _(act):
        steps = [0]

        def link(ins):
            steps[0] += 1
            ins.then_inc(act_step, 1)
            act.wait_ge(act_step, steps[0])

        def take(units, done, free, *name):
            wait_done(act, units, done, *name)
            return units.no(*name) % 2

        def copy_T(name, dst, src=None, scale=1.0):
            b = take(TRAN, tran_done, tran_free, *name)
            src = src(tp[b]) if src else tp[b][:, :].rearrange("p (k t) -> p k t", k=4)
            nc.scalar.activation(dst, src, ACT.Copy, scale=scale).then_inc(tran_free[b], 1)

        def part(n):
            return lambda bank: bank[:, 0:n * P].rearrange("p (k t) -> p k t", k=n)

        act.wait_ge(angles_ready, 1)
        nc.scalar.activation(tab[:, :, :, :], turns[:, :, :, :], ACT.Sin).then_inc(tables_ready, 1)
        for t in range(TT):
            for j in range(2):
                copy_T(("x", t, j), xT[:, 4 * j:4 * j + 4, t * P:(t + 1) * P])
        for c in range(2):
            for t in range(TT):
                copy_T(("ret", c, t), retT[c][:, :, t * P:(t + 1) * P])
        for t in range(TT):
            b = take(PROJ, proj_done, proj_free, "in", 2, t)
            nc.scalar.activation(rv[:, t, :], pp[b][:, :], ACT.Copy).then_inc(proj_free[b], 1)
        for t in range(TT):
            b = take(PROJ, proj_done, proj_free, "in", 3, t)
            nc.scalar.activation(swish[:, t, :], pp[b][:, :], ACT.Silu).then_inc(proj_free[b], 1)
        for h in range(RH):
            act.wait_ge(rstd_asked, h + 1)
            nc.scalar.activation(std[:, :], mv[:, :, 1], ACT.Sqrt, bias=eps).then_inc(rstd_ready, 1)
        for t in range(TT):
            copy_T(("oret", t), mixT[:, 0:4, t * P:(t + 1) * P])

        def stage_no(c, t):
            return [0, 1, 4, 5, 6].index(c) * TT + t

        def stage_free(n):
            c, t = [0, 1, 4, 5, 6][(n - 2) // TT], (n - 2) % TT
            name = {0: ("ret", 0, t), 1: ("ret", 1, t), 4: ("nq", t, 1), 5: ("kv5", t, 1), 6: ("kv6", t)}[c]
            wait_done(act, TRAN, tran_done, *name)

        def nq_copies(t):
            n = stage_no(4, t)
            stage_free(n)
            b = take(PROJ, proj_done, proj_free, "in", 4, t)
            nc.scalar.activation(stage[n % 2][:, 0:512], pp[b][:, :], ACT.Copy)
            nc.scalar.activation(stage[n % 2][:, 512:1024], pp[b][:, :], ACT.Copy).then_inc(raw_staged, 1)

        def twice(v):
            return v.rearrange("p (g o d) -> p g o d", o=1, d=ND).to_broadcast([P, v.shape[1] // ND, 2, ND])

        def kv5_copies(t):
            n = stage_no(5, t)
            stage_free(n)
            b = take(PROJ, proj_done, proj_free, "in", 5, t)
            dst = stage[n % 2][:, 0:768].rearrange("p (g a d) -> p g a d", a=2, d=ND)
            for a in range(2):
                nc.scalar.activation(dst[:, :, a, :], pp[b][:, 0:384].rearrange("p (g d) -> p g d", d=ND), ACT.Copy)
            nc.scalar.activation(vsw[:, 0, t, :], pp[b][:, 384:512], ACT.Copy).then_inc(raw_staged, 1)

        def kv6_copies(t):
            n = stage_no(6, t)
            stage_free(n)
            b = take(PROJ, proj_done, proj_free, "in", 6, t)
            dst = stage[n % 2][:, 0:256].rearrange("p (g a d) -> p g a d", a=2, d=ND)
            for a in range(2):
                nc.scalar.activation(dst[:, :, a, :], pp[b][:, 0:128].rearrange("p (g d) -> p g d", d=ND), ACT.Copy)
            nc.scalar.activation(vsw[:, 1, t, :], pp[b][:, 128:256], ACT.Copy)
            nc.scalar.activation(gate[:, t, :], pp[b][:, 256:280], ACT.Sigmoid).then_inc(raw_staged, 1)

        def nq_T(t):
            copy_T(("nq", t, 0), nqT[:, :, t * P:(t + 1) * P], scale=ND ** -0.5)
            copy_T(("nq", t, 1), nqrT[:, :, t * P:(t + 1) * P], scale=ND ** -0.5)

        def kv5_T(t):
            copy_T(("kv5", t, 0), kvcT[:, :, t * P:(t + 1) * P])
            copy_T(("kv5", t, 1), kselT[:, :, t * P:(t + 1) * P], part(2))

        def kv6_T(t):
            copy_T(("kv6", t), kwinT[:, :, t * P:(t + 1) * P], part(2))

        for copies, turned in ((nq_copies, nq_T), (kv5_copies, kv5_T), (kv6_copies, kv6_T)):
            for t in range(TT):
                copies(t)
                if t >= 1:
                    turned(t - 1)
            turned(TT - 1)

        for j in range(2):
            b = take(SCORE, score_done, score_free, "hid", j)
            nc.scalar.activation(hid[:, j, :], sp_[b][0:NG * NCMP, 0:CMP_HID], ACT.Silu).then_inc(hid_ready, 1)
            act.wait_ge(hid_ready, j + 1)
            act.sem_inc(score_free[b], 1)
        copy_T(("hid", 0), hidkT[:, :, :], lambda bank: bank[:, 0:256].rearrange("p (k c) -> p k c", k=2)[:, :, 0:NG * NCMP])
        act.wait_ge(zeros_ready, 3)
        b = take(TRAN, tran_done, tran_free, "hid", 1)
        for k in range(2):
            for g in range(NG):
                last = nc.scalar.activation(
                    hidvT[:, k, g, :, 0:NCMP],
                    tp[b][:, k * P + g * NCMP:k * P + (g + 1) * NCMP].rearrange("p (o c) -> p o c", o=1)
                    .to_broadcast([P, HPG, NCMP]), ACT.Copy)
        last.then_inc(tran_free[b], 1)
        b = take(SCORE, score_done, score_free, "kvc", 0)
        nc.scalar.activation(kcmpT[:, :], sp_[b][:, 0:NG * NCMP], ACT.Copy)
        nc.scalar.activation(vcmp[:, :, :], sp_[b][:, 128:256].rearrange("p (g d) -> p g d", g=NG), ACT.Copy)\
            .then_inc(kvcmp_ready, 1)
        act.wait_ge(kvcmp_ready, 1)
        act.sem_inc(score_free[b], 1)

        for m in range(2):
            for j in range(2):
                if m == 0 and j == 0:
                    act.wait_ge(score_done, SCORE.no("hid", 1) + 1)
                copy_T(("mem", m, j), memT[:, 4 * j:4 * j + 4, m * P:(m + 1) * P])
        for d in range(KD):
            b = take(PROJ, proj_done, proj_free, "xk", d)
            nc.scalar.activation(kxT[:, d, :], pp[b][:, 0:MEM], ACT.Copy, scale=(D // XH) ** -0.5).then_inc(proj_free[b], 1)
        for n in range(2):
            for m in range(2):
                b = take(PROJ, proj_done, proj_free, "xv", m, n)
                nc.scalar.activation(vx[:, m, n * 512:(n + 1) * 512], pp[b][:, :], ACT.Copy).then_inc(proj_free[b], 1)

        for t in range(TT):
            act.wait_ge(pc_asked, t + 1)
            v = pc[t % 2][:, :, 0:NCMP]
            nc.scalar.activation(v, v, ACT.Exp).then_inc(pc_exp, 1)
            if t >= 1:
                copy_T(("pc", t - 1), pcT[:, :, (t - 1) * P:t * P], part(2))
        copy_T(("pc", TT - 1), pcT[:, :, (TT - 1) * P:T], part(2))

        def copy_pair(pr):
            b = take(OUTP, outp_done, outp_free, "nsa", pr)
            nc.scalar.activation(mixT[:, 4 + pr, :], op[b][:, :], ACT.Copy).then_inc(outp_free[b], 1)

        LAG = 2
        for n in range(len(ATT) + LAG):
            if n < len(ATT):
                q = ATT[n][3]
                b = SCORE.no("att", n) % 2
                act.wait_ge(max_ready, n + 1)
                if n >= 2:
                    wait_done(act, TRAN, tran_done, "pt", n - 2)
                nc.scalar.activation(prob[n % 2][:, 0:(q + 1) * P], sp_[b][:, 0:(q + 1) * P], ACT.Exp,
                                     bias=nmax[:, n % 2, 0:1], accum_out=rsum[:, n % 2, 0:1]).then_inc(exp_ready, 1)
            if n >= LAG:
                m = n - LAG
                pr, h, br, q = ATT[m]
                if m % TT == 0 and m >= 2 * TT:
                    act.wait_ge(*pv_done_at(m // TT - 2))
                copy_T(("pt", m), PT[(m // TT) % 2][:, 0:q + 1, q * P:(q + 1) * P], part(q + 1))
                if m % (4 * TT) == 2 * TT - 1 and m > 2 * TT:
                    copy_pair(m // (4 * TT) - 1)
        copy_pair(NH // 2 - 1)

        def norm_std(which):
            for t in range(TT):
                act.wait_ge(var_ready, TT * which + t + 1)
                nc.scalar.activation(std[:, t:t + 1], mv[:, t, 1:2], ACT.Sqrt, bias=eps).then_inc(std_ready, 1)
                if which < 2 and t >= 1:
                    norm_T(which, t - 1)
            if which < 2:
                norm_T(which, TT - 1)

        def norm_T(which, t):
            kind, dst = (("x1", x1T), ("x2", x2T))[which]
            for j in range(2):
                copy_T((kind, t, j), dst[:, 4 * j:4 * j + 4, t * P:(t + 1) * P])

        norm_std(0)
        for d in range(KD):
            b = take(PROJ, proj_done, proj_free, "xq", d)
            nc.scalar.activation(xqT[:, d, :], pp[b][:, :], ACT.Copy).then_inc(proj_free[b], 1)

        def x_out(h):
            for d in range(2):
                b = take(OUTP, outp_done, outp_free, "x", h, d)
                nc.scalar.activation(xoT[:, 2 * h + d, :], op[b][:, :], ACT.Copy).then_inc(outp_free[b], 1)

        XU = [(h, t) for h in range(XH) for t in range(TT)]
        for n in range(len(XU) + LAG):
            if n < len(XU):
                b = SCORE.no("x", *XU[n]) % 2
                act.wait_ge(xmax_ready, n + 1)
                if n >= 2:
                    wait_done(act, TRAN, tran_done, "px", *XU[n - 2])
                nc.scalar.activation(probx[n % 2][:, :], sp_[b][:, 0:MEM], ACT.Exp, bias=nmax[:, n % 2, 0:1],
                                     accum_out=rsum[:, n % 2, 0:1]).then_inc(xexp_ready, 1)
            if n >= LAG:
                h, t = XU[n - LAG]
                if t == 0 and h >= 2:
                    wait_done(act, OUTP, outp_done, "x", h - 2, 1)
                copy_T(("px", h, t), PX[h % 2][:, :, t * P:(t + 1) * P], part(2))
                if t == 1 and h >= 1:
                    x_out(h - 1)
        x_out(XH - 1)
        norm_std(1)

        b = take(SCORE, score_done, score_free, "logit", 0)
        nc.scalar.activation(score[:, :, :], sp_[b][:, 0:TT * NE].rearrange("p (t e) -> p t e", t=TT), ACT.Sigmoid)\
            .then_inc(score_sig, 1)
        for t in range(TT):
            b = take(PROJ, proj_done, proj_free, "sgu", t)
            if t >= 1:
                act.wait_ge(sact_ready, t)
            nc.scalar.activation(sgate[:, :], pp[b][:, 0:FF], ACT.Silu).then_inc(sgate_ready, 1)
        for t in range(TT):
            copy_T(("sh", t), sactT[:, :, t * P:(t + 1) * P], part(2))

        def half_T():
            nc.scalar.activation(xgT[:, 0:4, :], tp[0][:, :].rearrange("p (k t) -> p k t", k=4), ACT.Copy)\
                .then_inc(xgT_a, 1)

        act.sem_inc(y_act, 1)
        act.wait_ge(xgT_done, 1)
        half_T()
        act.wait_ge(list_ready, 1)
        pairs = act.value_load(itabi[0:1, ITEMS:ITEMS + 1], min_val=NE // 2, max_val=(NE + MAX_EXTRA + 1) // 2)
        with act.Fori(0, pairs) as j:
            for b in range(2):
                act.wait_ge(h_done, j * 2 + (b + 1))
                nc.scalar.activation(egate[:, :], pp[0][:, 0:FF], ACT.Silu).then_inc(egate_ready, 1)
                act.wait_ge(xgT_done, j * 2 + (b + 2))
                half_T()
                act.wait_ge(eT_done, j * 2 + (b + 1))
                nc.scalar.activation(eactT[:, :, :], sp_[0][:, 0:2 * P].rearrange("p (k t) -> p k t", k=2), ACT.Copy)\
                    .then_inc(eT_ready, 1)
                act.wait_ge(y_done, j * 2 + (b + 1))
                act.wait_ge(scattered[b], j * 16 + 16)
                nc.scalar.activation(ysb[b][:, 0:512], op[0][:, :], ACT.Copy).then_inc(y_act, 1)
        norm_std(2)

    @block.vector
    def _(dve):
        V = nc.vector
        steps = [0]

        def mark(ins):
            steps[0] += 1
            return ins.then_inc(dve_step, 1)

        def link(ins=None):
            if ins is not None:
                mark(ins)
            dve.wait_ge(dve_step, steps[0])

        M, TWO_PI = 1.5 * 2.0 ** 23, 2 * np.pi
        A1 = 6.28125
        A2 = float(np.float32(np.floor((TWO_PI - A1) * 2 ** 21) / 2 ** 21))
        A3 = float(TWO_PI - A1 - A2)
        dve.wait_ge(const_in, 32)
        link(V.tensor_copy(posf[:, :], posi[:, :]))
        link(V.tensor_tensor(ang[:, :, :], posf[:, :].rearrange("p (t o) -> p t o", o=1).to_broadcast([P, TT, NFREQ]),
                             c1[:, C_INV:C_INV + NFREQ].rearrange("p (o f) -> p o f", o=1).to_broadcast([P, TT, NFREQ]),
                             ALU.mult))
        n_turns = oret[:, 0:2, 0:TT * NFREQ]
        for s in range(2):
            link(V.tensor_scalar(n_turns[:, s, :], ang[:, :, :].rearrange("p t f -> p (t f)"), float(1 / TWO_PI), 0.25 * s, ALU.mult, ALU.add))
        link(V.tensor_scalar(n_turns, n_turns, M, None, ALU.add))
        link(V.tensor_scalar(n_turns, n_turns, M, None, ALU.subtract))
        for s in range(2):
            flat = turns[:, s, :, :].rearrange("p t f -> p (t f)")
            src = ang[:, :, :].rearrange("p t f -> p (t f)")
            for a in (A1, A2, A3):
                link(V.scalar_tensor_tensor(out=flat, in0=n_turns[:, s, :], scalar=-a, in1=src, op0=ALU.mult, op1=ALU.add))
                src = flat
        link(V.tensor_scalar(turns[:, 1, :, :], turns[:, 1, :, :], float(np.pi / 2), None, ALU.add))
        PI = 3.1415925
        V.tensor_scalar(turns[:, :, :, :], turns[:, :, :, :], -PI, PI, ALU.max, ALU.min).then_inc(angles_ready, 1)
        dve.wait_ge(tables_ready, 1)

        def stage_no(c, t):
            return [0, 1, 4, 5, 6].index(c) * TT + t

        def stage_free(n):
            if n >= 2:
                c, t = [0, 1, 4, 5, 6][(n - 2) // TT], (n - 2) % TT
                name = {0: ("ret", 0, t), 1: ("ret", 1, t), 4: ("nq", t, 1), 5: ("kv5", t, 1), 6: ("kv6", t)}[c]
                wait_done(dve, TRAN, tran_done, *name)

        def table(s, t, lo, n, dims):
            v = tab[:, s, t, lo:lo + n]
            for _ in dims:
                v = v.rearrange("p (o f) -> p o f", o=1) if len(v.shape) == 2 else v
            return v

        for c in range(2):
            for t in range(TT):
                n = stage_no(c, t)
                b = PROJ.no("in", c, t) % 2
                wait_done(dve, PROJ, proj_done, "in", c, t)
                stage_free(n)
                src = pp[b][:, :].rearrange("p (h f) -> p h f", f=RROT)
                dst = stage[n % 2][:, 0:512].rearrange("p (h a f) -> p h a f", a=2, f=RROT)
                for s in range(2):
                    tb = tab[:, s, t, 0:RROT].rearrange("p (o f) -> p o f", o=1).to_broadcast([P, 2 * RH, RROT])
                    ins = V.tensor_tensor(rott[:, s, :].rearrange("p (h f) -> p h f", f=RROT), src, tb, ALU.mult)
                    mark(ins)
                link()
                rs = rott[:, 0, :].rearrange("p (h a f) -> p h a f", a=2, f=RROT)
                rc = rott[:, 1, :].rearrange("p (h a f) -> p h a f", a=2, f=RROT)
                mark(V.tensor_tensor(dst[:, :, 0, :], rc[:, :, 0, :], rs[:, :, 1, :], ALU.subtract))
                V.tensor_tensor(dst[:, :, 1, :], rc[:, :, 1, :], rs[:, :, 0, :], ALU.add).then_inc(staged, 1)
                dve.wait_ge(staged, n + 1)
                dve.sem_inc(proj_free[b], 1)

        dve.wait_ge(decay_in, 16)
        for h in range(RH):
            if h >= 1:
                wait_done(dve, OUTP, outp_done, "ret", h - 1)
            for k in range(TT):
                b = SCORE.no("ret", h, k) % 2
                wait_done(dve, SCORE, score_done, "ret", h, k)
                n = T - k * P
                V.tensor_tensor(retS[:, k, 0:n], sp_[b][:, 0:n], decay[:, h, 0:n], ALU.mult).then_inc(rets_ready, 1)
                dve.wait_ge(rets_ready, TT * h + k + 1)
                dve.sem_inc(score_free[b], 1)
            b = OUTP.no("ret", h) % 2
            wait_done(dve, OUTP, outp_done, "ret", h)
            for q in range(TT):
                mark(V.bn_stats(stat[:, q, :], op[b][:, q * P:(q + 1) * P]))
            link()
            if h == 0:
                dve.wait_ge(proj_free[0], 8)
                dve.wait_ge(proj_free[1], 8)
            for q in range(TT):
                last = V.bn_aggr(mv[:, q, :], stat[:, q, :])
                if q < TT - 1:
                    mark(last)
            last.then_inc(rstd_asked, 1)
            dve.wait_ge(rstd_ready, h + 1)
            dve.wait_ge(rstd_asked, h + 1)
            link(V.reciprocal(rinv[:, 0, 0:TT], std[:, :]))
            for q in range(TT):
                mark(V.tensor_scalar(oret[:, q, h * RD:(h + 1) * RD], op[b][:, q * P:(q + 1) * P], mv[:, q, 0:1],
                                     rinv[:, 0, q:q + 1], ALU.subtract, ALU.mult))
            link()
            dve.sem_inc(outp_free[b], 1)
            V.tensor_tensor(oret[:, :, h * RD:(h + 1) * RD], oret[:, :, h * RD:(h + 1) * RD],
                            swish[:, :, h * RD:(h + 1) * RD], ALU.mult).then_inc(oret_ready, 1)

        def small_rotation(b, src_cols, heads, dst, t, dup):
            src = pp[b][:, src_cols:src_cols + heads * ND].rearrange("p (h d) -> p h d", d=ND)[:, :, 0:2 * NROT]\
                .rearrange("p h (a f) -> p h a f", a=2)
            m = heads * 2 * NROT
            for s in range(2):
                for a in range(2):
                    tb = tab[:, s, t, RROT:NFREQ].rearrange("p (o f) -> p o f", o=1).to_broadcast([P, heads, NROT])
                    o = rottn[:, s, a * heads * NROT:(a + 1) * heads * NROT].rearrange("p (h f) -> p h f", h=heads)
                    mark(V.tensor_tensor(o, src[:, :, a, :], tb, ALU.mult))
            link()
            half = lambda s, a: rottn[:, s, a * heads * NROT:(a + 1) * heads * NROT].rearrange("p (h f) -> p h f", h=heads)
            for i, d in enumerate(dst):
                mark(V.tensor_tensor(d[:, :, 0:NROT], half(1, 0), half(0, 1), ALU.subtract))
                last = V.tensor_tensor(d[:, :, NROT:2 * NROT], half(1, 1), half(0, 0), ALU.add)
                if i < len(dst) - 1:
                    mark(last)
            return last

        for c in (4, 5, 6):
            for t in range(TT):
                n = stage_no(c, t)
                b = PROJ.no("in", c, t) % 2
                dve.wait_ge(raw_staged, n - 2 * TT + 1)
                st = stage[n % 2]
                if c == 4:
                    last = small_rotation(b, 0, NH, [st[:, 512:1024].rearrange("p (h d) -> p h d", d=ND)], t, False)
                elif c == 5:
                    v = st[:, 512:768].rearrange("p (g a d) -> p g a d", a=2, d=ND)
                    last = small_rotation(b, 256, NG, [v[:, :, a, :] for a in range(2)], t, True)
                else:
                    v = st[:, 0:256].rearrange("p (g a d) -> p g a d", a=2, d=ND)
                    last = small_rotation(b, 0, NG, [v[:, :, a, :] for a in range(2)], t, True)
                last.then_inc(staged, 1)
                dve.wait_ge(staged, n + 1)
                dve.sem_inc(proj_free[b], 1)

        V.memset(hidvT[:, :, :, :, :], 0.0).then_inc(zeros_ready, 1)
        for i in range(2):
            V.memset(pc[i][:, :, :], 0.0).then_inc(zeros_ready, 1)
        dve.wait_ge(pe_in, 48)
        for i in range(2):
            m = TRAN.no("kv5", TT - 1, i)
            dve.wait_ge(tran_free[m % 2], m // 2 + 1)
        for j in range(2):
            for half in range(2):
                lo = ND * half
                for g in range(NG):
                    src = kvcT[lo:lo + ND, 2 * j + g, :]
                    last_c = V
                    for part in range(2):
                        blk = src[:, 16 * part:16 * part + 16 * NCMP].rearrange("p (c l a) -> p a l c", l=8, a=2)[:, half]
                        pe_v = pe2[lo:lo + ND, j, 8 * part:8 * part + 8].rearrange("p (l o) -> p l o", o=1)\
                            .to_broadcast([ND, 8, NCMP])
                        ins = V.tensor_tensor(ab[lo:lo + ND, j, 8 * part:8 * part + 8, g, :], blk, pe_v, ALU.add)
                        if (half, g, part) == (1, NG - 1, 1):
                            ins.then_inc(ab_ready, 1)
                        else:
                            mark(ins)

        for t in range(TT):
            if t >= 2:
                wait_done(dve, TRAN, tran_done, "pc", t - 2)
            v = pc[t % 2][:, :, 0:NCMP]
            bc = lambda a, n: ccmp[:, a, t, :].rearrange("p (o c) -> p o c", o=1).to_broadcast([P, n, NCMP])
            wide = lambda x: x.rearrange("p (h o) -> p h o", o=1).to_broadcast([P, NH, NCMP])
            for a in range(2):
                b = SCORE.no("sc", t, a) % 2
                wait_done(dve, SCORE, score_done, "sc", t, a)
                s = sp_[b][:, 0:NH // 2 * 32].rearrange("p (h c) -> p h c", c=32)[:, :, 0:NCMP]
                link(V.tensor_tensor(pc[t % 2][:, a:NH:2, 0:NCMP], s, bc(1, NH // 2), ALU.add))
                dve.sem_inc(score_free[b], 1)
            link(V.tensor_reduce(cmpm[:, :], v, AX.X, ALU.max))
            V.tensor_tensor(v, v, wide(cmpm[:, :]), ALU.subtract).then_inc(pc_asked, 1)
            dve.wait_ge(pc_exp, t + 1)
            link(V.tensor_reduce(cmpm[:, :], v, AX.X, ALU.add))
            link(V.reciprocal(cmpm[:, :], cmpm[:, :]))
            link(V.tensor_tensor(cmpm[:, :], cmpm[:, :], gate[:, t, 0:3 * NH:3], ALU.mult))
            link(V.tensor_tensor(v, v, bc(0, NH), ALU.mult))
            V.tensor_tensor(v, v, wide(cmpm[:, :]), ALU.mult).then_inc(pc_ready, 1)

        def scale_prob(n):
            _, h, br, q = ATT[n]
            dve.wait_ge(exp_ready, n + 1)
            dve.sem_inc(score_free[SCORE.no("att", n) % 2], 1)
            link(V.reciprocal(rinv[:, n % 2, 0:1], rsum[:, n % 2, 0:1]))
            v = prob[n % 2][:, 0:(q + 1) * P]
            V.tensor_scalar(v, v, rinv[:, n % 2, 0:1], gate[:, q, 3 * h + 1 + br:3 * h + 2 + br], ALU.mult, ALU.mult)\
                .then_inc(prob_ready, 1)

        for n in range(len(ATT)):
            q = ATT[n][3]
            b = SCORE.no("att", n) % 2
            wait_done(dve, SCORE, score_done, "att", n)
            diag = sp_[b][:, q * P:(q + 1) * P]
            link(V.tensor_tensor(diag, diag, causal, ALU.add))
            V.tensor_reduce(nmax[:, n % 2, 0:1], sp_[b][:, 0:(q + 1) * P], AX.X, ALU.max, negate=True).then_inc(max_ready, 1)
            if n >= 1:
                scale_prob(n - 1)
        scale_prob(len(ATT) - 1)

        def add_norm(which, kind, gains, ln_values):
            for t in range(TT):
                x = xres[:, t, :]
                for n in range(2):
                    b = PROJ.no(kind, t, n) % 2
                    wait_done(dve, PROJ, proj_done, kind, t, n)
                    half = xres[:, t, n * 512:(n + 1) * 512]
                    link(V.scalar_tensor_tensor(out=half, in0=half, scalar=ALPHA, in1=pp[b][:, :], op0=ALU.mult, op1=ALU.add))
                    dve.sem_inc(proj_free[b], 1)
                    mark(V.bn_stats(stat[:, n, :], half))
                link()
                norm_rows(which, t, gains, ln_values)

        def norm_rows(which, t, gains, ln_values):
            x = xres[:, t, :]
            V.bn_aggr(mv[:, t, :], stat[:, 0:2, :].rearrange("p a b -> p (a b)")).then_inc(var_ready, 1)
            dve.wait_ge(std_ready, TT * which + t + 1)
            dve.wait_ge(var_ready, TT * which + t + 1)
            link(V.reciprocal(rinv[:, 0, t:t + 1], std[:, t:t + 1]))
            link(V.tensor_scalar(x, x, mv[:, t, 0:1], rinv[:, 0, t:t + 1], ALU.subtract, ALU.mult))
            dve.wait_ge(ln_in, ln_values)
            link(V.tensor_tensor(x, x, gains[:, 0, :], ALU.mult))
            done = ln_ready if which < 2 else fin_ready
            V.tensor_tensor(x, x, gains[:, 1, :], ALU.add).then_inc(done, 1)
            dve.wait_ge(done, (TT * which if which < 2 else 0) + t + 1)

        add_norm(0, "out", lng, 32)

        def scale_x(n):
            dve.wait_ge(xexp_ready, n + 1)
            dve.sem_inc(score_free[SCORE.no("x", *XU[n]) % 2], 1)
            link(V.reciprocal(rinv[:, n % 2, 0:1], rsum[:, n % 2, 0:1]))
            V.tensor_scalar(probx[n % 2][:, :], probx[n % 2][:, :], rinv[:, n % 2, 0:1], None, ALU.mult)\
                .then_inc(xprob_ready, 1)

        XU = [(h, t) for h in range(XH) for t in range(TT)]
        for n in range(len(XU)):
            b = SCORE.no("x", *XU[n]) % 2
            wait_done(dve, SCORE, score_done, "x", *XU[n])
            V.tensor_reduce(nmax[:, n % 2, 0:1], sp_[b][:, 0:MEM], AX.X, ALU.max, negate=True).then_inc(xmax_ready, 1)
            if n >= 1:
                scale_x(n - 1)
        scale_x(len(XU) - 1)
        add_norm(1, "xo", lng, 64)

        bc = lambda x, shape, pat, **kw: x.rearrange(pat, **kw).to_broadcast(shape)
        dve.wait_ge(route_in, 64)
        dve.wait_ge(score_sig, 1)
        dve.sem_inc(score_free[SCORE.no("logit", 0) % 2], 1)
        link(V.tensor_tensor(biased[:, :, :], score[:, :, :], bc(rbias[:, :], [P, TT, NE], "p (o e) -> p o e", o=1), ALU.add))
        for t in range(TT):
            for g in range(GROUPS):
                mark(V.max(gtop[:, t, g, :], biased[:, t, g * EPG:(g + 1) * EPG]))
        link()
        gs = rsmall[:, 0:TT * GROUPS].rearrange("p (t g) -> p t g", t=TT)
        gsort = rsmall[:, 32:64].rearrange("p (t g) -> p t g", t=TT)
        gok = rsmall[:, 64:96].rearrange("p (t g) -> p t g", t=TT)
        gpen = rsmall[:, 96:128].rearrange("p (t g) -> p t g", t=TT)
        link(V.tensor_tensor(gs, gtop[:, :, :, 0], gtop[:, :, :, 1], ALU.add))
        for t in range(TT):
            mark(V.max(gsort[:, t, :], gs[:, t, :]))
        link()
        for t in range(TT):
            mark(V.tensor_scalar(gok[:, t, :], gs[:, t, :], gsort[:, t, TOPG - 1:TOPG], None, ALU.is_ge))
        link()
        link(V.tensor_scalar(gpen, gok, -1.0, -NEG, ALU.add, ALU.mult))
        m4 = lambda x: x.rearrange("p t (g e) -> p (t g) e", g=GROUPS)
        wide = lambda x: x.rearrange("p t (g o) -> p (t g) o", o=1).to_broadcast([P, TT * GROUPS, EPG])
        link(V.tensor_tensor(m4(tmpa[:, :, :]), m4(biased[:, :, :]), wide(gok), ALU.mult))
        link(V.tensor_tensor(m4(tmpa[:, :, :]), m4(tmpa[:, :, :]), wide(gpen), ALU.add))
        top = rsmall[:, 128:160].rearrange("p (t k) -> p t k", t=TT)
        tidx = rsmall[:, 160:192].bitcast(U32).rearrange("p (t k) -> p t k", t=TT)
        tidf = rsmall[:, 192:224].rearrange("p (t k) -> p t k", t=TT)
        for t in range(TT):
            mark(V.max(top[:, t, :], tmpa[:, t, :]))
        link()
        for t in range(TT):
            mark(V.max_index(tidx[:, t, :], top[:, t, :], tmpa[:, t, :]))
        link()
        link(V.tensor_copy(tidf, tidx))
        iota64, iota8 = rcon[:, R_IOTA:R_IOTA + NE], rcon[:, R_IOTA:R_IOTA + TOPK]
        for t in range(TT):
            sh = [P, TOPK, NE]
            link(V.tensor_tensor(hot8[:, :, :], bc(iota64, sh, "p (o e) -> p o e", o=1),
                                 bc(tidf[:, t, :], sh, "p (k o) -> p k o", o=1), ALU.is_equal))
            mark(V.tensor_reduce(maskt[:, t, :], hot8[:, :, :].rearrange("p k e -> p e k"), AX.X, ALU.add))
            link(V.tensor_tensor(hot8w[:, :, :], hot8[:, :, :], bc(score[:, t, :], sh, "p (o e) -> p o e", o=1), ALU.mult))
            link(V.tensor_reduce(wtop[:, t, :], hot8w[:, :, :], AX.X, ALU.add))
            link(V.tensor_tensor(hot8w[:, :, :], hot8[:, :, :], bc(iota8, sh, "p (k o) -> p k o", o=1), ALU.mult))
            link(V.tensor_reduce(krank[:, t, :], hot8w[:, :, :].rearrange("p k e -> p e k"), AX.X, ALU.add))
        dve.sem_inc(mask_ready, 1)
        ws = rsmall[:, 224:228]
        link(V.tensor_reduce(ws, wtop[:, :, :], AX.X, ALU.add))
        link(V.reciprocal(ws, ws))
        link(V.tensor_scalar(ws, ws, SCALE_W, None, ALU.mult))
        link(V.tensor_tensor(wtop[:, :, :], wtop[:, :, :], bc(ws, [P, TT, TOPK], "p (t o) -> p t o", o=1), ALU.mult))

        for t in range(TT):
            b = PROJ.no("sgu", t) % 2
            dve.wait_ge(sgate_ready, t + 1)
            V.tensor_tensor(sact[:, t, :], sgate[:, :], pp[b][:, FF:2 * FF], ALU.mult).then_inc(sact_ready, 1)
            dve.wait_ge(sact_ready, t + 1)
            dve.sem_inc(proj_free[b], 1)
        dve.wait_ge(x2_saved, 16 * TT)
        for t in range(TT):
            for n in range(2):
                b = PROJ.no("sdn", t, n) % 2
                wait_done(dve, PROJ, proj_done, "sdn", t, n)
                half = xres[:, t, n * 512:(n + 1) * 512]
                link(V.scalar_tensor_tensor(out=half, in0=half, scalar=ALPHA, in1=pp[b][:, :], op0=ALU.mult, op1=ALU.add))
                dve.sem_inc(proj_free[b], 1)

        wait_done(dve, SCORE, score_done, "pos", 0)
        b = SCORE.no("pos", 0) % 2
        link(V.tensor_scalar(tmpa[:, :, :], maskt[:, :, :], -1.0, FAR, ALU.add, ALU.mult))
        link(V.tensor_tensor(posm[:, :, :], sp_[b][:, 0:TT * NE].rearrange("p (t e) -> p t e", t=TT), tmpa[:, :, :], ALU.add))
        ecol, etmp = rsmall[0:NE, 512:513], rsmall[0:NE, 513:516]
        for i in range(3):
            mark(V.tensor_scalar(etmp[:, i:i + 1], sp_[b][0:NE, 384:385], float(BLK * (i + 1)), None, ALU.is_gt))
        link()
        dve.sem_inc(score_free[b], 1)
        link(V.tensor_reduce(ecol, etmp, AX.X, ALU.add))
        V.tensor_copy(rsmall[0:NE, 768:768 + P], ecol.to_broadcast([NE, P])).then_inc(extra_ready, 1)
        wait_done(dve, SCORE, score_done, "extra", 0)
        b = SCORE.no("extra", 0) % 2
        cum, n_extra = rsmall[0:NE, 516:517], rsmall[:, 517:518]
        mark(V.tensor_copy(cum, sp_[b][0:NE, 0:1]))
        link(V.tensor_copy(n_extra, sp_[b][:, 1:2]))
        dve.sem_inc(score_free[b], 1)
        V.tensor_scalar(rsmall[0:NE, 640:640 + EXTRA], rcon[0:NE, R_IOTA:R_IOTA + EXTRA], cum, None, ALU.is_ge)\
            .then_inc(extra_ready, 1)
        wait_done(dve, SCORE, score_done, "cum", 0)
        b = SCORE.no("cum", 0) % 2
        mark(V.tensor_copy(itab[:, 0:NE], rcon[:, R_IOTA:R_IOTA + NE]))
        mark(V.memset(boff[:, 0:NE], 0.0))
        link(V.tensor_scalar(itab[:, NE:ITEMS], sp_[b][:, 0:EXTRA], float(NE - 1), None, ALU.min))
        bx = boff[:, NE:ITEMS]
        past = rsmall[:, 704:704 + EXTRA]
        link(V.tensor_tensor(bx, rcon[:, R_IOTA:R_IOTA + EXTRA], sp_[b][:, 64:64 + EXTRA], ALU.subtract))
        link(V.tensor_scalar(bx, bx, 1.0, float(BLK), ALU.add, ALU.mult))
        link(V.tensor_scalar(past, rcon[:, R_IOTA:R_IOTA + EXTRA], n_extra, FAR, ALU.is_ge, ALU.mult))
        link(V.tensor_tensor(bx, bx, past, ALU.add))
        dve.sem_inc(score_free[b], 1)
        mark(V.tensor_copy(itabi[:, 0:ITEMS], itab[:, :]))
        half_n = rsmall[:, 518:519]
        link(V.tensor_scalar(half_n, n_extra, float(NE) + 0.5, 0.5, ALU.add, ALU.mult))
        link(V.tensor_scalar(half_n, half_n, M, M, ALU.add, ALU.subtract))
        mark(V.tensor_copy(itabi[:, ITEMS:ITEMS + 1], half_n))
        mark(V.tensor_copy(info[:, :, 0], rcon[:, R_TOK:R_TOK + TT]))
        link(V.tensor_copy(info[:, :, 1], rcon[:, R_TOK + TT:R_TOK + 2 * TT]))
        link(V.memset(info[:, :, 3:4], 0.0))
        dve.sem_inc(list_ready, 1)

        for b in range(2):
            V.memset(xg[b][:, :], 0.0).then_inc(moe_set, 1)
            V.memset(ysb[b][:, :], 0.0).then_inc(moe_set, 1)
            V.memset(scur[b][:, :], int(OOB) * TOPK).then_inc(moe_set, 1)
        iota_b = mcon[:, :].rearrange("p (o s) -> p o s", o=1).to_broadcast([P, TT, BLK])

        def chain(ins, when):
            ins.then_inc(loop_step, 1)
            dve.wait_ge(loop_step, when)

        def one_hot(e, item, when):
            V.tensor_copy(info[:, :, 2], krank[:, :, e])
            chain(V.tensor_scalar(rel[:, :], posm[:, :, e], boff[:, item], None, ALU.subtract), when)
            V.tensor_tensor(onehot[:, :, :], iota_b,
                            rel[:, :].rearrange("p (t o) -> p t o", o=1).to_broadcast([P, TT, BLK]), ALU.is_equal)\
                .then_inc(hot_ready, 1)

        def row_numbers(b, when):
            i = pp[1]
            chain(V.tensor_scalar(gfl[:, :], i[:, 0:1], OOB, i[:, 1:2], ALU.add, ALU.add), when)
            V.tensor_copy(gidx[b][:, :], gfl[:, :])
            V.scalar_tensor_tensor(out=snext[b][:, :], in0=gfl[:, :], scalar=float(TOPK), in1=i[:, 2:3],
                                   op0=ALU.mult, op1=ALU.add).then_inc(idx_ready, 1)

        def half_T():
            V.tensor_copy(xgT[:, 4:8, :], tp[1][:, :].rearrange("p (k t) -> p k t", k=4)).then_inc(xgT_d, 1)

        dve.wait_ge(list_ready, 1)
        for b in range(2):
            if b == 1:
                dve.wait_ge(idx_done, 1)
            one_hot(slice(b, b + 1), slice(b, b + 1), 2 * b + 1)
            dve.wait_ge(idx_done, b + 1)
            row_numbers(b, 2 * b + 2)
        dve.sem_inc(y_dve, 1)
        dve.wait_ge(xgT_done, 1)
        half_T()
        pairs = dve.value_load(itabi[0:1, ITEMS:ITEMS + 1], min_val=NE // 2, max_val=(NE + MAX_EXTRA + 1) // 2)
        with dve.Fori(0, pairs) as j:
            for b in range(2):
                e = dve.value_load(itabi[0:1, DS(j * 2 + (b + 2), 1)], min_val=0, max_val=NE - 1)
                dve.wait_ge(scattered[b], j * 16 + 16)
                dve.wait_ge(idx_ready, j * 2 + (b + 2))
                V.tensor_copy(scur[b][:, :], snext[b][:, :]).then_inc(scur_ready, 1)
                one_hot(DS(e, 1), DS(j * 2 + (b + 2), 1), j * 4 + (2 * b + 5))
                dve.wait_ge(h_done, j * 2 + (b + 1))
                dve.wait_ge(egate_ready, j * 2 + (b + 1))
                V.tensor_tensor(eact[:, :], egate[:, :], pp[0][:, FF:2 * FF], ALU.mult).then_inc(eact_ready, 1)
                dve.wait_ge(idx_done, j * 2 + (b + 3))
                dve.wait_ge(gathered[b], j * 16 + 16)
                dve.wait_ge(scur_ready, j * 2 + (b + 1))
                row_numbers(b, j * 4 + (2 * b + 6))
                dve.wait_ge(xgT_done, j * 2 + (b + 2))
                half_T()
                dve.wait_ge(y_done, j * 2 + (b + 1))
                V.tensor_copy(ysb[b][:, 512:1024], op[1][:, :]).then_inc(y_dve, 1)

        for t in range(TT):
            x = xres[:, t, :]
            dve.wait_ge(y_in[t % 2], 16 * (t // 2 + 1))
            for k in range(TOPK):
                ins = V.scalar_tensor_tensor(out=x, in0=yb[t % 2][:, k, :], scalar=wtop[:, t, k:k + 1], in1=x,
                                             op0=ALU.mult, op1=ALU.add)
                link(ins)
            dve.sem_inc(sum_done, 1)
            for n in range(2):
                mark(V.bn_stats(stat[:, n, :], xres[:, t, n * 512:(n + 1) * 512]))
            link()
            norm_rows(2, t, lng3, 96)

    ctx.close()


_INS = ["x", "mem", "positions", "w_in", "cmp_pe_k", "cmp_pe_v", "cmp_w1_k", "cmp_w2_k", "cmp_w1_v", "cmp_w2_v",
        "w_out", "ln1_g", "ln1_b", "w_xq", "w_xkv", "w_xo", "ln2_g", "ln2_b", "w_router", "router_bias",
        "w_gate", "w_up", "w_down", "ws_gate", "ws_up", "ws_down", "ln3_g", "ln3_b"]


def kernel(**inputs):
    import numpy as _np
    import concourse.bacc as _bacc
    from concourse.bass_utils import run_bass_kernel_spmd as _run

    nc = _bacc.Bacc("TRN2", target_bir_lowering=False, num_devices=1)
    arrays = {f"in_{n}": _np.ascontiguousarray(inputs[n])[0] for n in _INS}
    arrays.update({f"in_{n}": a for n, a in constants().items()})
    io = {n[3:]: nc.dram_tensor(n, a.shape, mybir.dt.from_np(a.dtype), kind="ExternalInput").ap()
          for n, a in arrays.items()}
    out = nc.dram_tensor("out_0", (T, D), F32, kind="ExternalOutput").ap()
    build(nc, io, out)
    r = _run(nc, [arrays], core_ids=[0])
    return r.results[0]["out_0"].reshape(1, T, D)
```

```python
from contextlib import ExitStack

import numpy as np

import concourse.bass as bass
from concourse import mybir

F32 = mybir.dt.float32
BF16 = mybir.dt.bfloat16
I32 = mybir.dt.int32
U32 = mybir.dt.uint32
ALU = mybir.AluOpType
ACT = mybir.ActivationFunctionType
AX = mybir.AxisListType
DS = bass.DynSlice

P = 128
T = 512
D = 1024
TT = T // P
KD = D // P
MEM = 256
ALPHA = 2.0 ** 0.25
EPS = 1e-5
NEG = -1e30

RH, RD = 4, 128
NH, NG, ND = 8, 2, 64
HPG = NH // NG
NCMP, CMP_LEN, CMP_STRIDE, CMP_HID = 31, 32, 16, 256
RROT, NROT = RD // 2, 8
NFREQ = RROT + NROT
XH = 4

NE, TOPK, GROUPS, TOPG, FF = 64, 8, 8, 4, 256
EPG = NE // GROUPS
SCALE_W = 2.5
BLK = 128
MAX_EXTRA = T * TOPK // BLK - 1
EXTRA = 40
ITEMS = NE + EXTRA
FAR = 1.0e6
OOB = 8192.0

C_ID, C_CAUS, C_INV, C_EPS = 0, 128, 256, 256 + NFREQ
NC_A = C_EPS + 4
NC_B = TT * NCMP * 2
R_TRI, R_ONE, R_IOTA, R_TRI64, R_TOK = 0, 128, 256, 384, 448
NC_R = R_TOK + 2 * TT


def constants():
    p = np.arange(P)
    a = np.zeros((P, NC_A), np.float32)
    a[:, C_ID:C_ID + P] = np.eye(P)
    a[:, C_CAUS:C_CAUS + P] = np.where(p[None, :] <= p[:, None], 0.0, NEG)
    inv_r = 10000.0 ** (-np.arange(RROT) / RROT)
    inv_n = 500000.0 ** (-np.arange(NROT) / NROT)
    a[:, C_INV:C_INV + NFREQ] = np.concatenate([inv_r, inv_n])[None, :]
    a[:, C_EPS] = EPS
    t = np.arange(TT)[None, :, None] * P + p[:, None, None]
    ok = CMP_STRIDE * np.arange(NCMP)[None, None, :] + CMP_LEN - 1 <= t
    b = np.stack([ok.astype(np.float32), np.where(ok, 0.0, NEG)], 1).reshape(P, -1).astype(np.float32)
    decay = np.zeros((P, RH, T), np.float64)
    rel = np.arange(T)[None, :] - p[:, None]
    for h in range(RH):
        decay[:, h] = np.where(rel >= 0, np.exp(np.log(1 - 2.0 ** (-5 - h)) * np.maximum(rel, 0)), 0) * RD ** -0.5
    r = np.zeros((P, NC_R), np.float32)
    r[:, R_TRI:R_TRI + P] = p[:, None] < p[None, :]
    r[:, R_ONE:R_ONE + P] = 1.0
    r[:, R_IOTA:R_IOTA + P] = p[None, :]
    e = np.arange(NE)
    r[:NE, R_TRI64:R_TRI64 + NE] = e[:, None] <= e[None, :]
    r[:, R_TOK:R_TOK + TT] = p[:, None]
    r[:, R_TOK + TT:R_TOK + 2 * TT] = np.arange(TT)[None, :] * P - OOB
    return {"c_first": a, "c_cmp": b, "c_decay": decay.reshape(P, -1).astype(np.float32), "c_route": r}


class Units:

    def __init__(self, names):
        self.at = {name: n for n, name in enumerate(names)}
        self.n = len(names)

    def no(self, *name):
        return self.at[name if len(name) > 1 else name[0]]


W_COLS = [512] * 6 + [280]
PROJ = Units([("in", c, t) for c in range(7) for t in range(TT)]
             + [("xk", d) for d in range(KD)]
             + [("out", t, n) for t in range(TT) for n in range(2)]
             + [("xv", m, n) for n in range(2) for m in range(2)]
             + [("xq", d) for d in range(KD)]
             + [("xo", t, n) for t in range(TT) for n in range(2)]
             + [("sgu", t) for t in range(TT)] + [("sdn", t, n) for t in range(TT) for n in range(2)])
ATT = [(pr, h, br, q) for pr in range(NH // 2) for q in range(TT) for br in range(2) for h in (2 * pr, 2 * pr + 1)]
STAGED = [(c, t) for c in (0, 1, 4, 5, 6) for t in range(TT)]


def staged_units(c, t):
    return [("ret", c, t)] if c < 2 else [("nq", t, 0), ("nq", t, 1)] if c == 4 \
        else [("kv5", t, 0), ("kv5", t, 1)] if c == 5 else [("kv6", t)]


def x_units(t):
    return [("x", t, j) for j in range(2)]


TRAN = Units(x_units(0) + x_units(1) + x_units(2) + staged_units(0, 0) + x_units(3)
             + [u for c, t in STAGED[1:12] for u in staged_units(c, t)]
             + [("oret", t) for t in range(TT)]
             + [u for c, t in STAGED[12:] for u in staged_units(c, t)]
             + [("mem", m, j) for m in range(2) for j in range(2)]
             + [("hid", j) for j in range(2)]
             + [("pc", t) for t in range(TT)]
             + [("pt", n) for n in range(len(ATT))]
             + [("x1", t, j) for t in range(TT) for j in range(2)]
             + [("px", h, t) for h in range(XH) for t in range(TT)]
             + [("x2", t, j) for t in range(TT) for j in range(2)]
             + [("sh", t) for t in range(TT)])
SCORE = Units([("ret", h, k) for h in range(RH) for k in range(TT)]
              + [("hid", j) for j in range(2)] + [("kvc", 0)]
              + [("sc", t, a) for t in range(TT) for a in range(2)]
              + [("x", h, t) for h in range(XH) for t in range(TT)]
              + [("logit", t) for t in range(TT)] + [("pos", 0), ("extra", 0), ("cum", 0)])
OUTP = Units([("ret", h) for h in range(RH)] + [("nsa", pr) for pr in range(NH // 2)]
             + [("x", h, d) for h in range(XH) for d in range(2)])

CHUNKS = ([("in", c) for c in range(7)] + [("w1", 0), ("w1", 1)] + [("xkv", 0), ("xkv", 1)]
          + [("out", 0), ("out", 1), ("xkv", 2), ("xkv", 3), ("xq", 0), ("xq", 1), ("xo", 0), ("xo", 1), ("sgu", 0), ("sdn", 0)])
SLOT = [n % 4 for n in range(len(CHUNKS))]
SLOT[-1] = 2
CHUNK_NO = {name: n for n, name in enumerate(CHUNKS)}


def loads_before(n):
    return sum(SLOT[m] == SLOT[n] for m in range(n + 1))


def last_in_slot(slot, before):
    found = [m for m in range(before) if SLOT[m] == slot]
    return found[-1] if found else None


def build(nc, io, out):
    ctx = ExitStack()
    base = (nc.sbuf_base + 31) // 32 * 32
    KB = 1024

    def at(name, shape, dt, offset):
        return nc.alloc_sbuf_tensor_at(name, shape, dt, offset=base + offset)

    def sem(name):
        return ctx.enter_context(nc.semaphore(name))

    O_RING, O_DOWN, O_X, O_A, O_B, O_C, O_D, O_E, O_F = (k * KB for k in (0, 64, 96, 112, 128, 144, 160, 176, 200))
    ring = [at(f"ring{s}", [P, 4096], F32, O_RING + s * 16 * KB) for s in range(4)]
    xres = at("xres", [P, TT, D], F32, O_X)
    xT = at("xT", [P, KD, T], F32, O_A)
    nqT = at("nqT", [P, NH // 2, T], F32, O_DOWN)
    nqrT = at("nqrT", [P, NH // 2, T], F32, O_DOWN + 8 * KB)
    kT = [at(f"k{n}T", [P, NG, 2, T], F32, O_DOWN + (16 + 8 * k) * KB) for k, n in enumerate(("sel", "win"))]
    retT = [at(f"ret{n}T", [P, RH, T], F32, O_C + k * 8 * KB) for k, n in enumerate("qk")]
    rv = at("rv", [P, TT, RH * RD], F32, O_D)
    swish = at("swish", [P, TT, RH * RD], F32, O_D + 8 * KB)
    decay = at("decay", [P, RH, T], F32, O_E)
    retS = at("retS", [P, TT, T], F32, O_E + 8 * KB)
    oret = at("oret", [P, TT, RH * RD], F32, O_E + 16 * KB)
    mixT = at("mixT", [P, KD, T], F32, O_B)
    ang = at("ang", [P, TT, NFREQ], F32, O_B)
    turns = at("turns", [P, 2, TT, NFREQ], F32, O_B + 2 * KB)
    stage = [at(f"stage{b}", [P, D], F32, O_B + (8 + 4 * b) * KB) for b in range(2)]
    kvcT = at("kvcT", [P, 4, T], F32, O_D)
    ab = at("ab", [P, 2, 16, NG, NCMP], F32, O_D + 8 * KB)
    w2k = at("w2k", [P, 2, 2, ND], F32, O_C)
    w2v = at("w2v", [P, 2, ND], F32, O_C + 1024)
    hid = at("hid", [NG * NCMP, 2, CMP_HID], F32, O_C + 1536)
    hidkT = at("hidkT", [P, 2, NG * NCMP], F32, O_C + 3584)
    hidvT = at("hidvT", [P, 2, NG, HPG, 32], F32, O_C + 4096)
    pc = [at(f"pc{b}", [P, NH, 32], F32, O_C + 6144 + b * 1024) for b in range(2)]
    pcT = at("pcT", [P, NG, T], F32, O_C + 8 * KB)
    vsw = at("vsw", [P, 2, TT, NG * ND], F32, O_C + 12 * KB)
    PT = [at(f"PT{b}", [P, TT, P], F32, O_E + b * 2 * KB) for b in range(8)]
    prob = [at(f"prob{b}", [P, T], F32, O_E + (16 + 2 * b) * KB) for b in range(4)]
    vcmp = at("vcmp", [P, HPG, NG, ND], F32, O_C + 1536)
    mem_in = at("mem_in", [P, 2, D], F32, O_E)
    memT = at("memT", [P, KD, MEM], F32, O_D)
    kxT = at("kxT", [P, KD, MEM], F32, O_A)
    vx = at("vx", [P, 2, D], F32, O_A + 8 * KB)
    x1T = at("x1T", [P, KD, T], F32, O_C)
    xqT = at("xqT", [P, KD, T], F32, O_B)
    xoT = at("xoT", [P, KD, T], F32, O_C)
    PX = [at(f"PX{b}", [P, 2, T], F32, O_E + b * 4 * KB) for b in range(2)]
    probx = [at(f"probx{b}", [P, MEM], F32, O_E + (8 + b) * KB) for b in range(2)]
    lng = at("lng", [P, 2, D], F32, O_D + 8 * KB)
    x2T = at("x2T", [P, KD, T], F32, O_B)
    sgate = at("sgate", [P, FF], F32, O_C)
    sact = at("sact", [P, TT, FF], F32, O_C + 1 * KB)
    sactT = at("sactT", [P, 2, T], F32, O_C + 5 * KB)
    wrt = at("wrt", [P, KD, NE], F32, O_E + 22 * KB)
    rcon = at("rcon", [P, NC_R], F32, O_A + 6 * KB)
    rbias = at("rbias", [P, NE], F32, O_A + 8 * KB)
    score = at("score", [P, TT, NE], F32, O_D)
    biased = at("biased", [P, TT, NE], F32, O_D + 1 * KB)
    tmpa = at("tmpa", [P, TT, NE], F32, O_D + 2 * KB)
    hot8 = at("hot8", [P, TOPK, NE], F32, O_D + 3 * KB)
    maskt = at("maskt", [P, TT, NE], F32, O_A)
    gtop = at("gtop", [P, TT, GROUPS, 8], F32, O_A + 1 * KB)
    rsmall = at("rsmall", [P, 1024], F32, O_A + 2 * KB)
    wdown = [at(f"wdown{b}", [P, 2, D], F32, O_DOWN + b * 8 * KB) for b in range(2)]
    xg = [at(f"xg{b}", [P, D], F32, O_DOWN + (16 + 4 * b) * KB) for b in range(2)]
    ysb = [at(f"ysb{b}", [P, D], F32, O_DOWN + (24 + 4 * b) * KB) for b in range(2)]
    xgT = at("xgT", [P, KD, BLK], F32, O_E)
    egate = at("egate", [P, FF], F32, O_E + 4 * KB)
    eact = at("eact", [P, FF], F32, O_E + 5 * KB)
    eactT = at("eactT", [P, 2, BLK], F32, O_E + 6 * KB)
    onehot = at("onehot", [P, TT, BLK], BF16, O_E + 7 * KB)
    posm = at("posm", [P, TT, NE], F32, O_E + 8 * KB)
    wexp = at("wexp", [P, TT, NE], F32, O_A + 10 * KB)
    wpart = at("wpart", [P, TT, NE, 4], BF16, O_A + 12 * KB)
    info = at("info", [P, TT, 8], BF16, O_E + 10 * KB)
    itab = at("itab", [P, ITEMS], F32, O_E + 10 * KB + 256)
    itabi = at("itabi", [P, ITEMS + 2], I32, O_E + 11 * KB)
    boff = at("boff", [P, ITEMS], F32, O_E + 11 * KB + 512)
    rel = at("rel", [P, TT], F32, O_E + 12 * KB)
    gidx = [at(f"gidx{b}", [P, 1], I32, O_E + 12 * KB + 64 + 32 * b) for b in range(2)]
    snext = [at(f"snext{b}", [P, 2], F32, O_E + 12 * KB + 128 + 32 * b) for b in range(2)]
    scur = [at(f"scur{b}", [P, 1], I32, O_E + 12 * KB + 192 + 32 * b) for b in range(2)]
    wcur = [at(f"wcur{b}", [P, 1], F32, O_E + 12 * KB + 448 + 32 * b) for b in range(2)]
    first_down = at("first_down", [P, 8], F32, O_E + 12 * KB + 384)
    smid = [at(f"smid{b}", [P, 2], F32, O_E + 12 * KB + 320 + 32 * b) for b in range(2)]
    gfl = at("gfl", [P, 1], F32, O_E + 12 * KB + 256)
    mcon = at("mcon", [P, BLK], F32, O_E + 12 * KB + 512)
    lng3 = at("lng3", [P, 2, D], F32, O_E + 14 * KB)
    c1 = at("c1", [P, NC_A], F32, O_F)
    tab = at("tab", [P, 2, TT, NFREQ], F32, O_F + 1536)
    gate = at("gate", [P, TT, 3 * NH], F32, O_F + 3840)
    kcmpT = at("kcmpT", [P, NG * NCMP], F32, O_F + 4736)
    ccmp = at("ccmp", [P, 2, TT, NCMP], F32, O_F + 4992)
    posi = at("posi", [P, TT], I32, O_F + 6016)
    posf = at("posf", [P, TT], F32, O_F + 6048)
    stat = at("stat", [P, 4, 6], F32, O_F + 6080)
    mv = at("mv", [P, TT, 2], F32, O_F + 6208)
    std = at("std", [P, TT], F32, O_F + 6240)
    nmax = at("nmax", [P, 2, 8], F32, O_F + 6272)
    rsum = at("rsum", [P, 2, 8], F32, O_F + 6336)
    rinv = at("rinv", [P, 2, 8], F32, O_F + 6400)
    cmpm = at("cmpm", [P, NH], F32, O_F + 6496)
    pe2 = at("pe2", [P, 2, 16], F32, O_F + 6528)
    rott = at("rott", [P, 2, 512], F32, O_E + 16 * KB)
    rottn = at("rottn", [P, 2, 2 * NH * NROT], F32, O_F + 6656)

    ident = c1[:, C_ID:C_ID + P]
    causal = c1[:, C_CAUS:C_CAUS + P]
    eps = c1[:, C_EPS:C_EPS + 1]

    def pair(name):
        return [ctx.enter_context(nc.psum_tensor(f"{name}{b}", [P, 512], F32)) for b in range(2)]

    pp, tp, sp_, op = pair("proj"), pair("tran"), pair("score"), pair("outp")

    att_banks = sp_ + pp

    x2_dram = nc.dram_tensor("x2_rows", [T, D], F32, kind="Internal").ap()
    sum_dram = nc.dram_tensor("sum_rows", [T, D], F32, kind="Internal").ap()

    x_in = [sem(f"x_in{t}") for t in range(TT)]
    const_in, decay_in, mem_loaded, cmp_in = (sem(n) for n in ("const_in", "decay_in", "mem_loaded", "cmp_in"))
    ln_in = [sem(f"ln{n + 1}_in") for n in range(3)]
    pe_in, route_in = sem("pe_in"), sem("route_in")
    first_in = sem("first_in")
    loaded = [sem(f"loaded{s}") for s in range(4)]
    proj_done, tran_done, score_done, outp_done = (sem(n) for n in ("proj_done", "tran_done", "score_done", "outp_done"))
    proj_free, tran_free, score_free, outp_free = ([sem(f"{n}_free{b}") for b in range(2)] for n in ("proj", "tran", "score", "outp"))
    dve_step, act_step = sem("dve_step"), sem("act_step")
    angles_ready, tables_ready = sem("angles_ready"), sem("tables_ready")
    staged, raw_staged = sem("staged"), sem("raw_staged")
    sig_read = sem("sig_read")
    gates_ready = sem("gates_ready")
    rets_ready, rstd_asked, rstd_ready, oret_ready = (sem(n) for n in ("rets_ready", "rstd_asked", "rstd_ready", "oret_ready"))
    pads_ready = sem("pads_ready")
    zeros_ready, pv_done, smid_ready, loop_step = (sem(n) for n in ("zeros_ready", "pv_done", "smid_ready", "loop_step"))
    sp_turn = sem("sp_turn")
    offset_turn = sem("offset_turn")
    pool_turn = sem("pool_turn")
    ab_ready, hid_ready, kvcmp_ready = sem("ab_ready"), sem("hid_ready"), sem("kvcmp_ready")
    pc_asked, pc_exp, pc_ready = sem("pc_asked"), sem("pc_exp"), sem("pc_ready")
    att_scored = sem("att_scored")
    max_ready, exp_ready, prob_ready = sem("max_ready"), sem("exp_ready"), sem("prob_ready")
    var_ready, std_ready = sem("var_ready"), sem("std_ready")
    ln_ready = sem("ln_ready")
    xmax_ready, xexp_ready, xprob_ready = sem("xmax_ready"), sem("xexp_ready"), sem("xprob_ready")
    sgate_ready, sact_ready = sem("sgate_ready"), sem("sact_ready")
    score_sig, mask_ready, extra_ready = (sem(n) for n in ("score_sig", "mask_ready", "extra_ready"))
    x2_saved = sem("x2_saved")
    e_gu_in = [sem(f"e_gu_in{b}") for b in range(2)]
    e_dn_in = [sem(f"e_dn_in{b}") for b in range(2)]
    hot_ready, idx_done, idx_ready = sem("hot_ready"), sem("idx_done"), sem("idx_ready")
    gathered = [sem(f"gathered{b}") for b in range(2)]
    scattered = [sem(f"scattered{b}") for b in range(2)]
    xgT_done, xgT_a, xgT_d = sem("xgT_done"), sem("xgT_a"), sem("xgT_d")
    h_done, egate_ready, eact_ready, eT_done, eT_ready = (sem(n) for n in ("h_done", "egate_ready", "eact_ready", "eT_done", "eT_ready"))
    y_done, y_act, y_dve = sem("y_done"), sem("y_act"), sem("y_dve")
    list_ready, moe_set = sem("list_ready"), sem("moe_set")
    half_added = sem("half_added")
    base_ready, base_saved, w_ready = sem("base_ready"), sem("base_saved"), sem("w_ready")
    sum_in = [sem(f"sum_in{t}") for t in range(TT)]
    normed, gained, fin_ready, out_saved = sem("normed"), sem("gained"), sem("fin_ready"), sem("out_saved")

    def stage_no(c, t):
        return STAGED.index((c, t))

    def stage_free(eng, n):
        if n >= 2:
            wait_done(eng, TRAN, tran_done, *staged_units(*STAGED[n - 2])[-1])

    def wait_done(eng, units, done, *name):
        eng.wait_ge(done, units.no(*name) + 1)

    def chunk_view(slot, blocks, cols):
        return ring[slot][:, 0:blocks * cols].rearrange("p (k n) -> p k n", k=blocks)

    def chunk_parts(name):
        kind, c = name
        n = CHUNK_NO[name]
        kp = lambda w: w.rearrange("(k p) n -> p k n", p=P)
        if kind == "in":
            v = chunk_view(SLOT[n], KD, W_COLS[c])
            src = kp(io["w_in"][:, 512 * c:512 * c + W_COLS[c]])
            return v, [(v, src)] if c > 0 else [(v[:, KD // 2:], src[:, KD // 2:])]
        if kind == "w1":
            v = chunk_view(SLOT[n], 16, CMP_HID)
            return v, [(v, kp(io["cmp_w1_k" if c == 0 else "cmp_w1_v"]))]
        if kind == "sgu":
            v = ring[SLOT[n]][:, :].rearrange("p (g k n) -> p g k n", g=2, k=KD)
            return v, [(v[:, 0], kp(io["ws_gate"])), (v[:, 1], kp(io["ws_up"]))]
        if kind == "sdn":
            v = chunk_view(SLOT[n], 2, D)
            return v, [(v, kp(io["ws_down"]))]
        w = {"xkv": "w_xkv", "out": "w_out", "xq": "w_xq", "xo": "w_xo"}[kind]
        v = chunk_view(SLOT[n], KD, 512)
        return v, [(v, kp(io[w][:, 512 * c:512 * c + 512]))]

    def chunk_loaded(name):
        n = CHUNK_NO[name]
        return loaded[SLOT[n]], 16 * sum(len(chunk_parts(CHUNKS[m])[1]) for m in range(n + 1) if SLOT[m] == SLOT[n])

    def chunk_used(name):
        kind, c = name
        if kind == "w1":
            return score_done, SCORE.no("hid", c) + 1
        last = {"in": ("in", c, TT - 1), "xkv": ("xk", 4 * c + 3) if c < 2 else ("xv", 1, c - 2),
                "out": ("out", TT - 1, 1), "xq": ("xq", 4 * c + 3), "xo": ("xo", TT - 1, 1),
                "sgu": ("sgu", TT - 1), "sdn": ("sdn", TT - 1, 1)}[kind]
        return proj_done, PROJ.no(*last) + 1

    def pv_done_at(group):
        pr, q = divmod(group, TT)
        return (outp_done, OUTP.no("nsa", pr) + 1) if q == TT - 1 else (pv_done, (TT - 1) * pr + q + 1)

    POOL_TILES = 2
    block = ctx.enter_context(nc.Block())

    @block.sync
    def _(sp):
        def load_x(t):
            sp.dma_start(xres[:, t, :], io["x"][t * P:(t + 1) * P, :]).then_inc(x_in[t], 16)

        load_x(0)
        half = KD // 2 * P
        sp.dma_start(chunk_view(0, KD, W_COLS[0])[:, 0:KD // 2],
                     io["w_in"][0:half, 0:W_COLS[0]].rearrange("(k p) n -> p k n", p=P)).then_inc(first_in, 16)
        for n, name in enumerate(CHUNKS):
            if n == 1:
                for t in range(1, TT):
                    load_x(t)
            before = last_in_slot(SLOT[n], n)
            if before is not None:
                sp.wait_ge(*chunk_used(CHUNKS[before]))
            for dst, src in chunk_parts(name)[1]:
                sp.dma_start(dst, src).then_inc(loaded[SLOT[n]], 16)

        gu = [ring[b][:, :].rearrange("p (g k n) -> p g k n", g=2, k=KD) for b in range(2)]

        def load_expert(b, e):
            for g, w in enumerate(("w_gate", "w_up")):
                sp.dma_start(gu[b][:, g], io[w][DS(e, 1), :, :].rearrange("o (p k) n -> p (o k) n", k=KD))\
                  .then_inc(e_gu_in[b], 16)

        def load_down(b, e):
            sp.dma_start(wdown[b][:, :, :], io["w_down"][DS(e, 1), :, :].rearrange("o (p k) n -> p (o k) n", k=2))\
              .then_inc(e_dn_in[b], 16)

        for b in range(2):
            sp.wait_ge(*chunk_used(CHUNKS[last_in_slot(b, len(CHUNKS))]))
            load_expert(b, b)
        sp.wait_ge(outp_done, OUTP.no("nsa", NH // 2 - 1) + 1)
        sp.dma_start(first_down[:, :], io["c_route"][:, 0:8]).then_inc(e_dn_in[1], 16)
        for b in range(2):
            load_down(b, b)
        for t in range(TT):
            sp.wait_ge(base_ready, t + 1)
            sp.dma_start(sum_dram[t * P:(t + 1) * P, :], xres[:, t, :]).then_inc(base_saved, 16)
        sp.wait_ge(list_ready, 1)
        pairs = sp.value_load(itabi[0:1, ITEMS:ITEMS + 1], min_val=NE // 2, max_val=(NE + MAX_EXTRA + 1) // 2)
        with sp.Fori(1, pairs) as j:
            e = [sp.value_load(itabi[0:1, DS(j * 2 + b, 1)], min_val=0, max_val=NE - 1) for b in range(2)]
            for b in range(2):
                sp.wait_ge(h_done, j * 2 + (b - 1))
                sp.sem_inc(sp_turn, 1)
                load_expert(b, e[b])
            for b in range(2):
                sp.wait_ge(y_done, j * 2 + b)
                sp.sem_inc(sp_turn, 1)
                load_down(b, e[b])
        for b in range(2):
            sp.wait_ge(scattered[b], pairs * 16 + 16 * (b + 1))
            sp.sem_inc(sp_turn, 1)
        for t in range(TT):
            sp.dma_start(xres[:, t, :], sum_dram[t * P:(t + 1) * P, :]).then_inc(sum_in[t], 16)
        for t in range(TT):
            sp.wait_ge(*((gained, t + 1) if t < POOL_TILES else (fin_ready, t - POOL_TILES + 1)))
            sp.dma_start(out[t * P:(t + 1) * P, :], xres[:, t, :]).then_inc(out_saved, 16)
        sp.wait_ge(out_saved, 16 * TT)

    @block.gpsimd
    def _(pool):
        with nc.allow_non_contiguous_dma(reason="a few small rows"):
            pool.dma_start(c1[:, :], io["c_first"]).then_inc(const_in, 16)
            pool.dma_start(posi[:, :], io["positions"].rearrange("(t p) -> p t", p=P)).then_inc(const_in, 16)
            pool.wait_ge(proj_done, 2)
            pool.dma_start(decay[:, :, :], io["c_decay"].rearrange("p (h t) -> p h t", h=RH)).then_inc(decay_in, 16)
            for j, w in enumerate(("cmp_pe_k", "cmp_pe_v")):
                pool.dma_start(pe2[:, j, :], io[w].rearrange("(l h) d -> (h d) l", h=2)).then_inc(pe_in, 16)
            pool.dma_start(ccmp[:, :, :, :], io["c_cmp"].rearrange("p (a t c) -> p a t c", a=2, t=TT)).then_inc(pe_in, 16)
            pool.wait_ge(outp_done, OUTP.no("ret", RH - 1) + 1)
            pool.dma_start(mem_in[:, :, :], io["mem"].rearrange("(m p) n -> p m n", p=P)).then_inc(mem_loaded, 16)
            for j in range(2):
                pool.dma_start(w2k[:, :, j, :], io["cmp_w2_k"].rearrange("(k p) d -> p k d", p=P)).then_inc(cmp_in, 16)
            pool.dma_start(w2v[:, :, :], io["cmp_w2_v"].rearrange("(k p) d -> p k d", p=P)).then_inc(cmp_in, 16)

            def load_norm(dst, n):
                for j, w in enumerate(("g", "b")):
                    src = io[f"ln{n}_{w}"].rearrange("(o n) -> o n", o=1).to_broadcast([P, D])
                    pool.dma_start(dst[:, j, :], src).then_inc(ln_in[n - 1], 16)

            pool.wait_ge(score_done, SCORE.no("hid", 1) + 1)
            load_norm(lng, 1)
            pool.wait_ge(ln_ready, TT)
            load_norm(lng, 2)
            pool.dma_start(wrt[:, :, :], io["w_router"].rearrange("(k p) n -> p k n", p=P)).then_inc(route_in, 16)
            pool.dma_start(mcon[:, :], io["c_route"][:, R_IOTA:R_IOTA + BLK]).then_inc(route_in, 16)
            load_norm(lng3, 3)
            pool.wait_ge(outp_done, OUTP.n)
            pool.dma_start(rcon[:, :], io["c_route"]).then_inc(route_in, 16)
            pool.dma_start(rbias[:, :], io["router_bias"].rearrange("(o n) -> o n", o=1).to_broadcast([P, NE]))\
                .then_inc(route_in, 16)
        for t in range(TT):
            pool.wait_ge(ln_ready, TT + t + 1)
            pool.dma_start(x2_dram[t * P:(t + 1) * P, :], xres[:, t, :]).then_inc(x2_saved, 16)
        pool.wait_ge(x2_saved, 16 * TT)

        def gather(b):
            pool.indirect_dma_start(out=xg[b][:, :], out_offset=None, in_=x2_dram[:, :],
                                    in_offset=bass.IndirectOffsetOnAxis(ap=gidx[b][:, 0:1], axis=0),
                                    bounds_check=T - 1, oob_is_err=False).then_inc(gathered[b], 16)

        def scatter(b):
            pool.indirect_dma_start(out=sum_dram[:, :],
                                    out_offset=bass.IndirectOffsetOnAxis(ap=scur[b][:, 0:1], axis=0),
                                    in_=ysb[b][:, :], in_offset=None,
                                    bounds_check=T - 1, oob_is_err=False, compute_op=ALU.add).then_inc(scattered[b], 16)

        pool.wait_ge(moe_set, 7)
        for b in range(2):
            pool.wait_ge(idx_ready, b + 1)
            gather(b)
        pool.wait_ge(base_saved, 16 * TT)
        for b in range(2):
            scatter(b)
            pool.wait_ge(scattered[b], 16)
        pool.wait_ge(list_ready, 1)
        pairs = pool.value_load(itabi[0:1, ITEMS:ITEMS + 1], min_val=NE // 2, max_val=(NE + MAX_EXTRA + 1) // 2)
        with pool.Fori(0, pairs) as j:
            for b in range(2):
                pool.wait_ge(xgT_done, j * 2 + (b + 1))
                pool.wait_ge(idx_ready, j * 2 + (b + 3))
                pool.sem_inc(pool_turn, 1)
                gather(b)
                pool.wait_ge(y_act, j * 2 + (b + 2))
                pool.wait_ge(y_dve, j * 2 + (b + 2))
                pool.wait_ge(scattered[b], j * 16 + 16 * (b + 1))
                pool.sem_inc(pool_turn, 1)
                scatter(1 - b)
        pool.wait_ge(y_act, pairs * 2 + 2)
        pool.wait_ge(y_dve, pairs * 2 + 2)
        pool.wait_ge(scattered[0], pairs * 16 + 16)
        pool.sem_inc(pool_turn, 1)
        scatter(1)
        for b in range(2):
            pool.wait_ge(gathered[b], pairs * 16 + 16)
        pool.wait_ge(ln_in[2], 32)
        for t in range(POOL_TILES):
            x = xres[:, t, :]
            pool.wait_ge(normed, t + 1)
            nc.gpsimd.tensor_tensor(x, x, lng3[:, 0, :], ALU.mult).then_inc(offset_turn, 1)
            pool.wait_ge(offset_turn, t + 1)
            nc.gpsimd.tensor_tensor(x, x, lng3[:, 1, :], ALU.add).then_inc(gained, 1)

    @block.tensor
    def _(pe):
        mm, count = nc.tensor.matmul, {"p": 0, "t": 0, "s": 0, "o": 0}

        def take(key, units, free, name):
            n = units.no(*name)
            assert n == count[key], (name, n, count[key])
            count[key] += 1
            if n >= 2:
                pe.wait_ge(free[n % 2], n // 2)
            return n % 2

        def transposes(name, parts):
            b = take("t", TRAN, tran_free, name)
            for src, dst in parts:
                rows = src.shape[0]
                last = nc.tensor.transpose(dst(tp[b]), src, ident[0:rows, 0:rows])
            last.then_inc(tran_done, 1)

        def four(src, blocks):
            return [(src[:, k * P:(k + 1) * P], lambda bank, j=j: bank[:, j * P:(j + 1) * P])
                    for j, k in enumerate(blocks)]

        def copied(units, free, *name):
            m = units.no(*name)
            pe.wait_ge(free[m % 2], m // 2 + 1)

        def x_T(t):
            pe.wait_ge(x_in[t], 16)
            for j in range(2):
                transposes(("x", t, j), four(xres[:, t, :], range(4 * j, 4 * j + 4)))

        def proj(c, t):
            w = chunk_parts(("in", c))[0]
            if t == 0:
                pe.wait_ge(*((first_in, 16) if c == 0 else chunk_loaded(("in", c))))
            if c == 0:
                for j in range(2):
                    copied(TRAN, tran_free, "x", t, j)
            b = take("p", PROJ, proj_free, ("in", c, t))
            for k in range(KD):
                if (c, t, k) == (0, 0, KD // 2):
                    pe.wait_ge(*chunk_loaded(("in", 0)))
                last = mm(pp[b][:, 0:W_COLS[c]], xT[:, k, t * P:(t + 1) * P], w[:, k, :],
                          start=(k == 0), stop=(k == KD - 1))
            last.then_inc(proj_done, 1)

        def staged_T(c, t):
            n = stage_no(c, t)
            pe.wait_ge(staged, n + 1)
            st, names = stage[n % 2][:, :], staged_units(c, t)
            transposes(names[0], four(st, range(2 if c == 6 else 4)))
            if c in (4, 5):
                transposes(names[1], four(st, range(4, 8 if c == 4 else 6)))

        pe.wait_ge(const_in, 32)
        x_T(0)
        proj(0, 0)
        x_T(1)
        proj(0, 1)
        x_T(2)
        staged_T(0, 0)
        proj(0, 2)
        x_T(3)
        staged_T(0, 1)
        proj(0, 3)
        staged_T(0, 2)
        for t in range(TT):
            proj(1, t)
            staged_T(*STAGED[TT + t - 1])
        proj(2, 0)
        staged_T(1, TT - 1)
        for c, t in [(2, 1), (2, 2), (2, 3)] + [(3, t) for t in range(TT)]:
            proj(c, t)

        def ret_scores(h):
            for k in range(TT):
                b = take("s", SCORE, score_free, ("ret", h, k))
                n = T - k * P
                mm(sp_[b][:, 0:n], retT[1][:, h, k * P:(k + 1) * P], retT[0][:, h, k * P:T],
                   start=True, stop=True).then_inc(score_done, 1)

        def ret_out(h):
            pe.wait_ge(rets_ready, TT * (h + 1))
            b = take("o", OUTP, outp_free, ("ret", h))
            for q in range(TT):
                for k in range(q + 1):
                    last = mm(op[b][:, q * P:(q + 1) * P], retS[:, k, (q - k) * P:(q - k + 1) * P],
                              rv[:, k, h * RD:(h + 1) * RD], start=(k == 0), stop=(k == q))
            last.then_inc(outp_done, 1)

        for t in range(2, TT):
            copied(TRAN, tran_free, "ret", 1, t)
        for h in range(RH):
            ret_scores(h)
            proj(4, h)
            if h == 0:
                for t in range(2, TT):
                    copied(PROJ, proj_free, "in", 2, t)
            ret_out(h)
            if h >= 1:
                staged_T(4, h - 1)
        proj(5, 0)
        staged_T(4, TT - 1)
        pe.wait_ge(oret_ready, RH)
        for t in range(TT):
            transposes(("oret", t), four(oret[:, t, :], range(RH)))
        for n in range(stage_no(5, 1), len(STAGED)):
            proj(*STAGED[n])
            staged_T(*STAGED[n - 1])

        def cmp_hidden(j):
            w = chunk_parts(("w1", j))[0]
            pe.wait_ge(*chunk_loaded(("w1", j)))
            pe.wait_ge(ab_ready, j + 1)
            b = take("s", SCORE, score_free, ("hid", j))
            for l in range(16):
                last = mm(sp_[b][0:NG * NCMP, 0:CMP_HID], ab[:, j, l, :, :].rearrange("p g c -> p (g c)"), w[:, l, :],
                          start=(l == 0), stop=(l == 15))
            last.then_inc(score_done, 1)

        cmp_hidden(0)
        staged_T(6, TT - 1)
        cmp_hidden(1)
        pe.wait_ge(mem_loaded, 16)
        for m in range(2):
            for j in range(2):
                transposes(("mem", m, j), four(mem_in[:, m, :], range(4 * j, 4 * j + 4)))
        for j in range(2):
            pe.wait_ge(hid_ready, j + 1)
            transposes(("hid", j), [(hid[:, j, k * P:(k + 1) * P], lambda bank, k=k: bank[:, k * P:k * P + NG * NCMP])
                                    for k in range(2)])

        def mem_keys(d):
            w = chunk_parts(("xkv", d // 4))[0]
            if d % 4 == 0:
                pe.wait_ge(*chunk_loaded(("xkv", d // 4)))
            b = take("p", PROJ, proj_free, ("xk", d))
            for k in range(KD):
                last = mm(pp[b][:, 0:MEM], w[:, k, d % 4 * P:(d % 4 + 1) * P], memT[:, k, :],
                          start=(k == 0), stop=(k == KD - 1))
            last.then_inc(proj_done, 1)

        def mem_values(c, m):
            w = chunk_parts(("xkv", 2 + c))[0]
            if m == 0:
                pe.wait_ge(*chunk_loaded(("xkv", 2 + c)))
            b = take("p", PROJ, proj_free, ("xv", m, c))
            for k in range(KD):
                last = mm(pp[b][:, :], memT[:, k, m * P:(m + 1) * P], w[:, k, :], start=(k == 0), stop=(k == KD - 1))
            last.then_inc(proj_done, 1)

        for j in range(2):
            copied(TRAN, tran_free, "mem", 1, j)
        mem_keys(0)
        mem_keys(1)
        pe.wait_ge(cmp_in, 48)
        for j in range(2):
            copied(TRAN, tran_free, "hid", j)
        b = take("s", SCORE, score_free, ("kvc", 0))
        for k in range(2):
            mm(sp_[b][:, 0:NG * NCMP], w2k[:, k, :, :].rearrange("p a d -> p (a d)"), hidkT[:, k, :],
               start=(k == 0), stop=(k == 1))
        for g in range(NG):
            for k in range(2):
                last = mm(sp_[b][:, 128 + g * ND:128 + (g + 1) * ND],
                          hidvT[:, k, g, :, :].rearrange("p a c -> p (a c)"), w2v[:, k, :],
                          start=(k == 0), stop=(k == 1))
        last.then_inc(score_done, 1)
        mem_keys(2)

        def cmp_T(t):
            pe.wait_ge(pc_ready, t + 1)
            transposes(("pc", t), four(pc[t % 2][:, :, :].rearrange("p h c -> p (h c)"), range(NG)))

        pe.wait_ge(kvcmp_ready, 1)
        for t in range(TT):
            for a in range(2):
                b = take("s", SCORE, score_free, ("sc", t, a))
                for i in range(NH // 2):
                    g = (2 * i + a) // HPG
                    last = mm(sp_[b][:, i * 32:i * 32 + NCMP], nqT[a * ND:(a + 1) * ND, i, t * P:(t + 1) * P],
                              kcmpT[a * ND:(a + 1) * ND, g * NCMP:(g + 1) * NCMP], start=True, stop=True)
                last.then_inc(score_done, 1)
            mem_keys(3 + t)
            if t >= 1:
                cmp_T(t - 1)
        mem_keys(KD - 1)
        cmp_T(TT - 1)

        banks, LAG = att_banks, 3

        def att_scores(n):
            _, h, br, q = ATT[n]
            if n >= 4:
                pe.wait_ge(exp_ready, n - 3)
            mm(banks[n % 4][:, 0:(q + 1) * P], nqrT[:, h // 2, q * P:(q + 1) * P],
               kT[br][:, h // HPG, h % 2, 0:(q + 1) * P], start=True, stop=False)
            mm(banks[n % 4][:, q * P:(q + 1) * P], ident, causal, start=False, stop=True).then_inc(att_scored, 1)

        def att_T(n):
            pe.wait_ge(prob_ready, n + 1)
            transposes(("pt", n), four(prob[n % 4][:, :], range(ATT[n][3] + 1)))

        def att_pv(group):
            pr, q = divmod(group, TT)
            if q == 0:
                take("o", OUTP, outp_free, ("nsa", pr))
            if group == 0:
                for t in range(2, TT):
                    copied(TRAN, tran_free, "pc", t)
            for i in (2, 3):
                copied(TRAN, tran_free, "pt", 4 * group + i)
            o = op[OUTP.no("nsa", pr) % 2]
            g, cols = 2 * pr // HPG, slice(q * P, (q + 1) * P)
            heads = [(h, o[ND * (h % 2):ND * (h % 2) + ND, cols]) for h in (2 * pr, 2 * pr + 1)]
            for h, dst in heads:
                mm(dst, vcmp[:, h % HPG, g, :], pcT[:, g, cols], start=True, stop=False)
            for br in range(2):
                for k in range(q + 1):
                    for h, dst in heads:
                        last = mm(dst, vsw[:, br, k, g * ND:(g + 1) * ND], PT[(4 * group + 2 * br + h % 2) % 8][:, k, :],
                                  start=False, stop=(br == 1 and k == q))
            last.then_inc(pv_done_at(group)[0], 1)

        for t in range(2):
            copied(SCORE, score_free, "sc", TT - 1, t)
            copied(PROJ, proj_free, "xk", KD - 1 - t)
        for n in range(len(ATT) + LAG + 1):
            if n < len(ATT):
                att_scores(n)
            if LAG <= n < len(ATT) + LAG:
                att_T(n - LAG)
            if n >= LAG + 1 and (n - LAG - 1) % 4 == 3:
                att_pv((n - LAG - 1) // 4)

        def norm_T(which, kind, t):
            pe.wait_ge(ln_ready, TT * which + t + 1)
            for j in range(2):
                transposes((kind, t, j), four(xres[:, t, :], range(4 * j, 4 * j + 4)))

        def norm_copied(kind, t):
            for j in range(2):
                m = TRAN.no(kind, t, j)
                pe.wait_ge(tran_free[m % 2], m // 2 + 1)

        w = [chunk_parts(("out", n))[0] for n in range(2)]
        for n in range(2):
            pe.wait_ge(*chunk_loaded(("out", n)))
        for b in range(2):
            pe.wait_ge(outp_free[b], (RH + NH // 2) // 2)
        def mixed_out(t):
            for n in range(2):
                b = take("p", PROJ, proj_free, ("out", t, n))
                for k in range(KD):
                    last = mm(pp[b][:, :], mixT[:, k, t * P:(t + 1) * P], w[n][:, k, :], start=(k == 0), stop=(k == KD - 1))
                last.then_inc(proj_done, 1)

        mixed_out(0)
        for t in range(1, TT):
            mixed_out(t)
            if t < TT - 1:
                norm_T(0, "x1", t - 1)
        norm_T(0, "x1", TT - 2)
        for m in range(2):
            mem_values(0, m)
        norm_T(0, "x1", TT - 1)
        for m in range(2):
            mem_values(1, m)
        norm_copied("x1", TT - 1)
        for c in range(2):
            w = chunk_parts(("xq", c))[0]
            pe.wait_ge(*chunk_loaded(("xq", c)))
            for d in range(4):
                b = take("p", PROJ, proj_free, ("xq", 4 * c + d))
                for k in range(KD):
                    last = mm(pp[b][:, :], w[:, k, d * P:(d + 1) * P], x1T[:, k, :], start=(k == 0), stop=(k == KD - 1))
                last.then_inc(proj_done, 1)
        for d in range(KD - 2, KD):
            m = PROJ.no("xq", d)
            pe.wait_ge(proj_free[m % 2], m // 2 + 1)

        XU, LAG_X = [(h, t) for h in range(XH) for t in range(TT)], 2

        def x_pv(h):
            for i in range(2):
                m = TRAN.no("px", h, TT - 1 - i)
                pe.wait_ge(tran_free[m % 2], m // 2 + 1)
            for d in range(2):
                b = take("o", OUTP, outp_free, ("x", h, d))
                for m in range(2):
                    last = mm(op[b][:, :], vx[:, m, (2 * h + d) * P:(2 * h + d + 1) * P], PX[h % 2][:, m, :],
                              start=(m == 0), stop=(m == 1))
                last.then_inc(outp_done, 1)

        for n in range(len(XU) + LAG_X + 1):
            if n < len(XU):
                h, t = XU[n]
                b = take("s", SCORE, score_free, ("x", h, t))
                for d in range(2):
                    last = mm(sp_[b][:, 0:MEM], xqT[:, 2 * h + d, t * P:(t + 1) * P], kxT[:, 2 * h + d, :],
                              start=(d == 0), stop=(d == 1))
                last.then_inc(score_done, 1)
            if LAG_X <= n < len(XU) + LAG_X:
                h, t = XU[n - LAG_X]
                pe.wait_ge(xprob_ready, n - LAG_X + 1)
                transposes(("px", h, t), four(probx[(n - LAG_X) % 2][:, :], range(2)))
            if n >= LAG_X + 1 and (n - LAG_X - 1) % TT == TT - 1:
                x_pv((n - LAG_X - 1) // TT)

        w = [chunk_parts(("xo", n))[0] for n in range(2)]
        for n in range(2):
            pe.wait_ge(*chunk_loaded(("xo", n)))
        for b in range(2):
            pe.wait_ge(outp_free[b], OUTP.n // 2)
        def x_output(t):
            for n in range(2):
                b = take("p", PROJ, proj_free, ("xo", t, n))
                for k in range(KD):
                    last = mm(pp[b][:, :], xoT[:, k, t * P:(t + 1) * P], w[n][:, k, :], start=(k == 0), stop=(k == KD - 1))
                last.then_inc(proj_done, 1)

        def logits(t):
            norm_copied("x2", t)
            if t == 0:
                pe.wait_ge(route_in, 64)
            b = take("s", SCORE, score_free, ("logit", t))
            for k in range(KD):
                last = mm(sp_[b][:, 0:NE], x2T[:, k, t * P:(t + 1) * P], wrt[:, k, :], start=(k == 0), stop=(k == KD - 1))
            last.then_inc(score_done, 1)

        wg = chunk_parts(("sgu", 0))[0]
        wd = chunk_parts(("sdn", 0))[0]

        def shared_up(t):
            if t == 0:
                pe.wait_ge(*chunk_loaded(("sgu", 0)))
            b = take("p", PROJ, proj_free, ("sgu", t))
            for k in range(KD):
                last = mm(pp[b][:, :], x2T[:, k, t * P:(t + 1) * P], wg[:, :, k, :], start=(k == 0), stop=(k == KD - 1))
            last.then_inc(proj_done, 1)

        def shared_T(t):
            pe.wait_ge(sact_ready, t + 1)
            transposes(("sh", t), four(sact[:, t, :], range(2)))

        def shared_down(t):
            m = TRAN.no("sh", t)
            pe.wait_ge(tran_free[m % 2], m // 2 + 1)
            for n in range(2):
                b = take("p", PROJ, proj_free, ("sdn", t, n))
                for k in range(2):
                    last = mm(pp[b][:, :], sactT[:, k, t * P:(t + 1) * P], wd[:, k, n * 512:(n + 1) * 512],
                              start=(k == 0), stop=(k == 1))
                last.then_inc(proj_done, 1)

        for t in range(TT):
            x_output(t)
            if 1 <= t < TT - 1:
                norm_T(1, "x2", t - 1)
                logits(t - 1)
        norm_T(1, "x2", TT - 2)
        shared_up(0)
        logits(TT - 2)
        norm_T(1, "x2", TT - 1)
        shared_up(1)
        logits(TT - 1)
        shared_up(2)
        shared_T(0)
        shared_up(3)
        shared_T(1)

        tri, one = rcon[:, R_TRI:R_TRI + P], rcon[:, R_ONE:R_ONE + P]
        pe.wait_ge(mask_ready, TT)
        b = take("s", SCORE, score_free, ("pos", 0))
        for t in range(TT):
            for u in range(t + 1):
                mm(sp_[b][:, t * NE:(t + 1) * NE], tri if u == t else one, maskt[:, u, :], start=(u == 0), stop=(u == t))
        for u in range(TT):
            last = mm(sp_[b][0:NE, 384:385], maskt[:, u, :], one[:, 0:1], start=(u == 0), stop=(u == TT - 1))
        last.then_inc(score_done, 1)
        shared_T(2)
        shared_T(3)
        pe.wait_ge(*chunk_loaded(("sdn", 0)))
        shared_down(0)
        pe.wait_ge(extra_ready, 1)
        b = take("s", SCORE, score_free, ("extra", 0))
        ecol = rsmall[0:NE, 512:513]
        mm(sp_[b][0:NE, 0:1], rcon[0:NE, R_TRI64:R_TRI64 + NE], ecol, start=True, stop=True)
        mm(sp_[b][:, 1:2], rcon[0:NE, R_ONE:R_ONE + P], ecol, start=True, stop=True).then_inc(score_done, 1)
        shared_down(1)
        pe.wait_ge(extra_ready, 2)
        b = take("s", SCORE, score_free, ("cum", 0))
        ended = rsmall[0:NE, 640:640 + EXTRA]
        mm(sp_[b][:, 0:EXTRA], rcon[0:NE, R_ONE:R_ONE + P], ended, start=True, stop=True)
        mm(sp_[b][:, 64:64 + EXTRA], rsmall[0:NE, 768:768 + P], ended, start=True, stop=True).then_inc(score_done, 1)
        shared_down(2)

        gu = [ring[b][:, :].rearrange("p (g k n) -> p g k n", g=2, k=KD) for b in range(2)]
        hps, yps, eTps, idx_ps = pp[0], op, sp_[0], sp_[1]

        def number_rows():
            for t in range(TT):
                last = mm(idx_ps[:, 0:5], onehot[:, t, :], info[:, t, 0:5], start=(t == 0), stop=(t == TT - 1))
            return last

        def rows_T(b):
            for k in range(KD):
                last = nc.tensor.transpose(tp[k // 4][:, (k % 4) * P:(k % 4 + 1) * P], xg[b][:, k:D:KD], ident)
            return last

        def down(b):
            for n in range(2):
                for k in range(2):
                    last = mm(yps[n][:, :], eactT[:, k, :], wdown[b][:, k, n * 512:(n + 1) * 512],
                              start=(k == 0), stop=(k == 1))
            last.then_inc(y_done, 1)

        for b in range(2):
            pe.wait_ge(hot_ready, b + 1)
            if b == 1:
                pe.wait_ge(idx_ready, 1)
            else:
                for i in range(2):
                    pe.wait_ge(score_free[i], (SCORE.n + 1 - i) // 2)
            number_rows().then_inc(idx_done, 1)
            if b == 0:
                shared_down(3)
        pe.wait_ge(gathered[0], 16)
        rows_T(0).then_inc(xgT_done, 1)
        pe.wait_ge(e_dn_in[1], 32)
        for b in range(2):
            pe.wait_ge(proj_free[b], PROJ.n // 2)
        pe.wait_ge(list_ready, 1)
        pairs = pe.value_load(itabi[0:1, ITEMS:ITEMS + 1], min_val=NE // 2, max_val=(NE + MAX_EXTRA + 1) // 2)
        with pe.Fori(0, pairs) as j:
            for b in range(2):
                pe.wait_ge(e_gu_in[b], j * 32 + 32)
                pe.wait_ge(xgT_a, j * 2 + (b + 1))
                pe.wait_ge(xgT_d, j * 2 + (b + 1))
                for k in range(KD):
                    last = mm(hps[:, :], xgT[:, k, :], gu[b][:, :, k, :], start=(k == 0), stop=(k == KD - 1))
                last.then_inc(h_done, 1)
                pe.wait_ge(hot_ready, j * 2 + (b + 3))
                number_rows().then_inc(idx_done, 1)
                pe.wait_ge(gathered[1 - b], j * 16 + 16 * (b + 1))
                rows_T(1 - b).then_inc(xgT_done, 1)
                pe.wait_ge(eT_ready, j * 2 + (b + 1))
                pe.wait_ge(e_dn_in[1 - b], j * 16 + 16)
                pe.wait_ge(y_act, j * 2 + (b + 1))
                pe.wait_ge(y_dve, j * 2 + (b + 1))
                down(1 - b)
                pe.wait_ge(eact_ready, j * 2 + (b + 1))
                for k in range(2):
                    last = nc.tensor.transpose(eTps[:, k * P:(k + 1) * P], eact[:, k:FF:2], ident)
                last.then_inc(eT_done, 1)
        pe.wait_ge(e_dn_in[1], pairs * 16 + 16)
        pe.wait_ge(eT_ready, pairs * 2 + 1)
        pe.wait_ge(y_act, pairs * 2 + 1)
        pe.wait_ge(y_dve, pairs * 2 + 1)
        down(1)

    @block.scalar
    def _(act):
        steps = [0]

        def link(ins):
            steps[0] += 1
            ins.then_inc(act_step, 1)
            act.wait_ge(act_step, steps[0])

        def take(units, done, free, *name):
            wait_done(act, units, done, *name)
            return units.no(*name) % 2

        def copy_T(name, dst, src=None, scale=1.0):
            b = take(TRAN, tran_done, tran_free, *name)
            src = src(tp[b]) if src else tp[b][:, :].rearrange("p (k t) -> p k t", k=4)
            nc.scalar.activation(dst, src, ACT.Copy, scale=scale).then_inc(tran_free[b], 1)

        def part(n):
            return lambda bank: bank[:, 0:n * P].rearrange("p (k t) -> p k t", k=n)

        def x_T(t):
            for j in range(2):
                copy_T(("x", t, j), xT[:, 4 * j:4 * j + 4, t * P:(t + 1) * P])

        def ret_T(c, t):
            copy_T(("ret", c, t), retT[c][:, :, t * P:(t + 1) * P])

        x_T(0)
        act.wait_ge(angles_ready, 1)
        nc.scalar.activation(tab[:, :, :, :], turns[:, :, :, :], ACT.Sin).then_inc(tables_ready, 1)
        x_T(1)
        x_T(2)
        ret_T(0, 0)
        x_T(3)
        for c, t in STAGED[1:2 * TT - 1]:
            ret_T(c, t)
        for t in range(TT):
            b = take(PROJ, proj_done, proj_free, "in", 2, t)
            nc.scalar.activation(rv[:, t, :], pp[b][:, :], ACT.Copy).then_inc(proj_free[b], 1)
            if t == 0:
                ret_T(1, TT - 1)
        for t in range(TT):
            b = take(PROJ, proj_done, proj_free, "in", 3, t)
            nc.scalar.activation(swish[:, t, :], pp[b][:, :], ACT.Silu).then_inc(proj_free[b], 1)

        def nq_copies(t):
            n = stage_no(4, t)
            stage_free(act, n)
            b = take(PROJ, proj_done, proj_free, "in", 4, t)
            nc.scalar.activation(stage[n % 2][:, 0:512], pp[b][:, :], ACT.Copy)
            nc.scalar.activation(stage[n % 2][:, 512:1024], pp[b][:, :], ACT.Copy).then_inc(raw_staged, 1)

        def twice(v):
            return v.rearrange("p (g o d) -> p g o d", o=1, d=ND).to_broadcast([P, v.shape[1] // ND, 2, ND])

        def kv5_copies(t):
            n = stage_no(5, t)
            stage_free(act, n)
            b = take(PROJ, proj_done, proj_free, "in", 5, t)
            dst = stage[n % 2][:, 0:768].rearrange("p (g a d) -> p g a d", a=2, d=ND)
            for a in range(2):
                nc.scalar.activation(dst[:, :, a, :], pp[b][:, 0:384].rearrange("p (g d) -> p g d", d=ND), ACT.Copy)
            nc.scalar.activation(vsw[:, 0, t, :], pp[b][:, 384:512], ACT.Copy).then_inc(raw_staged, 1)

        def kv6_copies(t):
            n = stage_no(6, t)
            stage_free(act, n)
            b = take(PROJ, proj_done, proj_free, "in", 6, t)
            dst = stage[n % 2][:, 0:256].rearrange("p (g a d) -> p g a d", a=2, d=ND)
            for a in range(2):
                nc.scalar.activation(dst[:, :, a, :], pp[b][:, 0:128].rearrange("p (g d) -> p g d", d=ND), ACT.Copy)
            nc.scalar.activation(vsw[:, 1, t, :], pp[b][:, 128:256], ACT.Copy)
            nc.scalar.activation(gate[:, t, :], pp[b][:, 256:280], ACT.Sigmoid).then_inc(raw_staged, 1)

        def nq_T(t):
            copy_T(("nq", t, 0), nqT[:, :, t * P:(t + 1) * P], scale=ND ** -0.5)
            copy_T(("nq", t, 1), nqrT[:, :, t * P:(t + 1) * P], scale=ND ** -0.5)

        def key_T(name, br, t):
            if (br, t) == (0, 0):
                act.wait_ge(pads_ready, 4)
            b = take(TRAN, tran_done, tran_free, *name)
            for half in range(2):
                rows = slice(ND * half, ND * half + ND)
                last = nc.scalar.activation(kT[br][rows, :, half, t * P:(t + 1) * P], part(2)(tp[b])[rows], ACT.Copy)
            last.then_inc(tran_free[b], 1)

        def kv5_T(t):
            copy_T(("kv5", t, 0), kvcT[:, :, t * P:(t + 1) * P])
            key_T(("kv5", t, 1), 0, t)

        def kv6_T(t):
            key_T(("kv6", t), 1, t)

        def head_std(h):
            act.wait_ge(rstd_asked, h + 1)
            nc.scalar.activation(std[:, :], mv[:, :, 1], ACT.Sqrt, bias=eps).then_inc(rstd_ready, 1)

        for t in range(TT):
            if t >= 1:
                head_std(t - 1)
            nq_copies(t)
            if t >= 1:
                nq_T(t - 1)
        head_std(RH - 1)
        kv5_copies(0)
        nq_T(TT - 1)
        for t in range(TT):
            copy_T(("oret", t), mixT[:, 0:4, t * P:(t + 1) * P])
        for n in range(stage_no(5, 1), len(STAGED)):
            (kv5_copies if STAGED[n][0] == 5 else kv6_copies)(STAGED[n][1])
            (kv5_T if STAGED[n - 1][0] == 5 else kv6_T)(STAGED[n - 1][1])

        for j in range(2):
            b = take(SCORE, score_done, score_free, "hid", j)
            nc.scalar.activation(hid[:, j, :], sp_[b][0:NG * NCMP, 0:CMP_HID], ACT.Silu).then_inc(hid_ready, 1)
            act.wait_ge(hid_ready, j + 1)
            act.sem_inc(score_free[b], 1)
            if j == 0:
                kv6_T(TT - 1)
        for m in range(2):
            for j in range(2):
                copy_T(("mem", m, j), memT[:, 4 * j:4 * j + 4, m * P:(m + 1) * P])
        copy_T(("hid", 0), hidkT[:, :, :], lambda bank: bank[:, 0:256].rearrange("p (k c) -> p k c", k=2)[:, :, 0:NG * NCMP])
        act.wait_ge(zeros_ready, 3)
        b = take(TRAN, tran_done, tran_free, "hid", 1)
        for k in range(2):
            for g in range(NG):
                last = nc.scalar.activation(
                    hidvT[:, k, g, :, 0:NCMP],
                    tp[b][:, k * P + g * NCMP:k * P + (g + 1) * NCMP].rearrange("p (o c) -> p o c", o=1)
                    .to_broadcast([P, HPG, NCMP]), ACT.Copy)
        last.then_inc(tran_free[b], 1)
        def mem_keys(d):
            b = take(PROJ, proj_done, proj_free, "xk", d)
            nc.scalar.activation(kxT[:, d, :], pp[b][:, 0:MEM], ACT.Copy, scale=(D // XH) ** -0.5).then_inc(proj_free[b], 1)

        def mem_values(n, m):
            b = take(PROJ, proj_done, proj_free, "xv", m, n)
            nc.scalar.activation(vx[:, m, n * 512:(n + 1) * 512], pp[b][:, :], ACT.Copy).then_inc(proj_free[b], 1)

        def cmp_T(t):
            copy_T(("pc", t), pcT[:, :, t * P:(t + 1) * P], part(2))

        mem_keys(0)
        mem_keys(1)
        b = take(SCORE, score_done, score_free, "kvc", 0)
        nc.scalar.activation(kcmpT[:, :], sp_[b][:, 0:NG * NCMP], ACT.Copy)
        act.wait_ge(zeros_ready, 4)
        for i in range(HPG):
            rows = slice(32 * i, 32 * i + 32)
            last = nc.scalar.activation(vcmp[rows, i, :, :], sp_[b][rows, 128:256].rearrange("p (g d) -> p g d", g=NG), ACT.Copy)
        last.then_inc(kvcmp_ready, 1)
        act.wait_ge(kvcmp_ready, 1)
        act.sem_inc(score_free[b], 1)
        mem_keys(2)
        for t in range(TT):
            act.wait_ge(pc_asked, t + 1)
            v = pc[t % 2][:, :, 0:NCMP]
            nc.scalar.activation(v, v, ACT.Exp).then_inc(pc_exp, 1)
            mem_keys(3 + t)
            if t >= 1:
                cmp_T(t - 1)
        mem_keys(KD - 1)
        cmp_T(TT - 1)

        def copy_pair(pr):
            b = take(OUTP, outp_done, outp_free, "nsa", pr)
            nc.scalar.activation(mixT[:, 4 + pr, :], op[b][:, :], ACT.Copy).then_inc(outp_free[b], 1)

        LAG = 3
        for n in range(len(ATT) + LAG):
            if n < len(ATT):
                q = ATT[n][3]
                act.wait_ge(max_ready, n + 1)
                if n >= 4:
                    wait_done(act, TRAN, tran_done, "pt", n - 4)
                nc.scalar.activation(prob[n % 4][:, 0:(q + 1) * P], att_banks[n % 4][:, 0:(q + 1) * P], ACT.Exp,
                                     bias=nmax[:, 0, n % 4:n % 4 + 1], accum_out=rsum[:, 0, n % 4:n % 4 + 1])\
                    .then_inc(exp_ready, 1)
            if n >= LAG:
                m = n - LAG
                q = ATT[m][3]
                if m % 4 == 0 and m >= 8:
                    act.wait_ge(*pv_done_at(m // 4 - 2))
                copy_T(("pt", m), PT[m % 8][:, 0:q + 1, :], part(q + 1))
                if m % (4 * TT) == 7 and m > 8:
                    copy_pair(m // (4 * TT) - 1)
        copy_pair(NH // 2 - 1)

        def std_of(which, t):
            act.wait_ge(var_ready, TT * which + t + 1)
            nc.scalar.activation(std[:, t:t + 1], mv[:, t, 1:2], ACT.Sqrt, bias=eps).then_inc(std_ready, 1)

        def norm_T(which, t):
            kind, dst = (("x1", x1T), ("x2", x2T))[which]
            for j in range(2):
                copy_T((kind, t, j), dst[:, 4 * j:4 * j + 4, t * P:(t + 1) * P])

        std_of(0, 0)
        for t in range(1, TT):
            std_of(0, t)
            norm_T(0, t - 1)
        for m in range(2):
            mem_values(0, m)
        norm_T(0, TT - 1)
        for m in range(2):
            mem_values(1, m)
        for d in range(KD):
            b = take(PROJ, proj_done, proj_free, "xq", d)
            nc.scalar.activation(xqT[:, d, :], pp[b][:, :], ACT.Copy).then_inc(proj_free[b], 1)

        def x_out(h):
            for d in range(2):
                b = take(OUTP, outp_done, outp_free, "x", h, d)
                nc.scalar.activation(xoT[:, 2 * h + d, :], op[b][:, :], ACT.Copy).then_inc(outp_free[b], 1)

        XU, LAG_X = [(h, t) for h in range(XH) for t in range(TT)], 2
        for n in range(len(XU) + LAG_X):
            if n < len(XU):
                b = SCORE.no("x", *XU[n]) % 2
                act.wait_ge(xmax_ready, n + 1)
                if n >= 2:
                    wait_done(act, TRAN, tran_done, "px", *XU[n - 2])
                nc.scalar.activation(probx[n % 2][:, :], sp_[b][:, 0:MEM], ACT.Exp, bias=nmax[:, n % 2, 0:1],
                                     accum_out=rsum[:, n % 2, 0:1]).then_inc(xexp_ready, 1)
            if n >= LAG_X:
                h, t = XU[n - LAG_X]
                if t == 0 and h >= 2:
                    wait_done(act, OUTP, outp_done, "x", h - 2, 1)
                copy_T(("px", h, t), PX[h % 2][:, :, t * P:(t + 1) * P], part(2))
                if t == 1 and h >= 1:
                    x_out(h - 1)
        x_out(XH - 1)

        def router_score(t):
            b = take(SCORE, score_done, score_free, "logit", t)
            nc.scalar.activation(score[:, t, :], sp_[b][:, 0:NE], ACT.Sigmoid).then_inc(score_sig, 1)
            act.wait_ge(score_sig, t + 1)
            act.sem_inc(score_free[b], 1)

        def shared_gate(t):
            b = take(PROJ, proj_done, proj_free, "sgu", t)
            if t >= 1:
                act.wait_ge(sact_ready, t)
            nc.scalar.activation(sgate[:, :], pp[b][:, 0:FF], ACT.Silu).then_inc(sgate_ready, 1)

        def shared_T(t):
            copy_T(("sh", t), sactT[:, :, t * P:(t + 1) * P], part(2))

        for t in range(TT):
            std_of(1, t)
            if 1 <= t < TT - 1:
                norm_T(1, t - 1)
                router_score(t - 1)
        norm_T(1, TT - 2)
        shared_gate(0)
        router_score(TT - 2)
        norm_T(1, TT - 1)
        shared_gate(1)
        router_score(TT - 1)
        shared_gate(2)
        shared_T(0)
        shared_gate(3)
        for t in range(1, TT):
            shared_T(t)
        def half_T():
            nc.scalar.activation(xgT[:, 0:4, :], tp[0][:, :].rearrange("p (k t) -> p k t", k=4), ACT.Copy)\
                .then_inc(xgT_a, 1)

        def y_half(b, j):
            act.wait_ge(y_done, j * 2 + (2 - b))
            act.wait_ge(scattered[b], j * 16 + 16)
            act.wait_ge(w_ready, j * 2 + (2 - b))
            nc.scalar.activation(ysb[b][:, 0:512], op[0][:, :], ACT.Copy, scale=wcur[b][:, 0:1]).then_inc(y_act, 1)

        act.wait_ge(moe_set, 7)
        act.sem_inc(eT_ready, 1)
        act.sem_inc(y_act, 1)
        act.wait_ge(xgT_done, 1)
        half_T()
        act.wait_ge(list_ready, 1)
        pairs = act.value_load(itabi[0:1, ITEMS:ITEMS + 1], min_val=NE // 2, max_val=(NE + MAX_EXTRA + 1) // 2)
        with act.Fori(0, pairs) as j:
            for b in range(2):
                act.wait_ge(h_done, j * 2 + (b + 1))
                nc.scalar.activation(egate[:, :], pp[0][:, 0:FF], ACT.Silu).then_inc(egate_ready, 1)
                act.wait_ge(xgT_done, j * 2 + (b + 2))
                half_T()
                y_half(1 - b, j)
                act.wait_ge(eT_done, j * 2 + (b + 1))
                nc.scalar.activation(eactT[:, :, :], sp_[0][:, 0:2 * P].rearrange("p (k t) -> p k t", k=2), ACT.Copy)\
                    .then_inc(eT_ready, 1)
        y_half(1, pairs)
        for t in range(TT):
            std_of(2, t)

    @block.vector
    def _(dve):
        V = nc.vector
        steps = [0]

        def mark(ins):
            steps[0] += 1
            return ins.then_inc(dve_step, 1)

        def link(ins=None):
            if ins is not None:
                mark(ins)
            dve.wait_ge(dve_step, steps[0])

        for keys in kT:
            V.memset(keys[ND:P, :, 0, :], 0.0).then_inc(pads_ready, 1)
            V.memset(keys[0:ND, :, 1, :], 0.0).then_inc(pads_ready, 1)
        M, TWO_PI = 1.5 * 2.0 ** 23, 2 * np.pi
        A1 = 6.28125
        A2 = float(np.float32(np.floor((TWO_PI - A1) * 2 ** 21) / 2 ** 21))
        A3 = float(TWO_PI - A1 - A2)
        dve.wait_ge(const_in, 32)
        link(V.tensor_copy(posf[:, :], posi[:, :]))
        link(V.tensor_tensor(ang[:, :, :], posf[:, :].rearrange("p (t o) -> p t o", o=1).to_broadcast([P, TT, NFREQ]),
                             c1[:, C_INV:C_INV + NFREQ].rearrange("p (o f) -> p o f", o=1).to_broadcast([P, TT, NFREQ]),
                             ALU.mult))
        n_turns = oret[:, 0:2, 0:TT * NFREQ]
        for s in range(2):
            link(V.tensor_scalar(n_turns[:, s, :], ang[:, :, :].rearrange("p t f -> p (t f)"), float(1 / TWO_PI), 0.25 * s, ALU.mult, ALU.add))
        link(V.tensor_scalar(n_turns, n_turns, M, None, ALU.add))
        link(V.tensor_scalar(n_turns, n_turns, M, None, ALU.subtract))
        for s in range(2):
            flat = turns[:, s, :, :].rearrange("p t f -> p (t f)")
            src = ang[:, :, :].rearrange("p t f -> p (t f)")
            for a in (A1, A2, A3):
                link(V.scalar_tensor_tensor(out=flat, in0=n_turns[:, s, :], scalar=-a, in1=src, op0=ALU.mult, op1=ALU.add))
                src = flat
        link(V.tensor_scalar(turns[:, 1, :, :], turns[:, 1, :, :], float(np.pi / 2), None, ALU.add))
        PI = 3.1415925
        V.tensor_scalar(turns[:, :, :, :], turns[:, :, :, :], -PI, PI, ALU.max, ALU.min).then_inc(angles_ready, 1)
        dve.wait_ge(tables_ready, 1)

        for c in range(2):
            for t in range(TT):
                n = stage_no(c, t)
                b = PROJ.no("in", c, t) % 2
                wait_done(dve, PROJ, proj_done, "in", c, t)
                stage_free(dve, n)
                src = pp[b][:, :].rearrange("p (h f) -> p h f", f=RROT)
                dst = stage[n % 2][:, 0:512].rearrange("p (h a f) -> p h a f", a=2, f=RROT)
                for s in range(2):
                    tb = tab[:, s, t, 0:RROT].rearrange("p (o f) -> p o f", o=1).to_broadcast([P, 2 * RH, RROT])
                    ins = V.tensor_tensor(rott[:, s, :].rearrange("p (h f) -> p h f", f=RROT), src, tb, ALU.mult)
                    mark(ins)
                link()
                rs = rott[:, 0, :].rearrange("p (h a f) -> p h a f", a=2, f=RROT)
                rc = rott[:, 1, :].rearrange("p (h a f) -> p h a f", a=2, f=RROT)
                mark(V.tensor_tensor(dst[:, :, 0, :], rc[:, :, 0, :], rs[:, :, 1, :], ALU.subtract))
                V.tensor_tensor(dst[:, :, 1, :], rc[:, :, 1, :], rs[:, :, 0, :], ALU.add).then_inc(staged, 1)
                dve.wait_ge(staged, n + 1)
                dve.sem_inc(proj_free[b], 1)

        def ret_decay(h):
            if h >= 1:
                wait_done(dve, OUTP, outp_done, "ret", h - 1)
            for k in range(TT):
                b = SCORE.no("ret", h, k) % 2
                wait_done(dve, SCORE, score_done, "ret", h, k)
                n = T - k * P
                V.tensor_tensor(retS[:, k, 0:n], sp_[b][:, 0:n], decay[:, h, 0:n], ALU.mult).then_inc(rets_ready, 1)
                dve.wait_ge(rets_ready, TT * h + k + 1)
                dve.sem_inc(score_free[b], 1)

        def ret_norm(h):
            b = OUTP.no("ret", h) % 2
            wait_done(dve, OUTP, outp_done, "ret", h)
            for q in range(TT):
                mark(V.bn_stats(stat[:, q, :], op[b][:, q * P:(q + 1) * P]))
            link()
            for q in range(TT):
                last = V.bn_aggr(mv[:, q, :], stat[:, q, :])
                if q < TT - 1:
                    mark(last)
            last.then_inc(rstd_asked, 1)
            dve.wait_ge(rstd_ready, h + 1)
            dve.wait_ge(rstd_asked, h + 1)
            link(V.reciprocal(rinv[:, 0, 0:TT], std[:, :]))
            for q in range(TT):
                mark(V.tensor_scalar(oret[:, q, h * RD:(h + 1) * RD], op[b][:, q * P:(q + 1) * P], mv[:, q, 0:1],
                                     rinv[:, 0, q:q + 1], ALU.subtract, ALU.mult))
            link()
            dve.sem_inc(outp_free[b], 1)
            if h == 0:
                for t in range(2, TT):
                    m = PROJ.no("in", 3, t)
                    dve.wait_ge(proj_free[m % 2], m // 2 + 1)
            V.tensor_tensor(oret[:, :, h * RD:(h + 1) * RD], oret[:, :, h * RD:(h + 1) * RD],
                            swish[:, :, h * RD:(h + 1) * RD], ALU.mult).then_inc(oret_ready, 1)

        def small_rotation(b, src_cols, heads, dst, t):
            src = pp[b][:, src_cols:src_cols + heads * ND].rearrange("p (h d) -> p h d", d=ND)[:, :, 0:2 * NROT]\
                .rearrange("p h (a f) -> p h a f", a=2)
            m = heads * 2 * NROT
            for s in range(2):
                for a in range(2):
                    tb = tab[:, s, t, RROT:NFREQ].rearrange("p (o f) -> p o f", o=1).to_broadcast([P, heads, NROT])
                    o = rottn[:, s, a * heads * NROT:(a + 1) * heads * NROT].rearrange("p (h f) -> p h f", h=heads)
                    mark(V.tensor_tensor(o, src[:, :, a, :], tb, ALU.mult))
            link()
            half = lambda s, a: rottn[:, s, a * heads * NROT:(a + 1) * heads * NROT].rearrange("p (h f) -> p h f", h=heads)
            for i, d in enumerate(dst):
                mark(V.tensor_tensor(d[:, :, 0:NROT], half(1, 0), half(0, 1), ALU.subtract))
                last = V.tensor_tensor(d[:, :, NROT:2 * NROT], half(1, 1), half(0, 0), ALU.add)
                if i < len(dst) - 1:
                    mark(last)
            return last

        def rotated(c, t):
            n = stage_no(c, t)
            b = PROJ.no("in", c, t) % 2
            dve.wait_ge(raw_staged, n - 2 * TT + 1)
            st = stage[n % 2]
            if c == 4:
                last = small_rotation(b, 0, NH, [st[:, 512:1024].rearrange("p (h d) -> p h d", d=ND)], t)
            elif c == 5:
                v = st[:, 512:768].rearrange("p (g a d) -> p g a d", a=2, d=ND)
                last = small_rotation(b, 256, NG, [v[:, :, a, :] for a in range(2)], t)
            else:
                v = st[:, 0:256].rearrange("p (g a d) -> p g a d", a=2, d=ND)
                last = small_rotation(b, 0, NG, [v[:, :, a, :] for a in range(2)], t)
            last.then_inc(staged, 1)
            dve.wait_ge(staged, n + 1)
            dve.sem_inc(proj_free[b], 1)

        def cmp_blocks(j):
            for half in range(2):
                lo = ND * half
                for g in range(NG):
                    src = kvcT[lo:lo + ND, 2 * j + g, :]
                    for part in range(2):
                        blk = src[:, 16 * part:16 * part + 16 * NCMP].rearrange("p (c l a) -> p a l c", l=8, a=2)[:, half]
                        pe_v = pe2[lo:lo + ND, j, 8 * part:8 * part + 8].rearrange("p (l o) -> p l o", o=1)\
                            .to_broadcast([ND, 8, NCMP])
                        ins = V.tensor_tensor(ab[lo:lo + ND, j, 8 * part:8 * part + 8, g, :], blk, pe_v, ALU.add)
                        if (half, g, part) == (1, NG - 1, 1):
                            ins.then_inc(ab_ready, 1)
                        else:
                            mark(ins)

        dve.wait_ge(decay_in, 16)
        for h in range(RH):
            ret_decay(h)
            if h >= 1:
                ret_norm(h - 1)
            rotated(4, h)
        ret_norm(RH - 1)
        V.memset(hidvT[:, :, :, :, :], 0.0).then_inc(zeros_ready, 1)
        for i in range(2):
            V.memset(pc[i][:, :, :], 0.0).then_inc(zeros_ready, 1)
        for t in range(TT):
            rotated(5, t)
        for t in range(TT):
            rotated(6, t)
            if t == 0:
                dve.wait_ge(pe_in, 48)
                for i in range(2):
                    m = TRAN.no("kv5", TT - 1, i)
                    dve.wait_ge(tran_free[m % 2], m // 2 + 1)
            if t < 2:
                cmp_blocks(t)

        wait_done(dve, TRAN, tran_done, "hid", 1)
        V.memset(vcmp[:, :, :, :], 0.0).then_inc(zeros_ready, 1)
        for t in range(TT):
            if t >= 2:
                wait_done(dve, TRAN, tran_done, "pc", t - 2)
            v = pc[t % 2][:, :, 0:NCMP]
            bc = lambda a, n: ccmp[:, a, t, :].rearrange("p (o c) -> p o c", o=1).to_broadcast([P, n, NCMP])
            wide = lambda x: x.rearrange("p (h o) -> p h o", o=1).to_broadcast([P, NH, NCMP])
            for a in range(2):
                b = SCORE.no("sc", t, a) % 2
                wait_done(dve, SCORE, score_done, "sc", t, a)
                s = sp_[b][:, 0:NH // 2 * 32].rearrange("p (h c) -> p h c", c=32)[:, :, 0:NCMP]
                link(V.tensor_tensor(pc[t % 2][:, a:NH:2, 0:NCMP], s, bc(1, NH // 2), ALU.add))
                dve.sem_inc(score_free[b], 1)
            link(V.tensor_reduce(cmpm[:, :], v, AX.X, ALU.max))
            V.tensor_tensor(v, v, wide(cmpm[:, :]), ALU.subtract).then_inc(pc_asked, 1)
            dve.wait_ge(pc_exp, t + 1)
            link(V.tensor_reduce(cmpm[:, :], v, AX.X, ALU.add))
            link(V.reciprocal(cmpm[:, :], cmpm[:, :]))
            link(V.tensor_tensor(cmpm[:, :], cmpm[:, :], gate[:, t, 0:3 * NH:3], ALU.mult))
            link(V.tensor_tensor(v, v, bc(0, NH), ALU.mult))
            V.tensor_tensor(v, v, wide(cmpm[:, :]), ALU.mult).then_inc(pc_ready, 1)

        def scale_prob(n):
            _, h, br, q = ATT[n]
            col = slice(n % 4, n % 4 + 1)
            dve.wait_ge(exp_ready, n + 1)
            link(V.reciprocal(rinv[:, 0, col], rsum[:, 0, col]))
            v = prob[n % 4][:, 0:(q + 1) * P]
            V.tensor_scalar(v, v, rinv[:, 0, col], gate[:, q, 3 * h + 1 + br:3 * h + 2 + br], ALU.mult, ALU.mult)\
                .then_inc(prob_ready, 1)

        for n in range(len(ATT)):
            q = ATT[n][3]
            s = att_banks[n % 4]
            dve.wait_ge(att_scored, n + 1)
            V.tensor_reduce(nmax[:, 0, n % 4:n % 4 + 1], s[:, 0:(q + 1) * P], AX.X, ALU.max, negate=True).then_inc(max_ready, 1)
            if n >= 1:
                scale_prob(n - 1)
        scale_prob(len(ATT) - 1)

        def add_norm(which, kind, t):
            for n in range(2):
                b = PROJ.no(kind, t, n) % 2
                wait_done(dve, PROJ, proj_done, kind, t, n)
                half = xres[:, t, n * 512:(n + 1) * 512]
                link(V.scalar_tensor_tensor(out=half, in0=half, scalar=ALPHA, in1=pp[b][:, :], op0=ALU.mult, op1=ALU.add))
                dve.sem_inc(proj_free[b], 1)
                mark(V.bn_stats(stat[:, n, :], half))
            link()
            norm_rows(which, t, lng)

        def norm_rows(which, t, gains):
            x = xres[:, t, :]
            V.bn_aggr(mv[:, t, :], stat[:, 0:2, :].rearrange("p a b -> p (a b)")).then_inc(var_ready, 1)
            dve.wait_ge(std_ready, TT * which + t + 1)
            dve.wait_ge(var_ready, TT * which + t + 1)
            link(V.reciprocal(rinv[:, 0, t:t + 1], std[:, t:t + 1]))
            ins = V.tensor_scalar(x, x, mv[:, t, 0:1], rinv[:, 0, t:t + 1], ALU.subtract, ALU.mult)
            if which == 2 and t < POOL_TILES:
                ins.then_inc(normed, 1)
                return
            link(ins)
            dve.wait_ge(ln_in[which], 32)
            link(V.tensor_tensor(x, x, gains[:, 0, :], ALU.mult))
            done = ln_ready if which < 2 else fin_ready
            V.tensor_tensor(x, x, gains[:, 1, :], ALU.add).then_inc(done, 1)
            if which < 2:
                dve.wait_ge(done, TT * which + t + 1)

        for t in range(TT):
            add_norm(0, "out", t)

        def scale_x(n):
            dve.wait_ge(xexp_ready, n + 1)
            dve.sem_inc(score_free[SCORE.no("x", *XU[n]) % 2], 1)
            link(V.reciprocal(rinv[:, n % 2, 0:1], rsum[:, n % 2, 0:1]))
            V.tensor_scalar(probx[n % 2][:, :], probx[n % 2][:, :], rinv[:, n % 2, 0:1], None, ALU.mult)\
                .then_inc(xprob_ready, 1)

        XU = [(h, t) for h in range(XH) for t in range(TT)]
        for n in range(len(XU)):
            b = SCORE.no("x", *XU[n]) % 2
            wait_done(dve, SCORE, score_done, "x", *XU[n])
            V.tensor_reduce(nmax[:, n % 2, 0:1], sp_[b][:, 0:MEM], AX.X, ALU.max, negate=True).then_inc(xmax_ready, 1)
            if n >= 1:
                scale_x(n - 1)
        scale_x(len(XU) - 1)
        for b in range(2):
            V.memset(xg[b][:, :], 0.0).then_inc(moe_set, 1)
            V.memset(ysb[b][:, :], 0.0).then_inc(moe_set, 1)
            mark(V.memset(smid[b][:, :], OOB))
            V.memset(scur[b][:, :], int(OOB)).then_inc(moe_set, 1)
        dve.wait_ge(outp_done, OUTP.n)
        link(V.memset(eactT[:, :, :], 0.0))
        dve.sem_inc(moe_set, 1)

        bc = lambda x, shape, pat, **kw: x.rearrange(pat, **kw).to_broadcast(shape)
        iota64 = rcon[:, R_IOTA:R_IOTA + NE]

        def route(t):
            col = lambda i: rsmall[:, i * 8:(i + 1) * 8]
            gs, gsort, gok, gpen, top, tidf = (col(i) for i in range(6))
            tidx = col(6).bitcast(U32)
            ws = rsmall[:, 56:57]
            dve.wait_ge(score_sig, t + 1)
            link(V.tensor_tensor(biased[:, t, :], score[:, t, :], rbias[:, :], ALU.add))
            for g in range(GROUPS):
                mark(V.max(gtop[:, t, g, :], biased[:, t, g * EPG:(g + 1) * EPG]))
            link()
            link(V.tensor_tensor(gs, gtop[:, t, :, 0], gtop[:, t, :, 1], ALU.add))
            link(V.max(gsort, gs))
            link(V.tensor_scalar(gok, gs, gsort[:, TOPG - 1:TOPG], None, ALU.is_ge))
            link(V.tensor_scalar(gpen, gok, -1.0, -NEG, ALU.add, ALU.mult))
            m3 = lambda x: x.rearrange("p (g e) -> p g e", g=GROUPS)
            wide = lambda x: x.rearrange("p (g o) -> p g o", o=1).to_broadcast([P, GROUPS, EPG])
            link(V.tensor_tensor(m3(tmpa[:, t, :]), m3(biased[:, t, :]), wide(gok), ALU.mult))
            link(V.tensor_tensor(m3(tmpa[:, t, :]), m3(tmpa[:, t, :]), wide(gpen), ALU.add))
            link(V.max(top, tmpa[:, t, :]))
            link(V.max_index(tidx, top, tmpa[:, t, :]))
            link(V.tensor_copy(tidf, tidx))
            sh = [P, TOPK, NE]
            link(V.tensor_tensor(hot8[:, :, :], bc(iota64, sh, "p (o e) -> p o e", o=1),
                                 bc(tidf, sh, "p (k o) -> p k o", o=1), ALU.is_equal))
            V.tensor_reduce(maskt[:, t, :], hot8[:, :, :].rearrange("p k e -> p e k"), AX.X, ALU.add).then_inc(mask_ready, 1)
            dve.wait_ge(mask_ready, t + 1)
            link(V.tensor_tensor(wexp[:, t, :], score[:, t, :], maskt[:, t, :], ALU.mult))
            link(V.tensor_reduce(ws, wexp[:, t, :], AX.X, ALU.add))
            link(V.reciprocal(ws, ws))
            link(V.tensor_scalar(wexp[:, t, :], wexp[:, t, :], ws, SCALE_W, ALU.mult, ALU.mult))
            for i in range(3):
                link(V.tensor_copy(wpart[:, t, :, i], wexp[:, t, :]))
                if i < 2:
                    link(V.tensor_tensor(wexp[:, t, :], wexp[:, t, :], wpart[:, t, :, i], ALU.subtract))

        def shared_act(t):
            b = PROJ.no("sgu", t) % 2
            dve.wait_ge(sgate_ready, t + 1)
            V.tensor_tensor(sact[:, t, :], sgate[:, :], pp[b][:, FF:2 * FF], ALU.mult).then_inc(sact_ready, 1)
            dve.wait_ge(sact_ready, t + 1)
            dve.sem_inc(proj_free[b], 1)

        def shared_add(t):
            dve.wait_ge(x2_saved, 16 * TT)
            for n in range(2):
                b = PROJ.no("sdn", t, n) % 2
                wait_done(dve, PROJ, proj_done, "sdn", t, n)
                half = xres[:, t, n * 512:(n + 1) * 512]
                V.scalar_tensor_tensor(out=half, in0=half, scalar=ALPHA, in1=pp[b][:, :], op0=ALU.mult, op1=ALU.add)\
                    .then_inc(half_added, 1)
                dve.wait_ge(half_added, 2 * t + n + 1)
                dve.sem_inc(proj_free[b], 1)
            dve.sem_inc(base_ready, 1)

        for t in range(TT):
            add_norm(1, "xo", t)
            if t == 0:
                dve.wait_ge(route_in, 64)
            if 1 <= t < TT - 1:
                route(t - 1)
        shared_act(0)
        route(TT - 2)
        shared_act(1)
        route(TT - 1)
        shared_act(2)
        shared_act(3)

        wait_done(dve, SCORE, score_done, "pos", 0)
        b = SCORE.no("pos", 0) % 2
        link(V.tensor_scalar(tmpa[:, :, :], maskt[:, :, :], -1.0, FAR, ALU.add, ALU.mult))
        link(V.tensor_tensor(posm[:, :, :], sp_[b][:, 0:TT * NE].rearrange("p (t e) -> p t e", t=TT), tmpa[:, :, :], ALU.add))
        ecol, etmp = rsmall[0:NE, 512:513], rsmall[0:NE, 513:516]
        for i in range(3):
            mark(V.tensor_scalar(etmp[:, i:i + 1], sp_[b][0:NE, 384:385], float(BLK * (i + 1)), None, ALU.is_gt))
        link()
        dve.sem_inc(score_free[b], 1)
        link(V.tensor_reduce(ecol, etmp, AX.X, ALU.add))
        V.tensor_copy(rsmall[0:NE, 768:768 + P], ecol.to_broadcast([NE, P])).then_inc(extra_ready, 1)
        shared_add(0)
        wait_done(dve, SCORE, score_done, "extra", 0)
        b = SCORE.no("extra", 0) % 2
        cum, n_extra = rsmall[0:NE, 516:517], rsmall[:, 517:518]
        mark(V.tensor_copy(cum, sp_[b][0:NE, 0:1]))
        link(V.tensor_copy(n_extra, sp_[b][:, 1:2]))
        dve.sem_inc(score_free[b], 1)
        V.tensor_scalar(rsmall[0:NE, 640:640 + EXTRA], rcon[0:NE, R_IOTA:R_IOTA + EXTRA], cum, None, ALU.is_ge)\
            .then_inc(extra_ready, 1)
        shared_add(1)
        wait_done(dve, SCORE, score_done, "cum", 0)
        b = SCORE.no("cum", 0) % 2
        mark(V.tensor_copy(itab[:, 0:NE], rcon[:, R_IOTA:R_IOTA + NE]))
        mark(V.memset(boff[:, 0:NE], 0.0))
        link(V.tensor_scalar(itab[:, NE:ITEMS], sp_[b][:, 0:EXTRA], float(NE - 1), None, ALU.min))
        bx = boff[:, NE:ITEMS]
        past = rsmall[:, 704:704 + EXTRA]
        link(V.tensor_tensor(bx, rcon[:, R_IOTA:R_IOTA + EXTRA], sp_[b][:, 64:64 + EXTRA], ALU.subtract))
        link(V.tensor_scalar(bx, bx, 1.0, float(BLK), ALU.add, ALU.mult))
        link(V.tensor_scalar(past, rcon[:, R_IOTA:R_IOTA + EXTRA], n_extra, FAR, ALU.is_ge, ALU.mult))
        link(V.tensor_tensor(bx, bx, past, ALU.add))
        dve.sem_inc(score_free[b], 1)
        mark(V.tensor_copy(itabi[:, 0:ITEMS], itab[:, :]))
        half_n = rsmall[:, 518:519]
        link(V.tensor_scalar(half_n, n_extra, float(NE) + 0.5, 0.5, ALU.add, ALU.mult))
        link(V.tensor_scalar(half_n, half_n, M, M, ALU.add, ALU.subtract))
        mark(V.tensor_copy(itabi[:, ITEMS:ITEMS + 1], half_n))
        mark(V.tensor_copy(info[:, :, 0], rcon[:, R_TOK:R_TOK + TT]))
        link(V.tensor_copy(info[:, :, 1], rcon[:, R_TOK + TT:R_TOK + 2 * TT]))
        dve.sem_inc(list_ready, 1)

        iota_b = mcon[:, :].rearrange("p (o s) -> p o s", o=1).to_broadcast([P, TT, BLK])

        def chain(ins, when):
            ins.then_inc(loop_step, 1)
            dve.wait_ge(loop_step, when)

        def one_hot(e, item, when):
            V.tensor_copy(info[:, :, 2:5].rearrange("p t (o s) -> p t o s", o=1), wpart[:, :, e, 0:3])
            chain(V.tensor_scalar(rel[:, :], posm[:, :, e], boff[:, item], None, ALU.subtract), when)
            V.tensor_tensor(onehot[:, :, :], iota_b,
                            rel[:, :].rearrange("p (t o) -> p t o", o=1).to_broadcast([P, TT, BLK]), ALU.is_equal)\
                .then_inc(hot_ready, 1)

        def row_numbers(b, when):
            i = sp_[1]
            chain(V.tensor_scalar(gfl[:, :], i[:, 0:1], OOB, i[:, 1:2], ALU.add, ALU.add), when)
            V.tensor_copy(gidx[b][:, :], gfl[:, :])
            V.tensor_copy(snext[b][:, 0:1], gfl[:, :])
            V.tensor_reduce(snext[b][:, 1:2], i[:, 2:5], AX.X, ALU.add).then_inc(idx_ready, 1)

        def half_T():
            V.tensor_copy(xgT[:, 4:8, :], tp[1][:, :].rearrange("p (k t) -> p k t", k=4)).then_inc(xgT_d, 1)

        dve.wait_ge(list_ready, 1)
        for b in range(2):
            if b == 1:
                dve.wait_ge(idx_done, 1)
            one_hot(slice(b, b + 1), slice(b, b + 1), 2 * b + 1)
            if b == 0:
                shared_add(2)
            dve.wait_ge(idx_done, b + 1)
            row_numbers(b, 2 * b + 2)
        shared_add(3)

        def y_half(b, j):
            dve.wait_ge(scattered[b], j * 16 + 16)
            V.tensor_copy(scur[b][:, :], smid[b][:, 0:1])
            V.tensor_copy(wcur[b][:, :], smid[b][:, 1:2]).then_inc(w_ready, 1)
            dve.wait_ge(w_ready, j * 2 + (2 - b))
            dve.wait_ge(y_done, j * 2 + (2 - b))
            V.tensor_scalar(ysb[b][:, 512:1024], op[1][:, :], wcur[b][:, 0:1], None, ALU.mult).then_inc(y_dve, 1)

        dve.sem_inc(y_dve, 1)
        dve.wait_ge(xgT_done, 1)
        half_T()
        pairs = dve.value_load(itabi[0:1, ITEMS:ITEMS + 1], min_val=NE // 2, max_val=(NE + MAX_EXTRA + 1) // 2)
        with dve.Fori(0, pairs) as j:
            for b in range(2):
                e = dve.value_load(itabi[0:1, DS(j * 2 + (b + 2), 1)], min_val=0, max_val=NE - 1)
                dve.wait_ge(idx_ready, j * 2 + (b + 2))
                dve.wait_ge(y_dve, j * 2 + (b + 1))
                V.tensor_copy(smid[b][:, :], snext[b][:, :]).then_inc(smid_ready, 1)
                one_hot(DS(e, 1), DS(j * 2 + (b + 2), 1), j * 4 + (2 * b + 5))
                dve.wait_ge(h_done, j * 2 + (b + 1))
                dve.wait_ge(egate_ready, j * 2 + (b + 1))
                V.tensor_tensor(eact[:, :], egate[:, :], pp[0][:, FF:2 * FF], ALU.mult).then_inc(eact_ready, 1)
                dve.wait_ge(idx_done, j * 2 + (b + 3))
                dve.wait_ge(gathered[b], j * 16 + 16)
                dve.wait_ge(smid_ready, j * 2 + (b + 1))
                row_numbers(b, j * 4 + (2 * b + 6))
                dve.wait_ge(xgT_done, j * 2 + (b + 2))
                half_T()
                y_half(1 - b, j)
        y_half(1, pairs)

        for t in range(TT):
            dve.wait_ge(sum_in[t], 16)
            for n in range(2):
                mark(V.bn_stats(stat[:, n, :], xres[:, t, n * 512:(n + 1) * 512]))
            link()
            norm_rows(2, t, lng3)

    ctx.close()


_INS = ["x", "mem", "positions", "w_in", "cmp_pe_k", "cmp_pe_v", "cmp_w1_k", "cmp_w2_k", "cmp_w1_v", "cmp_w2_v",
        "w_out", "ln1_g", "ln1_b", "w_xq", "w_xkv", "w_xo", "ln2_g", "ln2_b", "w_router", "router_bias",
        "w_gate", "w_up", "w_down", "ws_gate", "ws_up", "ws_down", "ln3_g", "ln3_b"]


def kernel(**inputs):
    import numpy as _np
    import concourse.bacc as _bacc
    from concourse.bass_utils import run_bass_kernel_spmd as _run

    nc = _bacc.Bacc("TRN2", target_bir_lowering=False, num_devices=1)
    arrays = {f"in_{n}": _np.ascontiguousarray(inputs[n])[0] for n in _INS}
    arrays.update({f"in_{n}": a for n, a in constants().items()})
    io = {n[3:]: nc.dram_tensor(n, a.shape, mybir.dt.from_np(a.dtype), kind="ExternalInput").ap()
          for n, a in arrays.items()}
    out = nc.dram_tensor("out_0", (T, D), F32, kind="ExternalOutput").ap()
    build(nc, io, out)
    r = _run(nc, [arrays], core_ids=[0])
    return r.results[0]["out_0"].reshape(1, T, D)
```

```python
from contextlib import ExitStack

import numpy as np

import concourse.bass as bass
from concourse import mybir

F32 = mybir.dt.float32
BF16 = mybir.dt.bfloat16
I32 = mybir.dt.int32
U32 = mybir.dt.uint32
ALU = mybir.AluOpType
ACT = mybir.ActivationFunctionType
AX = mybir.AxisListType
DS = bass.DynSlice

P = 128
T = 512
D = 1024
TT = T // P
KD = D // P
MEM = 256
ALPHA = 2.0 ** 0.25
EPS = 1e-5
NEG = -1e30

RH, RD = 4, 128
NH, NG, ND = 8, 2, 64
HPG = NH // NG
NCMP, CMP_LEN, CMP_STRIDE, CMP_HID = 31, 32, 16, 256
RROT, NROT = RD // 2, 8
NFREQ = RROT + NROT
XH = 4

NE, TOPK, GROUPS, TOPG, FF = 64, 8, 8, 4, 256
EPG = NE // GROUPS
HALF = P // 2
SCALE_W = 2.5
BLK = 112
MAX_EXTRA = (T * TOPK - 1) // BLK
MAX_BLOCKS = (T + BLK - 1) // BLK
EXTRA = 40
ITEMS = NE + EXTRA
SETS = 4
MAX_TURNS = (NE + MAX_EXTRA + SETS - 1) // SETS
FAR = 1.0e6
OOB = 8192.0

C_ID, C_CAUS, C_INV, C_EPS = 0, 128, 256, 256 + NFREQ
NC_A = C_EPS + 4
NC_B = TT * NCMP * 2
R_TRI, R_ONE, R_IOTA, R_TRI64, R_TOK = 0, 128, 256, 384, 448
NC_R = R_TOK + 2 * TT


def constants():
    p = np.arange(P)
    a = np.zeros((P, NC_A), np.float32)
    a[:, C_ID:C_ID + P] = np.eye(P)
    a[:, C_CAUS:C_CAUS + P] = np.where(p[None, :] <= p[:, None], 0.0, NEG)
    inv_r = 10000.0 ** (-np.arange(RROT) / RROT)
    inv_n = 500000.0 ** (-np.arange(NROT) / NROT)
    a[:, C_INV:C_INV + NFREQ] = np.concatenate([inv_r, inv_n])[None, :]
    a[:, C_EPS] = EPS
    t = np.arange(TT)[None, :, None] * P + p[:, None, None]
    ok = CMP_STRIDE * np.arange(NCMP)[None, None, :] + CMP_LEN - 1 <= t
    b = np.stack([ok.astype(np.float32), np.where(ok, 0.0, NEG)], 1).reshape(P, -1).astype(np.float32)
    decay = np.zeros((P, RH, T), np.float64)
    rel = np.arange(T)[None, :] - p[:, None]
    for h in range(RH):
        decay[:, h] = np.where(rel >= 0, np.exp(np.log(1 - 2.0 ** (-5 - h)) * np.maximum(rel, 0)), 0) * RD ** -0.5
    r = np.zeros((P, NC_R), np.float32)
    r[:, R_TRI:R_TRI + P] = p[:, None] < p[None, :]
    r[:, R_ONE:R_ONE + P] = 1.0
    r[:, R_IOTA:R_IOTA + P] = p[None, :]
    e = np.arange(NE)
    r[:NE, R_TRI64:R_TRI64 + NE] = e[:, None] <= e[None, :]
    r[:, R_TOK:R_TOK + TT] = p[:, None]
    r[:, R_TOK + TT:R_TOK + 2 * TT] = np.arange(TT)[None, :] * P - OOB
    return {"c_first": a, "c_cmp": b, "c_decay": decay.reshape(P, -1).astype(np.float32), "c_route": r}


class Units:

    def __init__(self, names):
        self.at = {name: n for n, name in enumerate(names)}
        self.n = len(names)

    def no(self, *name):
        return self.at[name if len(name) > 1 else name[0]]


W_COLS = [512] * 6 + [280]
PROJ = Units([("in", c, t) for c in range(7) for t in range(TT)]
             + [("xk", d) for d in range(KD)]
             + [("out", t, n) for t in range(TT) for n in range(2)]
             + [("xv", m, n) for n in range(2) for m in range(2)]
             + [("xq", d) for d in range(KD)]
             + [("xo", t, n) for t in range(TT) for n in range(2)]
             + [("sgu", t) for t in range(TT)] + [("sdn", t, n) for t in range(TT) for n in range(2)])
ATT = [(pr, h, br, q) for pr in range(NH // 2) for q in range(TT) for br in range(2) for h in (2 * pr, 2 * pr + 1)]
STAGED = [(c, t) for c in (0, 1, 4, 5, 6) for t in range(TT)]


def staged_units(c, t):
    return [("ret", c, t)] if c < 2 else [("nq", t, 0), ("nq", t, 1)] if c == 4 \
        else [("kv5", t, 0), ("kv5", t, 1)] if c == 5 else [("kv6", t)]


def x_units(t):
    return [("x", t, j) for j in range(2)]


TRAN = Units(x_units(0) + x_units(1) + x_units(2) + staged_units(0, 0) + x_units(3)
             + [u for c, t in STAGED[1:12] for u in staged_units(c, t)]
             + [("oret", t) for t in range(TT)]
             + [u for c, t in STAGED[12:] for u in staged_units(c, t)]
             + [("mem", m, j) for m in range(2) for j in range(2)]
             + [("hid", j) for j in range(2)]
             + [("pc", t) for t in range(TT)]
             + [("pt", n) for n in range(len(ATT))]
             + [("x1", t, j) for t in range(TT) for j in range(2)]
             + [("px", h, t) for h in range(XH) for t in range(TT)]
             + [("x2", t, j) for t in range(TT) for j in range(2)]
             + [("sh", t) for t in range(TT)])
SCORE = Units([("ret", h, k) for h in range(RH) for k in range(TT)]
              + [("hid", j) for j in range(2)] + [("kvc", 0)]
              + [("sc", t, a) for t in range(TT) for a in range(2)]
              + [("logit", t) for t in range(TT)] + [("pos", 0), ("extra", 0), ("cum", 0)])
OUTP = Units([("ret", h) for h in range(RH)] + [("nsa", pr) for pr in range(NH // 2)]
             + [("x", h, d) for h in range(XH) for d in range(2)])

CHUNKS = ([("in", c) for c in range(7)] + [("w1", 0), ("w1", 1)] + [("xkv", 0), ("xkv", 1)]
          + [("out", 0), ("out", 1), ("xkv", 2), ("xkv", 3), ("xq", 0), ("xq", 1), ("xo", 0), ("xo", 1), ("sgu", 0), ("sdn", 0)])
SLOT = [n % 4 for n in range(len(CHUNKS))]
SLOT[-1] = 2
CHUNK_NO = {name: n for n, name in enumerate(CHUNKS)}


def loads_before(n):
    return sum(SLOT[m] == SLOT[n] for m in range(n + 1))


def last_in_slot(slot, before):
    found = [m for m in range(before) if SLOT[m] == slot]
    return found[-1] if found else None


def build(nc, io, out):
    ctx = ExitStack()
    base = (nc.sbuf_base + 31) // 32 * 32
    KB = 1024

    def at(name, shape, dt, offset):
        return nc.alloc_sbuf_tensor_at(name, shape, dt, offset=base + offset)

    def sem(name):
        return ctx.enter_context(nc.semaphore(name))

    O_RING, O_DOWN, O_X, O_A, O_B, O_C, O_D, O_E, O_F = (k * KB for k in (0, 64, 96, 112, 128, 144, 160, 176, 200))
    ring = [at(f"ring{s}", [P, 4096], F32, O_RING + s * 16 * KB) for s in range(4)]
    xres = at("xres", [P, TT, D], F32, O_X)
    xT = at("xT", [P, KD, T], F32, O_A)
    nqT = at("nqT", [P, NH // 2, T], F32, O_DOWN)
    nqrT = at("nqrT", [P, NH // 2, T], F32, O_DOWN + 8 * KB)
    kT = [at(f"k{n}T", [P, NG, 2, T], F32, O_DOWN + (16 + 8 * k) * KB) for k, n in enumerate(("sel", "win"))]
    retT = [at(f"ret{n}T", [P, RH, T], F32, O_C + k * 8 * KB) for k, n in enumerate("qk")]
    rv = at("rv", [P, TT, RH * RD], F32, O_D)
    swish = at("swish", [P, TT, RH * RD], F32, O_D + 8 * KB)
    decay = at("decay", [P, RH, T], F32, O_E)
    retS = at("retS", [P, TT, T], F32, O_E + 8 * KB)
    oret = at("oret", [P, TT, RH * RD], F32, O_E + 16 * KB)
    mixT = at("mixT", [P, KD, T], F32, O_B)
    ang = at("ang", [P, TT, NFREQ], F32, O_B)
    turns = at("turns", [P, 2, TT, NFREQ], F32, O_B + 2 * KB)
    stage = [at(f"stage{b}", [P, D], F32, O_B + (8 + 4 * b) * KB) for b in range(2)]
    kvcT = at("kvcT", [P, 4, T], F32, O_D)
    ab = at("ab", [P, 2, 16, NG, NCMP], F32, O_D + 8 * KB)
    w2k = at("w2k", [P, 2, 2, ND], F32, O_C)
    w2v = at("w2v", [P, 2, ND], F32, O_C + 1024)
    hid = at("hid", [P, CMP_HID], F32, O_C + 1536)
    hidkT = at("hidkT", [P, 2, NG * NCMP], F32, O_C + 3584)
    hidvT = at("hidvT", [P, 2, NG, HPG, 32], F32, O_C + 4096)
    pc = [at(f"pc{b}", [P, NH, 32], F32, O_C + 6144 + b * 1024) for b in range(2)]
    pcT = at("pcT", [P, NG, T], F32, O_C + 8 * KB)
    vsw = at("vsw", [P, 2, TT, NG * ND], F32, O_C + 12 * KB)
    PT = [at(f"PT{b}", [P, TT, P], F32, O_E + b * 2 * KB) for b in range(8)]
    prob = [at(f"prob{b}", [P, T], F32, O_E + (16 + 2 * b) * KB) for b in range(4)]
    vcmp = at("vcmp", [P, HPG, NG, ND], F32, O_C + 1536)
    mem_in = at("mem_in", [P, 2, D], F32, O_E)
    memT = at("memT", [P, KD, MEM], F32, O_D)
    kxT = at("kxT", [P, KD, MEM], F32, O_A)
    vx = at("vx", [P, 2, D], F32, O_A + 8 * KB)
    x1T = at("x1T", [P, KD, T], F32, O_C)
    xqT = at("xqT", [P, KD, T], F32, O_B)
    xoT = at("xoT", [P, KD, T], F32, O_C)
    PX = [at(f"PX{b}", [P, 2, T], F32, O_E + b * 4 * KB) for b in range(2)]
    probx = [at(f"probx{b}", [P, MEM], F32, O_E + (8 + b) * KB) for b in range(4)]
    lng = at("lng", [P, 2, D], F32, O_D + 8 * KB)
    x2T = at("x2T", [P, KD, T], F32, O_B)
    sgate = at("sgate", [P, FF], F32, O_C)
    sact = at("sact", [P, TT, FF], F32, O_C + 1 * KB)
    sactT = at("sactT", [P, 2, T], F32, O_C + 5 * KB)
    wrt = at("wrt", [P, KD, NE], F32, O_E + 22 * KB)
    rcon = at("rcon", [P, NC_R], F32, O_A + 6 * KB)
    rbias = at("rbias", [P, NE], F32, O_A + 8 * KB)
    score = at("score", [P, TT, NE], F32, O_D)
    biased = at("biased", [P, TT, NE], F32, O_D + 1 * KB)
    tmpa = at("tmpa", [P, TT, NE], F32, O_D + 2 * KB)
    hot8 = at("hot8", [P, TOPK, NE], F32, O_D + 3 * KB)
    maskt = at("maskt", [P, TT, NE], F32, O_A)
    gtop = at("gtop", [P, TT, GROUPS, 8], F32, O_A + 1 * KB)
    rsmall = at("rsmall", [P, 1024], F32, O_A + 2 * KB)
    gu = [at(f"wgu{b}", [P, 2, KD, FF], F32, o) for b, o in enumerate((O_RING, O_RING + 16 * KB, O_RING + 48 * KB, O_B))]
    wdown = [at(f"wdown{b}", [P, 2, D], F32, o)
             for b, o in enumerate((O_DOWN, O_DOWN + 8 * KB, O_RING + 40 * KB, O_D + 8 * KB))]
    xg = [at(f"xg{b}", [P, D], F32, O_DOWN + (16 + 4 * b) * KB) for b in range(2)]
    ysb = [at(f"ysb{b}", [P, D], F32, O_DOWN + (24 + 4 * b) * KB) for b in range(2)]
    xgT = at("xgT", [P, KD, BLK], F32, O_E)
    egate = at("egate", [P, FF], F32, O_E + 4 * KB)
    eact = at("eact", [P, FF], F32, O_E + 5 * KB)
    eactT = at("eactT", [P, 2, BLK], F32, O_E + 6 * KB)
    onehot = at("onehot", [P, TT, BLK], BF16, O_E + 7 * KB)
    posm = at("posm", [P, TT, NE], F32, O_E + 8 * KB)
    wexp = at("wexp", [P, TT, NE], F32, O_A + 10 * KB)
    wpart = at("wpart", [P, TT, NE, 4], BF16, O_A + 12 * KB)
    info = at("info", [P, TT, 8], BF16, O_E + 10 * KB)
    itab = at("itab", [P, ITEMS], F32, O_E + 10 * KB + 256)
    itabi = at("itabi", [P, ITEMS + 2], I32, O_E + 11 * KB)
    boff = at("boff", [P, ITEMS], F32, O_E + 11 * KB + 512)
    rel = at("rel", [P, TT], F32, O_E + 12 * KB)
    gidx = [at(f"gidx{b}", [P, 1], I32, O_E + 12 * KB + 64 + 32 * b) for b in range(2)]
    snext = [at(f"snext{b}", [P, 2], F32, O_E + 12 * KB + 128 + 32 * b) for b in range(2)]
    scur = [at(f"scur{b}", [P, 1], I32, O_E + 12 * KB + 192 + 32 * b) for b in range(2)]
    wcur = [at(f"wcur{b}", [P, 1], F32, O_E + 12 * KB + 448 + 32 * b) for b in range(2)]
    first_down = at("first_down", [P, 8], F32, O_E + 12 * KB + 384)
    smid = [at(f"smid{b}", [P, 2], F32, O_E + 12 * KB + 320 + 32 * b) for b in range(2)]
    gfl = at("gfl", [P, 1], F32, O_E + 12 * KB + 256)
    mcon = at("mcon", [P, BLK], F32, O_E + 12 * KB + 512)
    lng3 = at("lng3", [P, 2, D], F32, O_E + 14 * KB)
    c1 = at("c1", [P, NC_A], F32, O_F)
    tab = at("tab", [P, 2, TT, NFREQ], F32, O_F + 1536)
    gate = at("gate", [P, TT, 3 * NH], F32, O_F + 3840)
    ident_b = at("ident_b", [P, P], BF16, O_F + 4224)
    causal_b = at("causal_b", [P, P], BF16, O_F + 4480)
    kcmpT = at("kcmpT", [P, NG * NCMP], F32, O_F + 4736)
    ccmp = at("ccmp", [P, 2, TT, NCMP], F32, O_F + 4992)
    posi = at("posi", [P, TT], I32, O_F + 6016)
    posf = at("posf", [P, TT], F32, O_F + 6048)
    stat = at("stat", [P, 4, 6], F32, O_F + 6080)
    mv = at("mv", [P, TT, 2], F32, O_F + 6208)
    std = at("std", [P, TT], F32, O_F + 6240)
    nmax = at("nmax", [P, 2, 8], F32, O_F + 6272)
    rsum = at("rsum", [P, 2, 8], F32, O_F + 6336)
    rinv = at("rinv", [P, 2, 8], F32, O_F + 6400)
    cmpm = at("cmpm", [P, NH], F32, O_F + 6496)
    pe2 = at("pe2", [P, 2, 16], F32, O_F + 6528)
    rott = at("rott", [P, 2, 512], F32, O_E + 16 * KB)
    rottn = at("rottn", [P, 2, 2 * NH * NROT], F32, O_F + 6656)

    ident = c1[:, C_ID:C_ID + P]
    eps = c1[:, C_EPS:C_EPS + 1]

    def pair(name):
        return [ctx.enter_context(nc.psum_tensor(f"{name}{b}", [P, 512], F32)) for b in range(2)]

    pp, tp, sp_, op = pair("proj"), pair("tran"), pair("score"), pair("outp")

    att_banks = sp_ + pp

    x2_dram = nc.dram_tensor("x2_rows", [T, D], F32, kind="Internal").ap()
    sum_dram = nc.dram_tensor("sum_rows", [T, D], F32, kind="Internal").ap()

    x_in = [sem(f"x_in{t}") for t in range(TT)]
    const_in, decay_in, mem_loaded, cmp_in = (sem(n) for n in ("const_in", "decay_in", "mem_loaded", "cmp_in"))
    ln_in = [sem(f"ln{n + 1}_in") for n in range(3)]
    pe_in, route_in = sem("pe_in"), sem("route_in")
    pos_in, mask_made = sem("pos_in"), sem("mask_made")
    first_in = sem("first_in")
    loaded = [sem(f"loaded{s}") for s in range(4)]
    proj_done, tran_done, score_done, outp_done = (sem(n) for n in ("proj_done", "tran_done", "score_done", "outp_done"))
    proj_free, tran_free, score_free, outp_free = ([sem(f"{n}_free{b}") for b in range(2)] for n in ("proj", "tran", "score", "outp"))
    dve_step, act_step = sem("dve_step"), sem("act_step")
    angles_ready, tables_ready = sem("angles_ready"), sem("tables_ready")
    staged, raw_staged = sem("staged"), sem("raw_staged")
    rets_ready, rstd_asked, rstd_ready, oret_ready = (sem(n) for n in ("rets_ready", "rstd_asked", "rstd_ready", "oret_ready"))
    pads_ready = sem("pads_ready")
    zeros_ready, pv_done, smid_ready, loop_step = (sem(n) for n in ("zeros_ready", "pv_done", "smid_ready", "loop_step"))
    sp_turn = sem("sp_turn")
    offset_turn = sem("offset_turn")
    pool_turn = sem("pool_turn")
    ab_ready, hid_ready, kvcmp_ready = sem("ab_ready"), sem("hid_ready"), sem("kvcmp_ready")
    pc_asked, pc_exp, pc_ready = sem("pc_asked"), sem("pc_exp"), sem("pc_ready")
    att_scored, x_scored = sem("att_scored"), sem("x_scored")
    max_ready, exp_ready, prob_ready = sem("max_ready"), sem("exp_ready"), sem("prob_ready")
    var_ready, std_ready = sem("var_ready"), sem("std_ready")
    ln_ready = sem("ln_ready")
    xmax_ready, xexp_ready, xprob_ready = sem("xmax_ready"), sem("xexp_ready"), sem("xprob_ready")
    sgate_ready, sact_ready = sem("sgate_ready"), sem("sact_ready")
    score_sig, mask_ready, extra_ready = (sem(n) for n in ("score_sig", "mask_ready", "extra_ready"))
    x2_saved = sem("x2_saved")
    e_gu_in = [sem(f"e_gu_in{b}") for b in range(SETS)]
    e_dn_in = [sem(f"e_dn_in{b}") for b in range(SETS)]
    hot_ready, idx_done, idx_ready = sem("hot_ready"), sem("idx_done"), sem("idx_ready")
    gathered = [sem(f"gathered{b}") for b in range(2)]
    scattered = [sem(f"scattered{b}") for b in range(2)]
    xgT_done, xgT_a, xgT_d = sem("xgT_done"), sem("xgT_a"), sem("xgT_d")
    h_done, egate_ready, eact_ready, eT_done, eT_ready = (sem(n) for n in ("h_done", "egate_ready", "eact_ready", "eT_done", "eT_ready"))
    y_done, y_act, y_dve = sem("y_done"), sem("y_act"), sem("y_dve")
    list_ready, moe_set = sem("list_ready"), sem("moe_set")
    half_added = sem("half_added")
    base_ready, base_saved, w_ready = sem("base_ready"), sem("base_saved"), sem("w_ready")
    sum_in = [sem(f"sum_in{t}") for t in range(TT)]
    normed, gained, fin_ready, out_saved = sem("normed"), sem("gained"), sem("fin_ready"), sem("out_saved")

    def stage_no(c, t):
        return STAGED.index((c, t))

    def stage_free(eng, n):
        if n >= 2:
            wait_done(eng, TRAN, tran_done, *staged_units(*STAGED[n - 2])[-1])

    def wait_done(eng, units, done, *name):
        eng.wait_ge(done, units.no(*name) + 1)

    def chunk_view(slot, blocks, cols):
        return ring[slot][:, 0:blocks * cols].rearrange("p (k n) -> p k n", k=blocks)

    def chunk_parts(name):
        kind, c = name
        n = CHUNK_NO[name]
        kp = lambda w: w.rearrange("(k p) n -> p k n", p=P)
        if kind == "in":
            v = chunk_view(SLOT[n], KD, W_COLS[c])
            src = kp(io["w_in"][:, 512 * c:512 * c + W_COLS[c]])
            return v, [(v, src)] if c > 0 else [(v[:, KD // 2:], src[:, KD // 2:])]
        if kind == "w1":
            v = chunk_view(SLOT[n], 16, CMP_HID)
            return v, [(v, kp(io["cmp_w1_k" if c == 0 else "cmp_w1_v"]))]
        if kind == "sgu":
            v = ring[SLOT[n]][:, :].rearrange("p (g k n) -> p g k n", g=2, k=KD)
            return v, [(v[:, 0], kp(io["ws_gate"])), (v[:, 1], kp(io["ws_up"]))]
        if kind == "sdn":
            v = chunk_view(SLOT[n], 2, D)
            return v, [(v, kp(io["ws_down"]))]
        w = {"xkv": "w_xkv", "out": "w_out", "xq": "w_xq", "xo": "w_xo"}[kind]
        v = chunk_view(SLOT[n], KD, 512)
        return v, [(v, kp(io[w][:, 512 * c:512 * c + 512]))]

    def chunk_loaded(name):
        n = CHUNK_NO[name]
        return loaded[SLOT[n]], 16 * sum(len(chunk_parts(CHUNKS[m])[1]) for m in range(n + 1) if SLOT[m] == SLOT[n])

    def chunk_used(name):
        kind, c = name
        if kind == "w1":
            return score_done, SCORE.no("hid", c) + 1
        last = {"in": ("in", c, TT - 1), "xkv": ("xk", 4 * c + 3) if c < 2 else ("xv", 1, c - 2),
                "out": ("out", TT - 1, 1), "xq": ("xq", 4 * c + 3), "xo": ("xo", TT - 1, 1),
                "sgu": ("sgu", TT - 1), "sdn": ("sdn", TT - 1, 1)}[kind]
        return proj_done, PROJ.no(*last) + 1

    def pv_done_at(group):
        pr, q = divmod(group, TT)
        return (outp_done, OUTP.no("nsa", pr) + 1) if q == TT - 1 else (pv_done, (TT - 1) * pr + q + 1)

    POOL_TILES = 2
    block = ctx.enter_context(nc.Block())

    @block.sync
    def _(sp):
        def load_x(t):
            sp.dma_start(xres[:, t, :], io["x"][t * P:(t + 1) * P, :]).then_inc(x_in[t], 16)

        sp.dma_start(c1[:, :], io["c_first"]).then_inc(const_in, 16)
        load_x(0)
        with nc.allow_non_contiguous_dma(reason="a position for each row"):
            sp.dma_start(posi[:, :], io["positions"].rearrange("(t p) -> p t", p=P)).then_inc(pos_in, 16)
        half = KD // 2 * P
        sp.dma_start(chunk_view(0, KD, W_COLS[0])[:, 0:KD // 2],
                     io["w_in"][0:half, 0:W_COLS[0]].rearrange("(k p) n -> p k n", p=P)).then_inc(first_in, 16)
        for n, name in enumerate(CHUNKS):
            if n == 1:
                for t in range(1, TT):
                    load_x(t)
            before = last_in_slot(SLOT[n], n)
            if before is not None:
                sp.wait_ge(*chunk_used(CHUNKS[before]))
            for dst, src in chunk_parts(name)[1]:
                sp.dma_start(dst, src).then_inc(loaded[SLOT[n]], 16)

        def load_expert(b, e):
            for g, w in enumerate(("w_gate", "w_up")):
                sp.dma_start(gu[b][:, g], io[w][DS(e, 1), :, :].rearrange("o (p k) n -> p (o k) n", k=KD))\
                  .then_inc(e_gu_in[b], 16)

        def load_down(b, e):
            sp.dma_start(wdown[b][:, :, :], io["w_down"][DS(e, 1), :, :].rearrange("o (p k) n -> p (o k) n", k=2))\
              .then_inc(e_dn_in[b], 16)

        for b in range(2):
            sp.wait_ge(*chunk_used(CHUNKS[last_in_slot(b, len(CHUNKS))]))
            load_expert(b, b)
        sp.wait_ge(outp_done, OUTP.no("nsa", NH // 2 - 1) + 1)
        for b in range(2):
            load_down(b, b)
        sp.wait_ge(*chunk_used(("xo", 1)))
        load_down(2, 2)
        sp.dma_start(first_down[:, :], io["c_route"][:, 0:8]).then_inc(e_dn_in[3], 16)
        sp.wait_ge(ln_ready, 2 * TT)
        load_down(3, 3)
        sp.wait_ge(*chunk_used(("sgu", 0)))
        for b in (2, 3):
            load_expert(b, b)
        for t in range(TT):
            sp.wait_ge(base_ready, t + 1)
            sp.dma_start(sum_dram[t * P:(t + 1) * P, :], xres[:, t, :]).then_inc(base_saved, 16)
        sp.wait_ge(list_ready, 1)
        turns_n = sp.value_load(itabi[0:1, ITEMS:ITEMS + 1], min_val=NE // SETS, max_val=MAX_TURNS)
        with sp.Fori(1, turns_n) as j:
            for b in range(SETS):
                e = sp.value_load(itabi[0:1, DS(j * SETS + b, 1)], min_val=0, max_val=NE - 1)
                sp.wait_ge(h_done, j * SETS + (b - 3))
                sp.sem_inc(sp_turn, 1)
                load_expert(b, e)
                sp.wait_ge(y_done, j * SETS + (b - 2))
                sp.sem_inc(sp_turn, 1)
                load_down(b, e)
        for b in range(2):
            sp.wait_ge(scattered[b], turns_n * 32 + 16 * (b + 1))
            sp.sem_inc(sp_turn, 1)
        for t in range(TT):
            sp.dma_start(xres[:, t, :], sum_dram[t * P:(t + 1) * P, :]).then_inc(sum_in[t], 16)
        for t in range(TT):
            sp.wait_ge(*((gained, t + 1) if t < POOL_TILES else (fin_ready, t - POOL_TILES + 1)))
            sp.dma_start(out[t * P:(t + 1) * P, :], xres[:, t, :]).then_inc(out_saved, 16)
        sp.wait_ge(out_saved, 16 * TT)

    @block.gpsimd
    def _(pool):
        with nc.allow_non_contiguous_dma(reason="a few small rows"):
            pool.wait_ge(proj_done, 2)
            pool.dma_start(decay[:, :, :], io["c_decay"].rearrange("p (h t) -> p h t", h=RH)).then_inc(decay_in, 16)
            for j, w in enumerate(("cmp_pe_k", "cmp_pe_v")):
                pool.dma_start(pe2[:, j, :], io[w].rearrange("(l h) d -> (h d) l", h=2)).then_inc(pe_in, 16)
            pool.dma_start(ccmp[:, :, :, :], io["c_cmp"].rearrange("p (a t c) -> p a t c", a=2, t=TT)).then_inc(pe_in, 16)
            pool.wait_ge(outp_done, OUTP.no("ret", RH - 1) + 1)
            pool.dma_start(mem_in[:, :, :], io["mem"].rearrange("(m p) n -> p m n", p=P)).then_inc(mem_loaded, 16)
            for j in range(2):
                pool.dma_start(w2k[:, :, j, :], io["cmp_w2_k"].rearrange("(k p) d -> p k d", p=P)).then_inc(cmp_in, 16)
            pool.dma_start(w2v[:, :, :], io["cmp_w2_v"].rearrange("(k p) d -> p k d", p=P)).then_inc(cmp_in, 16)

            def load_norm(dst, n):
                for j, w in enumerate(("g", "b")):
                    src = io[f"ln{n}_{w}"].rearrange("(o n) -> o n", o=1).to_broadcast([P, D])
                    pool.dma_start(dst[:, j, :], src).then_inc(ln_in[n - 1], 16)

            pool.wait_ge(score_done, SCORE.no("hid", 1) + 1)
            load_norm(lng, 1)
            pool.wait_ge(ln_ready, TT)
            load_norm(lng, 2)
            pool.dma_start(wrt[:, :, :], io["w_router"].rearrange("(k p) n -> p k n", p=P)).then_inc(route_in, 16)
            pool.dma_start(mcon[:, :], io["c_route"][:, R_IOTA:R_IOTA + BLK]).then_inc(route_in, 16)
            load_norm(lng3, 3)
            pool.wait_ge(outp_done, OUTP.n)
            pool.dma_start(rcon[:, :], io["c_route"]).then_inc(route_in, 16)
            pool.dma_start(rbias[:, :], io["router_bias"].rearrange("(o n) -> o n", o=1).to_broadcast([P, NE]))\
                .then_inc(route_in, 16)
        for t in range(TT):
            pool.wait_ge(ln_ready, TT + t + 1)
            pool.dma_start(x2_dram[t * P:(t + 1) * P, :], xres[:, t, :]).then_inc(x2_saved, 16)
        pool.wait_ge(x2_saved, 16 * TT)

        def gather(b):
            pool.indirect_dma_start(out=xg[b][0:BLK, :], out_offset=None, in_=x2_dram[:, :],
                                    in_offset=bass.IndirectOffsetOnAxis(ap=gidx[b][0:BLK, 0:1], axis=0),
                                    bounds_check=T - 1, oob_is_err=False).then_inc(gathered[b], 16)

        def scatter(b):
            pool.indirect_dma_start(out=sum_dram[:, :],
                                    out_offset=bass.IndirectOffsetOnAxis(ap=scur[b][0:BLK, 0:1], axis=0),
                                    in_=ysb[b][0:BLK, :], in_offset=None,
                                    bounds_check=T - 1, oob_is_err=False, compute_op=ALU.add).then_inc(scattered[b], 16)

        pool.wait_ge(moe_set, 7)
        for b in range(2):
            pool.wait_ge(idx_ready, b + 1)
            gather(b)
        pool.wait_ge(base_saved, 16 * TT)
        for b in range(2):
            scatter(b)
            pool.wait_ge(scattered[b], 16)
        pool.wait_ge(list_ready, 1)
        turns_n = pool.value_load(itabi[0:1, ITEMS:ITEMS + 1], min_val=NE // SETS, max_val=MAX_TURNS)
        with pool.Fori(0, turns_n) as j:
            for b in range(SETS):
                pool.wait_ge(xgT_done, j * SETS + (b + 1))
                pool.wait_ge(idx_ready, j * SETS + (b + 3))
                pool.sem_inc(pool_turn, 1)
                gather(b % 2)
                pool.wait_ge(y_act, j * SETS + (b + 2))
                pool.wait_ge(y_dve, j * SETS + (b + 2))
                pool.wait_ge(scattered[b % 2], j * 32 + 16 * ((b + 1) // 2 + 1))
                pool.sem_inc(pool_turn, 1)
                scatter(1 - b % 2)
        pool.wait_ge(y_act, turns_n * SETS + 2)
        pool.wait_ge(y_dve, turns_n * SETS + 2)
        pool.wait_ge(scattered[0], turns_n * 32 + 16)
        pool.sem_inc(pool_turn, 1)
        scatter(1)
        for b in range(2):
            pool.wait_ge(gathered[b], turns_n * 32 + 16)
        pool.wait_ge(ln_in[2], 32)
        for t in range(POOL_TILES):
            x = xres[:, t, :]
            pool.wait_ge(normed, t + 1)
            nc.gpsimd.tensor_tensor(x, x, lng3[:, 0, :], ALU.mult).then_inc(offset_turn, 1)
            pool.wait_ge(offset_turn, t + 1)
            nc.gpsimd.tensor_tensor(x, x, lng3[:, 1, :], ALU.add).then_inc(gained, 1)

    @block.tensor
    def _(pe):
        mm, count = nc.tensor.matmul, {"p": 0, "t": 0, "s": 0, "o": 0}

        def take(key, units, free, name):
            n = units.no(*name)
            assert n == count[key], (name, n, count[key])
            count[key] += 1
            if n >= 2:
                pe.wait_ge(free[n % 2], n // 2)
            return n % 2

        def transposes(name, parts):
            b = take("t", TRAN, tran_free, name)
            for src, dst in parts:
                rows = slice(0, P) if src.shape[0] == P else slice(HALF * name[1], HALF * name[1] + src.shape[0])
                last = nc.tensor.transpose(dst(tp[b]), src, ident[rows, rows])
            last.then_inc(tran_done, 1)

        def four(src, blocks):
            return [(src[:, k * P:(k + 1) * P], lambda bank, j=j: bank[:, j * P:(j + 1) * P])
                    for j, k in enumerate(blocks)]

        def copied(units, free, *name):
            m = units.no(*name)
            pe.wait_ge(free[m % 2], m // 2 + 1)

        def x_T(t):
            pe.wait_ge(x_in[t], 16)
            for j in range(2):
                transposes(("x", t, j), four(xres[:, t, :], range(4 * j, 4 * j + 4)))

        def proj(c, t):
            w = chunk_parts(("in", c))[0]
            if t == 0:
                pe.wait_ge(*((first_in, 16) if c == 0 else chunk_loaded(("in", c))))
            if c == 0:
                for j in range(2):
                    copied(TRAN, tran_free, "x", t, j)
            b = take("p", PROJ, proj_free, ("in", c, t))
            for k in range(KD):
                if (c, t, k) == (0, 0, KD // 2):
                    pe.wait_ge(*chunk_loaded(("in", 0)))
                last = mm(pp[b][:, 0:W_COLS[c]], xT[:, k, t * P:(t + 1) * P], w[:, k, :],
                          start=(k == 0), stop=(k == KD - 1))
            last.then_inc(proj_done, 1)

        def staged_T(c, t):
            n = stage_no(c, t)
            pe.wait_ge(staged, n + 1)
            st, names = stage[n % 2][:, :], staged_units(c, t)
            transposes(names[0], four(st, range(2 if c == 6 else 4)))
            if c in (4, 5):
                transposes(names[1], four(st, range(4, 8 if c == 4 else 6)))

        pe.wait_ge(const_in, 16)
        x_T(0)
        proj(0, 0)
        x_T(1)
        proj(0, 1)
        x_T(2)
        staged_T(0, 0)
        proj(0, 2)
        x_T(3)
        staged_T(0, 1)
        proj(0, 3)
        staged_T(0, 2)
        for t in range(TT):
            proj(1, t)
            staged_T(*STAGED[TT + t - 1])
        proj(2, 0)
        staged_T(1, TT - 1)
        for c, t in [(2, 1), (2, 2), (2, 3)] + [(3, t) for t in range(TT)]:
            proj(c, t)

        def ret_scores(h):
            for k in range(TT):
                b = take("s", SCORE, score_free, ("ret", h, k))
                n = T - k * P
                mm(sp_[b][:, 0:n], retT[1][:, h, k * P:(k + 1) * P], retT[0][:, h, k * P:T],
                   start=True, stop=True).then_inc(score_done, 1)

        def ret_out(h):
            pe.wait_ge(rets_ready, TT * (h + 1))
            b = take("o", OUTP, outp_free, ("ret", h))
            for q in range(TT):
                for k in range(q + 1):
                    last = mm(op[b][:, q * P:(q + 1) * P], retS[:, k, (q - k) * P:(q - k + 1) * P],
                              rv[:, k, h * RD:(h + 1) * RD], start=(k == 0), stop=(k == q))
            last.then_inc(outp_done, 1)

        for t in range(2, TT):
            copied(TRAN, tran_free, "ret", 1, t)
        for h in range(RH):
            ret_scores(h)
            proj(4, h)
            if h == 0:
                for t in range(2, TT):
                    copied(PROJ, proj_free, "in", 2, t)
            ret_out(h)
            if h >= 1:
                staged_T(4, h - 1)
        proj(5, 0)
        staged_T(4, TT - 1)
        pe.wait_ge(oret_ready, RH)
        for t in range(TT):
            transposes(("oret", t), four(oret[:, t, :], range(RH)))
        for n in range(stage_no(5, 1), len(STAGED)):
            proj(*STAGED[n])
            staged_T(*STAGED[n - 1])

        w1 = [chunk_parts(("w1", j))[0] for j in range(2)]
        for j in range(2):
            pe.wait_ge(*chunk_loaded(("w1", j)))
            pe.wait_ge(ab_ready, j + 1)
        hb = [take("s", SCORE, score_free, ("hid", j)) for j in range(2)]
        for l in range(16):
            for j in range(2):
                last = mm(sp_[hb[j]][HALF * j:HALF * j + NG * NCMP, 0:CMP_HID],
                          ab[:, j, l, :, :].rearrange("p g c -> p (g c)"), w1[j][:, l, :], start=(l == 0), stop=(l == 15))
                if l == 15:
                    last.then_inc(score_done, 1)
        staged_T(6, TT - 1)
        pe.wait_ge(mem_loaded, 16)
        for m in range(2):
            for j in range(2):
                transposes(("mem", m, j), four(mem_in[:, m, :], range(4 * j, 4 * j + 4)))
        for j in range(2):
            pe.wait_ge(hid_ready, j + 1)
            transposes(("hid", j), [(hid[HALF * j:HALF * j + NG * NCMP, k * P:(k + 1) * P],
                                     lambda bank, k=k: bank[:, k * P:k * P + NG * NCMP]) for k in range(2)])

        def mem_keys(d):
            w = chunk_parts(("xkv", d // 4))[0]
            if d % 4 == 0:
                pe.wait_ge(*chunk_loaded(("xkv", d // 4)))
            b = take("p", PROJ, proj_free, ("xk", d))
            for k in range(KD):
                last = mm(pp[b][:, 0:MEM], w[:, k, d % 4 * P:(d % 4 + 1) * P], memT[:, k, :],
                          start=(k == 0), stop=(k == KD - 1))
            last.then_inc(proj_done, 1)

        def mem_values(c, m):
            w = chunk_parts(("xkv", 2 + c))[0]
            if m == 0:
                pe.wait_ge(*chunk_loaded(("xkv", 2 + c)))
            b = take("p", PROJ, proj_free, ("xv", m, c))
            for k in range(KD):
                last = mm(pp[b][:, :], memT[:, k, m * P:(m + 1) * P], w[:, k, :], start=(k == 0), stop=(k == KD - 1))
            last.then_inc(proj_done, 1)

        for j in range(2):
            copied(TRAN, tran_free, "mem", 1, j)
        mem_keys(0)
        mem_keys(1)
        pe.wait_ge(cmp_in, 48)
        for j in range(2):
            copied(TRAN, tran_free, "hid", j)
        b = take("s", SCORE, score_free, ("kvc", 0))
        for k in range(2):
            mm(sp_[b][:, 0:NG * NCMP], w2k[:, k, :, :].rearrange("p a d -> p (a d)"), hidkT[:, k, :],
               start=(k == 0), stop=(k == 1))
        for g in range(NG):
            for k in range(2):
                last = mm(sp_[b][:, 128 + g * ND:128 + (g + 1) * ND],
                          hidvT[:, k, g, :, :].rearrange("p a c -> p (a c)"), w2v[:, k, :],
                          start=(k == 0), stop=(k == 1))
        last.then_inc(score_done, 1)
        mem_keys(2)

        def cmp_T(t):
            pe.wait_ge(pc_ready, t + 1)
            transposes(("pc", t), four(pc[t % 2][:, :, :].rearrange("p h c -> p (h c)"), range(NG)))

        pe.wait_ge(kvcmp_ready, 1)
        for t in range(TT):
            for a in range(2):
                b = take("s", SCORE, score_free, ("sc", t, a))
                for i in range(NH // 2):
                    g = (2 * i + a) // HPG
                    last = mm(sp_[b][:, i * 32:i * 32 + NCMP], nqT[a * ND:(a + 1) * ND, i, t * P:(t + 1) * P],
                              kcmpT[a * ND:(a + 1) * ND, g * NCMP:(g + 1) * NCMP], start=True, stop=True)
                last.then_inc(score_done, 1)
            mem_keys(3 + t)
            if t >= 1:
                cmp_T(t - 1)
        mem_keys(KD - 1)
        cmp_T(TT - 1)

        banks, LAG = att_banks, 3

        def att_scores(n):
            _, h, br, q = ATT[n]
            if n >= 4:
                pe.wait_ge(exp_ready, n - 3)
            mm(banks[n % 4][:, 0:(q + 1) * P], nqrT[:, h // 2, q * P:(q + 1) * P],
               kT[br][:, h // HPG, h % 2, 0:(q + 1) * P], start=True, stop=False)
            mm(banks[n % 4][:, q * P:(q + 1) * P], ident_b[:, :], causal_b[:, :], start=False, stop=True).then_inc(att_scored, 1)

        def att_T(n):
            pe.wait_ge(prob_ready, n + 1)
            transposes(("pt", n), four(prob[n % 4][:, :], range(ATT[n][3] + 1)))

        def att_pv(group):
            pr, q = divmod(group, TT)
            if q == 0:
                take("o", OUTP, outp_free, ("nsa", pr))
            if group == 0:
                for t in range(2, TT):
                    copied(TRAN, tran_free, "pc", t)
            for i in (2, 3):
                copied(TRAN, tran_free, "pt", 4 * group + i)
            o = op[OUTP.no("nsa", pr) % 2]
            g, cols = 2 * pr // HPG, slice(q * P, (q + 1) * P)
            heads = [(h, o[ND * (h % 2):ND * (h % 2) + ND, cols]) for h in (2 * pr, 2 * pr + 1)]
            for h, dst in heads:
                mm(dst, vcmp[:, h % HPG, g, :], pcT[:, g, cols], start=True, stop=False)
            for br in range(2):
                for k in range(q + 1):
                    for h, dst in heads:
                        last = mm(dst, vsw[:, br, k, g * ND:(g + 1) * ND], PT[(4 * group + 2 * br + h % 2) % 8][:, k, :],
                                  start=False, stop=(br == 1 and k == q))
            last.then_inc(pv_done_at(group)[0], 1)

        pe.wait_ge(mask_made, 2)
        for t in range(2):
            copied(SCORE, score_free, "sc", TT - 1, t)
            copied(PROJ, proj_free, "xk", KD - 1 - t)
        for n in range(len(ATT) + LAG + 1):
            if n < len(ATT):
                att_scores(n)
            if LAG <= n < len(ATT) + LAG:
                att_T(n - LAG)
            if n >= LAG + 1 and (n - LAG - 1) % 4 == 3:
                att_pv((n - LAG - 1) // 4)

        def norm_T(which, kind, t):
            pe.wait_ge(ln_ready, TT * which + t + 1)
            for j in range(2):
                transposes((kind, t, j), four(xres[:, t, :], range(4 * j, 4 * j + 4)))

        def norm_copied(kind, t):
            for j in range(2):
                m = TRAN.no(kind, t, j)
                pe.wait_ge(tran_free[m % 2], m // 2 + 1)

        w = [chunk_parts(("out", n))[0] for n in range(2)]
        for n in range(2):
            pe.wait_ge(*chunk_loaded(("out", n)))
        for b in range(2):
            pe.wait_ge(outp_free[b], (RH + NH // 2) // 2)
        def mixed_out(t):
            for n in range(2):
                b = take("p", PROJ, proj_free, ("out", t, n))
                for k in range(KD):
                    last = mm(pp[b][:, :], mixT[:, k, t * P:(t + 1) * P], w[n][:, k, :], start=(k == 0), stop=(k == KD - 1))
                last.then_inc(proj_done, 1)

        mixed_out(0)
        for t in range(1, TT):
            mixed_out(t)
            if t < TT - 1:
                norm_T(0, "x1", t - 1)
        norm_T(0, "x1", TT - 2)
        for m in range(2):
            mem_values(0, m)
        norm_T(0, "x1", TT - 1)
        for m in range(2):
            mem_values(1, m)
        norm_copied("x1", TT - 1)
        for c in range(2):
            w = chunk_parts(("xq", c))[0]
            pe.wait_ge(*chunk_loaded(("xq", c)))
            for d in range(4):
                b = take("p", PROJ, proj_free, ("xq", 4 * c + d))
                for k in range(KD):
                    last = mm(pp[b][:, :], w[:, k, d * P:(d + 1) * P], x1T[:, k, :], start=(k == 0), stop=(k == KD - 1))
                last.then_inc(proj_done, 1)
        for d in range(KD - 2, KD):
            m = PROJ.no("xq", d)
            pe.wait_ge(proj_free[m % 2], m // 2 + 1)

        XU, LAG_X = [(h, t) for h in range(XH) for t in range(TT)], 3

        def x_pv(h):
            for i in range(2):
                m = TRAN.no("px", h, TT - 1 - i)
                pe.wait_ge(tran_free[m % 2], m // 2 + 1)
            for d in range(2):
                b = take("o", OUTP, outp_free, ("x", h, d))
                for m in range(2):
                    last = mm(op[b][:, :], vx[:, m, (2 * h + d) * P:(2 * h + d + 1) * P], PX[h % 2][:, m, :],
                              start=(m == 0), stop=(m == 1))
                last.then_inc(outp_done, 1)

        for n in range(len(XU) + LAG_X + 1):
            if n < len(XU):
                h, t = XU[n]
                if n >= 4:
                    pe.wait_ge(xexp_ready, n - 3)
                for d in range(2):
                    last = mm(att_banks[n % 4][:, 0:MEM], xqT[:, 2 * h + d, t * P:(t + 1) * P], kxT[:, 2 * h + d, :],
                              start=(d == 0), stop=(d == 1))
                last.then_inc(x_scored, 1)
            if LAG_X <= n < len(XU) + LAG_X:
                h, t = XU[n - LAG_X]
                pe.wait_ge(xprob_ready, n - LAG_X + 1)
                transposes(("px", h, t), four(probx[(n - LAG_X) % 4][:, :], range(2)))
            if n >= LAG_X + 1 and (n - LAG_X - 1) % TT == TT - 1:
                x_pv((n - LAG_X - 1) // TT)

        w = [chunk_parts(("xo", n))[0] for n in range(2)]
        for n in range(2):
            pe.wait_ge(*chunk_loaded(("xo", n)))
        for b in range(2):
            pe.wait_ge(outp_free[b], OUTP.n // 2)
        def x_output(t, halves=range(2)):
            for n in halves:
                b = take("p", PROJ, proj_free, ("xo", t, n))
                for k in range(KD):
                    last = mm(pp[b][:, :], xoT[:, k, t * P:(t + 1) * P], w[n][:, k, :], start=(k == 0), stop=(k == KD - 1))
                last.then_inc(proj_done, 1)

        def logits(t):
            norm_copied("x2", t)
            if t == 0:
                pe.wait_ge(route_in, 64)
            b = take("s", SCORE, score_free, ("logit", t))
            for k in range(KD):
                last = mm(sp_[b][:, 0:NE], x2T[:, k, t * P:(t + 1) * P], wrt[:, k, :], start=(k == 0), stop=(k == KD - 1))
            last.then_inc(score_done, 1)

        wg = chunk_parts(("sgu", 0))[0]
        wd = chunk_parts(("sdn", 0))[0]

        def shared_up(t):
            if t == 0:
                pe.wait_ge(*chunk_loaded(("sgu", 0)))
            b = take("p", PROJ, proj_free, ("sgu", t))
            for k in range(KD):
                last = mm(pp[b][:, :], x2T[:, k, t * P:(t + 1) * P], wg[:, :, k, :], start=(k == 0), stop=(k == KD - 1))
            last.then_inc(proj_done, 1)

        def shared_T(t):
            pe.wait_ge(sact_ready, t + 1)
            transposes(("sh", t), four(sact[:, t, :], range(2)))

        def shared_down(t):
            m = TRAN.no("sh", t)
            pe.wait_ge(tran_free[m % 2], m // 2 + 1)
            for n in range(2):
                b = take("p", PROJ, proj_free, ("sdn", t, n))
                for k in range(2):
                    last = mm(pp[b][:, :], sactT[:, k, t * P:(t + 1) * P], wd[:, k, n * 512:(n + 1) * 512],
                              start=(k == 0), stop=(k == 1))
                last.then_inc(proj_done, 1)

        x_output(0)
        x_output(1)
        for t in range(2, TT):
            norm_T(1, "x2", t - 2)
            x_output(t, [0])
            logits(t - 2)
            x_output(t, [1])
        norm_T(1, "x2", TT - 2)
        shared_up(0)
        logits(TT - 2)
        norm_T(1, "x2", TT - 1)
        shared_up(1)
        logits(TT - 1)
        shared_up(2)
        shared_T(0)
        shared_up(3)
        shared_T(1)

        def number_rows(bank):
            for t in range(TT):
                last = mm(bank[0:BLK, 0:5], onehot[:, t, :], info[:, t, 0:5], start=(t == 0), stop=(t == TT - 1))
            return last

        tri, one = rcon[:, R_TRI:R_TRI + P], rcon[:, R_ONE:R_ONE + P]
        pe.wait_ge(mask_ready, TT)
        b = take("s", SCORE, score_free, ("pos", 0))
        for t in range(TT):
            for u in range(t + 1):
                mm(sp_[b][:, t * NE:(t + 1) * NE], tri if u == t else one, maskt[:, u, :], start=(u == 0), stop=(u == t))
        for u in range(TT):
            last = mm(sp_[b][0:NE, 384:385], maskt[:, u, :], one[:, 0:1], start=(u == 0), stop=(u == TT - 1))
        last.then_inc(score_done, 1)
        shared_T(2)
        shared_T(3)
        pe.wait_ge(hot_ready, 1)
        number_rows(op[1]).then_inc(idx_done, 1)
        pe.wait_ge(*chunk_loaded(("sdn", 0)))
        shared_down(0)
        pe.wait_ge(extra_ready, 1)
        b = take("s", SCORE, score_free, ("extra", 0))
        ecol = rsmall[0:NE, 512:513]
        mm(sp_[b][0:NE, 0:1], rcon[0:NE, R_TRI64:R_TRI64 + NE], ecol, start=True, stop=True)
        mm(sp_[b][:, 1:2], rcon[0:NE, R_ONE:R_ONE + P], ecol, start=True, stop=True).then_inc(score_done, 1)
        shared_down(1)
        pe.wait_ge(hot_ready, 2)
        pe.wait_ge(idx_ready, 1)
        number_rows(op[1]).then_inc(idx_done, 1)
        pe.wait_ge(extra_ready, 2)
        b = take("s", SCORE, score_free, ("cum", 0))
        ended = rsmall[0:NE, 640:640 + EXTRA]
        mm(sp_[b][:, 0:EXTRA], rcon[0:NE, R_ONE:R_ONE + P], ended, start=True, stop=True)
        mm(sp_[b][:, 64:64 + EXTRA], rsmall[0:NE, 768:768 + P], ended, start=True, stop=True).then_inc(score_done, 1)
        shared_down(2)
        shared_down(3)

        hps, yps, eTps, idx_ps = pp[0], op, sp_[0], sp_[1]

        def rows_T(b):
            for k in range(KD):
                last = nc.tensor.transpose(tp[k // 4][:, (k % 4) * P:(k % 4) * P + BLK], xg[b][0:BLK, k:D:KD],
                                           ident[0:BLK, 0:BLK])
            return last

        def down(b):
            for n in range(2):
                for k in range(2):
                    last = mm(yps[n][0:BLK, :], eactT[:, k, :], wdown[b][:, k, n * 512:(n + 1) * 512],
                              start=(k == 0), stop=(k == 1))
            last.then_inc(y_done, 1)

        pe.wait_ge(gathered[0], 16)
        rows_T(0).then_inc(xgT_done, 1)
        pe.wait_ge(e_dn_in[3], 32)
        for b in range(2):
            pe.wait_ge(proj_free[b], PROJ.n // 2)
            pe.wait_ge(score_free[b], (SCORE.n + 1 - b) // 2)
        pe.wait_ge(idx_ready, 2)
        pe.wait_ge(list_ready, 1)
        turns_n = pe.value_load(itabi[0:1, ITEMS:ITEMS + 1], min_val=NE // SETS, max_val=MAX_TURNS)
        with pe.Fori(0, turns_n) as j:
            for b in range(SETS):
                pe.wait_ge(e_gu_in[b], j * 32 + 32)
                pe.wait_ge(xgT_a, j * SETS + (b + 1))
                pe.wait_ge(xgT_d, j * SETS + (b + 1))
                for k in range(KD):
                    last = mm(hps[0:BLK, :], xgT[:, k, :], gu[b][:, :, k, :], start=(k == 0), stop=(k == KD - 1))
                last.then_inc(h_done, 1)
                pe.wait_ge(hot_ready, j * SETS + (b + 3))
                number_rows(idx_ps).then_inc(idx_done, 1)
                pe.wait_ge(gathered[1 - b % 2], j * 32 + 16 * ((b + 1) // 2 + 1))
                rows_T(1 - b % 2).then_inc(xgT_done, 1)
                pe.wait_ge(eT_ready, j * SETS + (b + 1))
                pe.wait_ge(e_dn_in[(b - 1) % SETS], j * 16 + 16)
                pe.wait_ge(y_act, j * SETS + (b + 1))
                pe.wait_ge(y_dve, j * SETS + (b + 1))
                down((b - 1) % SETS)
                pe.wait_ge(eact_ready, j * SETS + (b + 1))
                for k in range(2):
                    last = nc.tensor.transpose(eTps[:, k * P:k * P + BLK], eact[0:BLK, k:FF:2], ident[0:BLK, 0:BLK])
                last.then_inc(eT_done, 1)
        pe.wait_ge(e_dn_in[SETS - 1], turns_n * 16 + 16)
        pe.wait_ge(eT_ready, turns_n * SETS + 1)
        pe.wait_ge(y_act, turns_n * SETS + 1)
        pe.wait_ge(y_dve, turns_n * SETS + 1)
        down(SETS - 1)

    @block.scalar
    def _(act):
        steps = [0]

        def link(ins):
            steps[0] += 1
            ins.then_inc(act_step, 1)
            act.wait_ge(act_step, steps[0])

        def take(units, done, free, *name):
            wait_done(act, units, done, *name)
            return units.no(*name) % 2

        def copy_T(name, dst, src=None, scale=1.0):
            b = take(TRAN, tran_done, tran_free, *name)
            src = src(tp[b]) if src else tp[b][:, :].rearrange("p (k t) -> p k t", k=4)
            nc.scalar.activation(dst, src, ACT.Copy, scale=scale).then_inc(tran_free[b], 1)

        def part(n):
            return lambda bank: bank[:, 0:n * P].rearrange("p (k t) -> p k t", k=n)

        def x_T(t):
            for j in range(2):
                copy_T(("x", t, j), xT[:, 4 * j:4 * j + 4, t * P:(t + 1) * P])

        def ret_T(c, t):
            copy_T(("ret", c, t), retT[c][:, :, t * P:(t + 1) * P])

        x_T(0)
        act.wait_ge(angles_ready, 1)
        nc.scalar.activation(tab[:, :, :, :], turns[:, :, :, :], ACT.Sin).then_inc(tables_ready, 1)
        x_T(1)
        x_T(2)
        ret_T(0, 0)
        x_T(3)
        for c, t in STAGED[1:2 * TT - 1]:
            ret_T(c, t)
        for t in range(TT):
            b = take(PROJ, proj_done, proj_free, "in", 2, t)
            nc.scalar.activation(rv[:, t, :], pp[b][:, :], ACT.Copy).then_inc(proj_free[b], 1)
            if t == 0:
                ret_T(1, TT - 1)
        for t in range(TT):
            b = take(PROJ, proj_done, proj_free, "in", 3, t)
            nc.scalar.activation(swish[:, t, :], pp[b][:, :], ACT.Silu).then_inc(proj_free[b], 1)

        def nq_copies(t):
            n = stage_no(4, t)
            stage_free(act, n)
            b = take(PROJ, proj_done, proj_free, "in", 4, t)
            nc.scalar.activation(stage[n % 2][:, 0:512], pp[b][:, :], ACT.Copy)
            nc.scalar.activation(stage[n % 2][:, 512:1024], pp[b][:, :], ACT.Copy).then_inc(raw_staged, 1)

        def twice(v):
            return v.rearrange("p (g o d) -> p g o d", o=1, d=ND).to_broadcast([P, v.shape[1] // ND, 2, ND])

        def kv5_copies(t):
            n = stage_no(5, t)
            stage_free(act, n)
            b = take(PROJ, proj_done, proj_free, "in", 5, t)
            dst = stage[n % 2][:, 0:768].rearrange("p (g a d) -> p g a d", a=2, d=ND)
            for a in range(2):
                nc.scalar.activation(dst[:, :, a, :], pp[b][:, 0:384].rearrange("p (g d) -> p g d", d=ND), ACT.Copy)
            nc.scalar.activation(vsw[:, 0, t, :], pp[b][:, 384:512], ACT.Copy).then_inc(raw_staged, 1)

        def kv6_copies(t):
            n = stage_no(6, t)
            stage_free(act, n)
            b = take(PROJ, proj_done, proj_free, "in", 6, t)
            dst = stage[n % 2][:, 0:256].rearrange("p (g a d) -> p g a d", a=2, d=ND)
            for a in range(2):
                nc.scalar.activation(dst[:, :, a, :], pp[b][:, 0:128].rearrange("p (g d) -> p g d", d=ND), ACT.Copy)
            nc.scalar.activation(vsw[:, 1, t, :], pp[b][:, 128:256], ACT.Copy)
            nc.scalar.activation(gate[:, t, :], pp[b][:, 256:280], ACT.Sigmoid).then_inc(raw_staged, 1)

        def nq_T(t):
            copy_T(("nq", t, 0), nqT[:, :, t * P:(t + 1) * P], scale=ND ** -0.5)
            copy_T(("nq", t, 1), nqrT[:, :, t * P:(t + 1) * P], scale=ND ** -0.5)

        def key_T(name, br, t):
            if (br, t) == (0, 0):
                act.wait_ge(pads_ready, 4)
            b = take(TRAN, tran_done, tran_free, *name)
            for half in range(2):
                rows = slice(ND * half, ND * half + ND)
                last = nc.scalar.activation(kT[br][rows, :, half, t * P:(t + 1) * P], part(2)(tp[b])[rows], ACT.Copy)
            last.then_inc(tran_free[b], 1)

        def kv5_T(t):
            copy_T(("kv5", t, 0), kvcT[:, :, t * P:(t + 1) * P])
            key_T(("kv5", t, 1), 0, t)

        def kv6_T(t):
            key_T(("kv6", t), 1, t)

        def head_std(h):
            act.wait_ge(rstd_asked, h + 1)
            nc.scalar.activation(std[:, :], mv[:, :, 1], ACT.Sqrt, bias=eps).then_inc(rstd_ready, 1)

        for t in range(TT):
            if t >= 1:
                head_std(t - 1)
            nq_copies(t)
            if t >= 1:
                nq_T(t - 1)
        head_std(RH - 1)
        kv5_copies(0)
        nq_T(TT - 1)
        for t in range(TT):
            copy_T(("oret", t), mixT[:, 0:4, t * P:(t + 1) * P])
        for n in range(stage_no(5, 1), len(STAGED)):
            (kv5_copies if STAGED[n][0] == 5 else kv6_copies)(STAGED[n][1])
            (kv5_T if STAGED[n - 1][0] == 5 else kv6_T)(STAGED[n - 1][1])

        for j in range(2):
            b = take(SCORE, score_done, score_free, "hid", j)
            rows = slice(HALF * j, HALF * j + NG * NCMP)
            nc.scalar.activation(hid[rows, :], sp_[b][rows, 0:CMP_HID], ACT.Silu).then_inc(hid_ready, 1)
            act.wait_ge(hid_ready, j + 1)
            act.sem_inc(score_free[b], 1)
        kv6_T(TT - 1)
        for m in range(2):
            for j in range(2):
                copy_T(("mem", m, j), memT[:, 4 * j:4 * j + 4, m * P:(m + 1) * P])
        copy_T(("hid", 0), hidkT[:, :, :], lambda bank: bank[:, 0:256].rearrange("p (k c) -> p k c", k=2)[:, :, 0:NG * NCMP])
        act.wait_ge(zeros_ready, 3)
        b = take(TRAN, tran_done, tran_free, "hid", 1)
        for k in range(2):
            for g in range(NG):
                last = nc.scalar.activation(
                    hidvT[:, k, g, :, 0:NCMP],
                    tp[b][:, k * P + g * NCMP:k * P + (g + 1) * NCMP].rearrange("p (o c) -> p o c", o=1)
                    .to_broadcast([P, HPG, NCMP]), ACT.Copy)
        last.then_inc(tran_free[b], 1)
        def mem_keys(d):
            b = take(PROJ, proj_done, proj_free, "xk", d)
            nc.scalar.activation(kxT[:, d, :], pp[b][:, 0:MEM], ACT.Copy, scale=(D // XH) ** -0.5).then_inc(proj_free[b], 1)

        def mem_values(n, m):
            b = take(PROJ, proj_done, proj_free, "xv", m, n)
            nc.scalar.activation(vx[:, m, n * 512:(n + 1) * 512], pp[b][:, :], ACT.Copy).then_inc(proj_free[b], 1)

        def cmp_T(t):
            copy_T(("pc", t), pcT[:, :, t * P:(t + 1) * P], part(2))

        mem_keys(0)
        mem_keys(1)
        b = take(SCORE, score_done, score_free, "kvc", 0)
        nc.scalar.activation(kcmpT[:, :], sp_[b][:, 0:NG * NCMP], ACT.Copy)
        act.wait_ge(zeros_ready, 4)
        for i in range(HPG):
            rows = slice(32 * i, 32 * i + 32)
            last = nc.scalar.activation(vcmp[rows, i, :, :], sp_[b][rows, 128:256].rearrange("p (g d) -> p g d", g=NG), ACT.Copy)
        last.then_inc(kvcmp_ready, 1)
        act.wait_ge(kvcmp_ready, 1)
        act.sem_inc(score_free[b], 1)
        mem_keys(2)
        for t in range(TT):
            act.wait_ge(pc_asked, t + 1)
            v = pc[t % 2][:, :, 0:NCMP]
            nc.scalar.activation(v, v, ACT.Exp).then_inc(pc_exp, 1)
            mem_keys(3 + t)
            if t >= 1:
                cmp_T(t - 1)
        mem_keys(KD - 1)
        cmp_T(TT - 1)

        def copy_pair(pr):
            b = take(OUTP, outp_done, outp_free, "nsa", pr)
            nc.scalar.activation(mixT[:, 4 + pr, :], op[b][:, :], ACT.Copy).then_inc(outp_free[b], 1)

        LAG = 3
        for n in range(len(ATT) + LAG):
            if n < len(ATT):
                q = ATT[n][3]
                act.wait_ge(max_ready, n + 1)
                if n >= 4:
                    wait_done(act, TRAN, tran_done, "pt", n - 4)
                nc.scalar.activation(prob[n % 4][:, 0:(q + 1) * P], att_banks[n % 4][:, 0:(q + 1) * P], ACT.Exp,
                                     bias=nmax[:, 0, n % 4:n % 4 + 1], accum_out=rsum[:, 0, n % 4:n % 4 + 1])\
                    .then_inc(exp_ready, 1)
            if n >= LAG:
                m = n - LAG
                q = ATT[m][3]
                if m % 4 == 0 and m >= 8:
                    act.wait_ge(*pv_done_at(m // 4 - 2))
                copy_T(("pt", m), PT[m % 8][:, 0:q + 1, :], part(q + 1))
                if m % (4 * TT) == 7 and m > 8:
                    copy_pair(m // (4 * TT) - 1)
        copy_pair(NH // 2 - 1)

        def std_of(which, t):
            act.wait_ge(var_ready, TT * which + t + 1)
            nc.scalar.activation(std[:, t:t + 1], mv[:, t, 1:2], ACT.Sqrt, bias=eps).then_inc(std_ready, 1)

        def norm_T(which, t):
            kind, dst = (("x1", x1T), ("x2", x2T))[which]
            for j in range(2):
                copy_T((kind, t, j), dst[:, 4 * j:4 * j + 4, t * P:(t + 1) * P])

        std_of(0, 0)
        for t in range(1, TT):
            std_of(0, t)
            norm_T(0, t - 1)
        for m in range(2):
            mem_values(0, m)
        norm_T(0, TT - 1)
        for m in range(2):
            mem_values(1, m)
        for d in range(KD):
            b = take(PROJ, proj_done, proj_free, "xq", d)
            nc.scalar.activation(xqT[:, d, :], pp[b][:, :], ACT.Copy).then_inc(proj_free[b], 1)

        def x_out(h):
            for d in range(2):
                b = take(OUTP, outp_done, outp_free, "x", h, d)
                nc.scalar.activation(xoT[:, 2 * h + d, :], op[b][:, :], ACT.Copy).then_inc(outp_free[b], 1)

        XU, LAG_X = [(h, t) for h in range(XH) for t in range(TT)], 3
        for n in range(len(XU) + LAG_X):
            if n < len(XU):
                act.wait_ge(xmax_ready, n + 1)
                if n >= 4:
                    wait_done(act, TRAN, tran_done, "px", *XU[n - 4])
                nc.scalar.activation(probx[n % 4][:, :], att_banks[n % 4][:, 0:MEM], ACT.Exp, bias=nmax[:, 0, n % 4:n % 4 + 1],
                                     accum_out=rsum[:, 0, n % 4:n % 4 + 1]).then_inc(xexp_ready, 1)
            if n >= LAG_X:
                h, t = XU[n - LAG_X]
                if t == 0 and h >= 2:
                    wait_done(act, OUTP, outp_done, "x", h - 2, 1)
                copy_T(("px", h, t), PX[h % 2][:, :, t * P:(t + 1) * P], part(2))
                if t == 1 and h >= 1:
                    x_out(h - 1)
        x_out(XH - 1)

        def router_score(t):
            b = take(SCORE, score_done, score_free, "logit", t)
            nc.scalar.activation(score[:, t, :], sp_[b][:, 0:NE], ACT.Sigmoid).then_inc(score_sig, 1)
            act.wait_ge(score_sig, t + 1)
            act.sem_inc(score_free[b], 1)

        def shared_gate(t):
            b = take(PROJ, proj_done, proj_free, "sgu", t)
            if t >= 1:
                act.wait_ge(sact_ready, t)
            nc.scalar.activation(sgate[:, :], pp[b][:, 0:FF], ACT.Silu).then_inc(sgate_ready, 1)

        def shared_T(t):
            copy_T(("sh", t), sactT[:, :, t * P:(t + 1) * P], part(2))

        for t in range(TT):
            std_of(1, t)
            if 1 <= t < TT - 1:
                norm_T(1, t - 1)
                router_score(t - 1)
        norm_T(1, TT - 2)
        shared_gate(0)
        router_score(TT - 2)
        norm_T(1, TT - 1)
        shared_gate(1)
        router_score(TT - 1)
        shared_gate(2)
        shared_T(0)
        shared_gate(3)
        for t in range(1, TT):
            shared_T(t)
        def half_T():
            nc.scalar.activation(xgT[:, 0:4, :], tp[0][:, :].rearrange("p (k t) -> p k t", k=4)[:, :, 0:BLK], ACT.Copy)\
                .then_inc(xgT_a, 1)

        def y_half(b, j):
            buf = (b + 1) % 2
            act.wait_ge(y_done, j * SETS + (b + 1))
            act.wait_ge(scattered[buf], j * 32 + 16 * (b // 2 + 1))
            act.wait_ge(w_ready, j * SETS + (b + 1))
            nc.scalar.activation(ysb[buf][0:BLK, 0:512], op[0][0:BLK, :], ACT.Copy, scale=wcur[buf][0:BLK, 0:1]).then_inc(y_act, 1)

        act.wait_ge(moe_set, 7)
        act.sem_inc(eT_ready, 1)
        act.sem_inc(y_act, 1)
        act.wait_ge(xgT_done, 1)
        half_T()
        act.wait_ge(list_ready, 1)
        turns_n = act.value_load(itabi[0:1, ITEMS:ITEMS + 1], min_val=NE // SETS, max_val=MAX_TURNS)
        with act.Fori(0, turns_n) as j:
            for b in range(SETS):
                act.wait_ge(h_done, j * SETS + (b + 1))
                nc.scalar.activation(egate[0:BLK, :], pp[0][0:BLK, 0:FF], ACT.Silu).then_inc(egate_ready, 1)
                act.wait_ge(xgT_done, j * SETS + (b + 2))
                half_T()
                y_half(b, j)
                act.wait_ge(eT_done, j * SETS + (b + 1))
                nc.scalar.activation(eactT[:, :, :], sp_[0][:, 0:2 * P].rearrange("p (k t) -> p k t", k=2)[:, :, 0:BLK], ACT.Copy)\
                    .then_inc(eT_ready, 1)
        y_half(0, turns_n)
        for t in range(TT):
            std_of(2, t)

    @block.vector
    def _(dve):
        V = nc.vector
        steps = [0]

        def mark(ins):
            steps[0] += 1
            return ins.then_inc(dve_step, 1)

        def link(ins=None):
            if ins is not None:
                mark(ins)
            dve.wait_ge(dve_step, steps[0])

        for keys in kT:
            V.memset(keys[ND:P, :, 0, :], 0.0).then_inc(pads_ready, 1)
            V.memset(keys[0:ND, :, 1, :], 0.0).then_inc(pads_ready, 1)
        M, TWO_PI = 1.5 * 2.0 ** 23, 2 * np.pi
        A1 = 6.28125
        A2 = float(np.float32(np.floor((TWO_PI - A1) * 2 ** 21) / 2 ** 21))
        A3 = float(TWO_PI - A1 - A2)
        dve.wait_ge(const_in, 16)
        V.tensor_copy(ident_b[:, :], ident).then_inc(mask_made, 1)
        V.tensor_copy(causal_b[:, :], c1[:, C_CAUS:C_CAUS + P]).then_inc(mask_made, 1)
        dve.wait_ge(pos_in, 16)
        link(V.tensor_copy(posf[:, :], posi[:, :]))
        link(V.tensor_tensor(ang[:, :, :], posf[:, :].rearrange("p (t o) -> p t o", o=1).to_broadcast([P, TT, NFREQ]),
                             c1[:, C_INV:C_INV + NFREQ].rearrange("p (o f) -> p o f", o=1).to_broadcast([P, TT, NFREQ]),
                             ALU.mult))
        n_turns = oret[:, 0:2, 0:TT * NFREQ]
        for s in range(2):
            link(V.tensor_scalar(n_turns[:, s, :], ang[:, :, :].rearrange("p t f -> p (t f)"), float(1 / TWO_PI), 0.25 * s, ALU.mult, ALU.add))
        link(V.tensor_scalar(n_turns, n_turns, M, None, ALU.add))
        link(V.tensor_scalar(n_turns, n_turns, M, None, ALU.subtract))
        for s in range(2):
            flat = turns[:, s, :, :].rearrange("p t f -> p (t f)")
            src = ang[:, :, :].rearrange("p t f -> p (t f)")
            for a in (A1, A2, A3):
                link(V.scalar_tensor_tensor(out=flat, in0=n_turns[:, s, :], scalar=-a, in1=src, op0=ALU.mult, op1=ALU.add))
                src = flat
        link(V.tensor_scalar(turns[:, 1, :, :], turns[:, 1, :, :], float(np.pi / 2), None, ALU.add))
        PI = 3.1415925
        V.tensor_scalar(turns[:, :, :, :], turns[:, :, :, :], -PI, PI, ALU.max, ALU.min).then_inc(angles_ready, 1)
        dve.wait_ge(tables_ready, 1)

        for c in range(2):
            for t in range(TT):
                n = stage_no(c, t)
                b = PROJ.no("in", c, t) % 2
                wait_done(dve, PROJ, proj_done, "in", c, t)
                stage_free(dve, n)
                src = pp[b][:, :].rearrange("p (h f) -> p h f", f=RROT)
                dst = stage[n % 2][:, 0:512].rearrange("p (h a f) -> p h a f", a=2, f=RROT)
                for s in range(2):
                    tb = tab[:, s, t, 0:RROT].rearrange("p (o f) -> p o f", o=1).to_broadcast([P, 2 * RH, RROT])
                    ins = V.tensor_tensor(rott[:, s, :].rearrange("p (h f) -> p h f", f=RROT), src, tb, ALU.mult)
                    mark(ins)
                link()
                rs = rott[:, 0, :].rearrange("p (h a f) -> p h a f", a=2, f=RROT)
                rc = rott[:, 1, :].rearrange("p (h a f) -> p h a f", a=2, f=RROT)
                mark(V.tensor_tensor(dst[:, :, 0, :], rc[:, :, 0, :], rs[:, :, 1, :], ALU.subtract))
                V.tensor_tensor(dst[:, :, 1, :], rc[:, :, 1, :], rs[:, :, 0, :], ALU.add).then_inc(staged, 1)
                dve.wait_ge(staged, n + 1)
                dve.sem_inc(proj_free[b], 1)

        def ret_decay(h):
            if h >= 1:
                wait_done(dve, OUTP, outp_done, "ret", h - 1)
            for k in range(TT):
                b = SCORE.no("ret", h, k) % 2
                wait_done(dve, SCORE, score_done, "ret", h, k)
                n = T - k * P
                V.tensor_tensor(retS[:, k, 0:n], sp_[b][:, 0:n], decay[:, h, 0:n], ALU.mult).then_inc(rets_ready, 1)
                dve.wait_ge(rets_ready, TT * h + k + 1)
                dve.sem_inc(score_free[b], 1)

        def ret_norm(h):
            b = OUTP.no("ret", h) % 2
            wait_done(dve, OUTP, outp_done, "ret", h)
            for q in range(TT):
                mark(V.bn_stats(stat[:, q, :], op[b][:, q * P:(q + 1) * P]))
            link()
            for q in range(TT):
                last = V.bn_aggr(mv[:, q, :], stat[:, q, :])
                if q < TT - 1:
                    mark(last)
            last.then_inc(rstd_asked, 1)
            dve.wait_ge(rstd_ready, h + 1)
            dve.wait_ge(rstd_asked, h + 1)
            link(V.reciprocal(rinv[:, 0, 0:TT], std[:, :]))
            for q in range(TT):
                mark(V.tensor_scalar(oret[:, q, h * RD:(h + 1) * RD], op[b][:, q * P:(q + 1) * P], mv[:, q, 0:1],
                                     rinv[:, 0, q:q + 1], ALU.subtract, ALU.mult))
            link()
            dve.sem_inc(outp_free[b], 1)
            if h == 0:
                for t in range(2, TT):
                    m = PROJ.no("in", 3, t)
                    dve.wait_ge(proj_free[m % 2], m // 2 + 1)
            V.tensor_tensor(oret[:, :, h * RD:(h + 1) * RD], oret[:, :, h * RD:(h + 1) * RD],
                            swish[:, :, h * RD:(h + 1) * RD], ALU.mult).then_inc(oret_ready, 1)

        def small_rotation(b, src_cols, heads, dst, t):
            src = pp[b][:, src_cols:src_cols + heads * ND].rearrange("p (h d) -> p h d", d=ND)[:, :, 0:2 * NROT]\
                .rearrange("p h (a f) -> p h a f", a=2)
            m = heads * 2 * NROT
            for s in range(2):
                for a in range(2):
                    tb = tab[:, s, t, RROT:NFREQ].rearrange("p (o f) -> p o f", o=1).to_broadcast([P, heads, NROT])
                    o = rottn[:, s, a * heads * NROT:(a + 1) * heads * NROT].rearrange("p (h f) -> p h f", h=heads)
                    mark(V.tensor_tensor(o, src[:, :, a, :], tb, ALU.mult))
            link()
            half = lambda s, a: rottn[:, s, a * heads * NROT:(a + 1) * heads * NROT].rearrange("p (h f) -> p h f", h=heads)
            for i, d in enumerate(dst):
                mark(V.tensor_tensor(d[:, :, 0:NROT], half(1, 0), half(0, 1), ALU.subtract))
                last = V.tensor_tensor(d[:, :, NROT:2 * NROT], half(1, 1), half(0, 0), ALU.add)
                if i < len(dst) - 1:
                    mark(last)
            return last

        def rotated(c, t):
            n = stage_no(c, t)
            b = PROJ.no("in", c, t) % 2
            dve.wait_ge(raw_staged, n - 2 * TT + 1)
            st = stage[n % 2]
            if c == 4:
                last = small_rotation(b, 0, NH, [st[:, 512:1024].rearrange("p (h d) -> p h d", d=ND)], t)
            elif c == 5:
                v = st[:, 512:768].rearrange("p (g a d) -> p g a d", a=2, d=ND)
                last = small_rotation(b, 256, NG, [v[:, :, a, :] for a in range(2)], t)
            else:
                v = st[:, 0:256].rearrange("p (g a d) -> p g a d", a=2, d=ND)
                last = small_rotation(b, 0, NG, [v[:, :, a, :] for a in range(2)], t)
            last.then_inc(staged, 1)
            dve.wait_ge(staged, n + 1)
            dve.sem_inc(proj_free[b], 1)

        def cmp_blocks(j):
            for half in range(2):
                lo = ND * half
                for g in range(NG):
                    src = kvcT[lo:lo + ND, 2 * j + g, :]
                    for part in range(2):
                        blk = src[:, 16 * part:16 * part + 16 * NCMP].rearrange("p (c l a) -> p a l c", l=8, a=2)[:, half]
                        pe_v = pe2[lo:lo + ND, j, 8 * part:8 * part + 8].rearrange("p (l o) -> p l o", o=1)\
                            .to_broadcast([ND, 8, NCMP])
                        ins = V.tensor_tensor(ab[lo:lo + ND, j, 8 * part:8 * part + 8, g, :], blk, pe_v, ALU.add)
                        if (half, g, part) == (1, NG - 1, 1):
                            ins.then_inc(ab_ready, 1)
                        else:
                            mark(ins)

        dve.wait_ge(decay_in, 16)
        for h in range(RH):
            ret_decay(h)
            if h >= 1:
                ret_norm(h - 1)
            rotated(4, h)
        ret_norm(RH - 1)
        V.memset(hidvT[:, :, :, :, :], 0.0).then_inc(zeros_ready, 1)
        for i in range(2):
            V.memset(pc[i][:, :, :], 0.0).then_inc(zeros_ready, 1)
        for t in range(TT):
            rotated(5, t)
        for t in range(TT):
            rotated(6, t)
            if t == 0:
                dve.wait_ge(pe_in, 48)
                for i in range(2):
                    m = TRAN.no("kv5", TT - 1, i)
                    dve.wait_ge(tran_free[m % 2], m // 2 + 1)
            if t < 2:
                cmp_blocks(t)

        wait_done(dve, TRAN, tran_done, "hid", 1)
        V.memset(vcmp[:, :, :, :], 0.0).then_inc(zeros_ready, 1)
        for t in range(TT):
            if t >= 2:
                wait_done(dve, TRAN, tran_done, "pc", t - 2)
            v = pc[t % 2][:, :, 0:NCMP]
            bc = lambda a, n: ccmp[:, a, t, :].rearrange("p (o c) -> p o c", o=1).to_broadcast([P, n, NCMP])
            wide = lambda x: x.rearrange("p (h o) -> p h o", o=1).to_broadcast([P, NH, NCMP])
            for a in range(2):
                b = SCORE.no("sc", t, a) % 2
                wait_done(dve, SCORE, score_done, "sc", t, a)
                s = sp_[b][:, 0:NH // 2 * 32].rearrange("p (h c) -> p h c", c=32)[:, :, 0:NCMP]
                link(V.tensor_tensor(pc[t % 2][:, a:NH:2, 0:NCMP], s, bc(1, NH // 2), ALU.add))
                dve.sem_inc(score_free[b], 1)
            link(V.tensor_reduce(cmpm[:, :], v, AX.X, ALU.max))
            V.tensor_tensor(v, v, wide(cmpm[:, :]), ALU.subtract).then_inc(pc_asked, 1)
            dve.wait_ge(pc_exp, t + 1)
            link(V.tensor_reduce(cmpm[:, :], v, AX.X, ALU.add))
            link(V.reciprocal(cmpm[:, :], cmpm[:, :]))
            link(V.tensor_tensor(cmpm[:, :], cmpm[:, :], gate[:, t, 0:3 * NH:3], ALU.mult))
            link(V.tensor_tensor(v, v, bc(0, NH), ALU.mult))
            V.tensor_tensor(v, v, wide(cmpm[:, :]), ALU.mult).then_inc(pc_ready, 1)

        def scale_prob(n):
            _, h, br, q = ATT[n]
            col = slice(n % 4, n % 4 + 1)
            dve.wait_ge(exp_ready, n + 1)
            link(V.reciprocal(rinv[:, 0, col], rsum[:, 0, col]))
            v = prob[n % 4][:, 0:(q + 1) * P]
            V.tensor_scalar(v, v, rinv[:, 0, col], gate[:, q, 3 * h + 1 + br:3 * h + 2 + br], ALU.mult, ALU.mult)\
                .then_inc(prob_ready, 1)

        for n in range(len(ATT)):
            q = ATT[n][3]
            s = att_banks[n % 4]
            dve.wait_ge(att_scored, n + 1)
            V.tensor_reduce(nmax[:, 0, n % 4:n % 4 + 1], s[:, 0:(q + 1) * P], AX.X, ALU.max, negate=True).then_inc(max_ready, 1)
            if n >= 1:
                scale_prob(n - 1)
        scale_prob(len(ATT) - 1)

        def add_norm(which, kind, t):
            for n in range(2):
                b = PROJ.no(kind, t, n) % 2
                wait_done(dve, PROJ, proj_done, kind, t, n)
                half = xres[:, t, n * 512:(n + 1) * 512]
                link(V.scalar_tensor_tensor(out=half, in0=half, scalar=ALPHA, in1=pp[b][:, :], op0=ALU.mult, op1=ALU.add))
                dve.sem_inc(proj_free[b], 1)
                mark(V.bn_stats(stat[:, n, :], half))
            link()
            norm_rows(which, t, lng)

        def norm_rows(which, t, gains):
            x = xres[:, t, :]
            V.bn_aggr(mv[:, t, :], stat[:, 0:2, :].rearrange("p a b -> p (a b)")).then_inc(var_ready, 1)
            dve.wait_ge(std_ready, TT * which + t + 1)
            dve.wait_ge(var_ready, TT * which + t + 1)
            link(V.reciprocal(rinv[:, 0, t:t + 1], std[:, t:t + 1]))
            ins = V.tensor_scalar(x, x, mv[:, t, 0:1], rinv[:, 0, t:t + 1], ALU.subtract, ALU.mult)
            if which == 2 and t < POOL_TILES:
                ins.then_inc(normed, 1)
                return
            link(ins)
            dve.wait_ge(ln_in[which], 32)
            link(V.tensor_tensor(x, x, gains[:, 0, :], ALU.mult))
            done = ln_ready if which < 2 else fin_ready
            V.tensor_tensor(x, x, gains[:, 1, :], ALU.add).then_inc(done, 1)
            if which < 2:
                dve.wait_ge(done, TT * which + t + 1)

        for t in range(TT):
            add_norm(0, "out", t)

        def scale_x(n):
            dve.wait_ge(xexp_ready, n + 1)
            col = slice(n % 4, n % 4 + 1)
            link(V.reciprocal(rinv[:, 0, col], rsum[:, 0, col]))
            V.tensor_scalar(probx[n % 4][:, :], probx[n % 4][:, :], rinv[:, 0, col], None, ALU.mult)\
                .then_inc(xprob_ready, 1)

        for n in range(XH * TT):
            dve.wait_ge(x_scored, n + 1)
            V.tensor_reduce(nmax[:, 0, n % 4:n % 4 + 1], att_banks[n % 4][:, 0:MEM], AX.X, ALU.max, negate=True)\
                .then_inc(xmax_ready, 1)
            if n >= 1:
                scale_x(n - 1)
        scale_x(XH * TT - 1)
        for b in range(2):
            V.memset(xg[b][:, :], 0.0).then_inc(moe_set, 1)
            V.memset(ysb[b][:, :], 0.0).then_inc(moe_set, 1)
            mark(V.memset(smid[b][:, :], OOB))
            V.memset(scur[b][:, :], int(OOB)).then_inc(moe_set, 1)
        dve.wait_ge(outp_done, OUTP.n)
        link(V.memset(eactT[:, :, :], 0.0))
        dve.sem_inc(moe_set, 1)

        bc = lambda x, shape, pat, **kw: x.rearrange(pat, **kw).to_broadcast(shape)
        iota64 = rcon[:, R_IOTA:R_IOTA + NE]

        def route(t):
            col = lambda i: rsmall[:, i * 8:(i + 1) * 8]
            gs, gsort, gok, gpen, top, tidf = (col(i) for i in range(6))
            tidx = col(6).bitcast(U32)
            ws = rsmall[:, 56:57]
            dve.wait_ge(score_sig, t + 1)
            link(V.tensor_tensor(biased[:, t, :], score[:, t, :], rbias[:, :], ALU.add))
            for g in range(GROUPS):
                mark(V.max(gtop[:, t, g, :], biased[:, t, g * EPG:(g + 1) * EPG]))
            link()
            link(V.tensor_tensor(gs, gtop[:, t, :, 0], gtop[:, t, :, 1], ALU.add))
            link(V.max(gsort, gs))
            link(V.tensor_scalar(gok, gs, gsort[:, TOPG - 1:TOPG], None, ALU.is_ge))
            link(V.tensor_scalar(gpen, gok, -1.0, -NEG, ALU.add, ALU.mult))
            m3 = lambda x: x.rearrange("p (g e) -> p g e", g=GROUPS)
            wide = lambda x: x.rearrange("p (g o) -> p g o", o=1).to_broadcast([P, GROUPS, EPG])
            link(V.tensor_tensor(m3(tmpa[:, t, :]), m3(biased[:, t, :]), wide(gok), ALU.mult))
            link(V.tensor_tensor(m3(tmpa[:, t, :]), m3(tmpa[:, t, :]), wide(gpen), ALU.add))
            link(V.max(top, tmpa[:, t, :]))
            link(V.max_index(tidx, top, tmpa[:, t, :]))
            link(V.tensor_copy(tidf, tidx))
            sh = [P, TOPK, NE]
            link(V.tensor_tensor(hot8[:, :, :], bc(iota64, sh, "p (o e) -> p o e", o=1),
                                 bc(tidf, sh, "p (k o) -> p k o", o=1), ALU.is_equal))
            V.tensor_reduce(maskt[:, t, :], hot8[:, :, :].rearrange("p k e -> p e k"), AX.X, ALU.add).then_inc(mask_ready, 1)
            dve.wait_ge(mask_ready, t + 1)
            link(V.tensor_tensor(wexp[:, t, :], score[:, t, :], maskt[:, t, :], ALU.mult))
            link(V.tensor_reduce(ws, wexp[:, t, :], AX.X, ALU.add))
            link(V.reciprocal(ws, ws))
            link(V.tensor_scalar(wexp[:, t, :], wexp[:, t, :], ws, SCALE_W, ALU.mult, ALU.mult))
            for i in range(3):
                link(V.tensor_copy(wpart[:, t, :, i], wexp[:, t, :]))
                if i < 2:
                    link(V.tensor_tensor(wexp[:, t, :], wexp[:, t, :], wpart[:, t, :, i], ALU.subtract))

        def shared_act(t):
            b = PROJ.no("sgu", t) % 2
            dve.wait_ge(sgate_ready, t + 1)
            V.tensor_tensor(sact[:, t, :], sgate[:, :], pp[b][:, FF:2 * FF], ALU.mult).then_inc(sact_ready, 1)
            dve.wait_ge(sact_ready, t + 1)
            dve.sem_inc(proj_free[b], 1)

        def shared_add(t):
            dve.wait_ge(x2_saved, 16 * TT)
            for n in range(2):
                b = PROJ.no("sdn", t, n) % 2
                wait_done(dve, PROJ, proj_done, "sdn", t, n)
                half = xres[:, t, n * 512:(n + 1) * 512]
                V.scalar_tensor_tensor(out=half, in0=half, scalar=ALPHA, in1=pp[b][:, :], op0=ALU.mult, op1=ALU.add)\
                    .then_inc(half_added, 1)
                dve.wait_ge(half_added, 2 * t + n + 1)
                dve.sem_inc(proj_free[b], 1)
            dve.sem_inc(base_ready, 1)

        for t in range(TT):
            add_norm(1, "xo", t)
            if t == 0:
                dve.wait_ge(route_in, 64)
            if 1 <= t < TT - 1:
                route(t - 1)
        shared_act(0)
        route(TT - 2)
        shared_act(1)
        route(TT - 1)
        shared_act(2)
        shared_act(3)

        iota_b = mcon[:, :].rearrange("p (o s) -> p o s", o=1).to_broadcast([P, TT, BLK])

        def chain(ins, when):
            ins.then_inc(loop_step, 1)
            dve.wait_ge(loop_step, when)

        def one_hot(e, item, when):
            V.tensor_copy(info[:, :, 2:5].rearrange("p t (o s) -> p t o s", o=1), wpart[:, :, e, 0:3])
            chain(V.tensor_scalar(rel[:, :], posm[:, :, e], boff[:, item], None, ALU.subtract), when)
            V.tensor_tensor(onehot[:, :, :], iota_b,
                            rel[:, :].rearrange("p (t o) -> p t o", o=1).to_broadcast([P, TT, BLK]), ALU.is_equal)\
                .then_inc(hot_ready, 1)

        def row_numbers(b, when, bank):
            i = bank[0:BLK, :]
            chain(V.tensor_scalar(gfl[0:BLK, :], i[:, 0:1], OOB, i[:, 1:2], ALU.add, ALU.add), when)
            V.tensor_copy(gidx[b][0:BLK, :], gfl[0:BLK, :])
            V.tensor_copy(snext[b][0:BLK, 0:1], gfl[0:BLK, :])
            V.tensor_reduce(snext[b][0:BLK, 1:2], i[:, 2:5], AX.X, ALU.add).then_inc(idx_ready, 1)

        mark(V.tensor_copy(itab[:, 0:NE], rcon[:, R_IOTA:R_IOTA + NE]))
        mark(V.memset(boff[:, 0:NE], 0.0))
        mark(V.tensor_copy(info[:, :, 0], rcon[:, R_TOK:R_TOK + TT]))
        link(V.tensor_copy(info[:, :, 1], rcon[:, R_TOK + TT:R_TOK + 2 * TT]))

        wait_done(dve, SCORE, score_done, "pos", 0)
        b = SCORE.no("pos", 0) % 2
        link(V.tensor_scalar(tmpa[:, :, :], maskt[:, :, :], -1.0, FAR, ALU.add, ALU.mult))
        link(V.tensor_tensor(posm[:, :, :], sp_[b][:, 0:TT * NE].rearrange("p (t e) -> p t e", t=TT), tmpa[:, :, :], ALU.add))
        one_hot(slice(0, 1), slice(0, 1), 1)
        ecol, etmp = rsmall[0:NE, 512:513], rsmall[0:NE, 520:520 + MAX_BLOCKS - 1]
        for i in range(MAX_BLOCKS - 1):
            mark(V.tensor_scalar(etmp[:, i:i + 1], sp_[b][0:NE, 384:385], float(BLK * (i + 1)), None, ALU.is_gt))
        link()
        dve.sem_inc(score_free[b], 1)
        link(V.tensor_reduce(ecol, etmp, AX.X, ALU.add))
        V.tensor_copy(rsmall[0:NE, 768:768 + P], ecol.to_broadcast([NE, P])).then_inc(extra_ready, 1)
        dve.wait_ge(idx_done, 1)
        row_numbers(0, 2, op[1])
        shared_add(0)
        wait_done(dve, SCORE, score_done, "extra", 0)
        b = SCORE.no("extra", 0) % 2
        cum, n_extra = rsmall[0:NE, 516:517], rsmall[:, 517:518]
        mark(V.tensor_copy(cum, sp_[b][0:NE, 0:1]))
        link(V.tensor_copy(n_extra, sp_[b][:, 1:2]))
        dve.sem_inc(score_free[b], 1)
        V.tensor_scalar(rsmall[0:NE, 640:640 + EXTRA], rcon[0:NE, R_IOTA:R_IOTA + EXTRA], cum, None, ALU.is_ge)\
            .then_inc(extra_ready, 1)
        one_hot(slice(1, 2), slice(1, 2), 3)
        shared_add(1)
        dve.wait_ge(idx_done, 2)
        row_numbers(1, 4, op[1])
        wait_done(dve, SCORE, score_done, "cum", 0)
        b = SCORE.no("cum", 0) % 2
        link(V.tensor_scalar(itab[:, NE:ITEMS], sp_[b][:, 0:EXTRA], float(NE - 1), None, ALU.min))
        bx = boff[:, NE:ITEMS]
        past = rsmall[:, 704:704 + EXTRA]
        link(V.tensor_tensor(bx, rcon[:, R_IOTA:R_IOTA + EXTRA], sp_[b][:, 64:64 + EXTRA], ALU.subtract))
        link(V.tensor_scalar(bx, bx, 1.0, float(BLK), ALU.add, ALU.mult))
        link(V.tensor_scalar(past, rcon[:, R_IOTA:R_IOTA + EXTRA], n_extra, FAR, ALU.is_ge, ALU.mult))
        link(V.tensor_tensor(bx, bx, past, ALU.add))
        dve.sem_inc(score_free[b], 1)
        mark(V.tensor_copy(itabi[:, 0:ITEMS], itab[:, :]))
        n_turn = rsmall[:, 518:519]
        link(V.tensor_scalar(n_turn, n_extra, float(NE) + (SETS - 1) / 2, 1.0 / SETS, ALU.add, ALU.mult))
        link(V.tensor_scalar(n_turn, n_turn, M, M, ALU.add, ALU.subtract))
        link(V.tensor_copy(itabi[:, ITEMS:ITEMS + 1], n_turn))
        dve.sem_inc(list_ready, 1)

        def half_T():
            V.tensor_copy(xgT[:, 4:8, :], tp[1][:, :].rearrange("p (k t) -> p k t", k=4)[:, :, 0:BLK]).then_inc(xgT_d, 1)

        dve.wait_ge(list_ready, 1)
        shared_add(2)
        shared_add(3)

        def y_half(b, j):
            buf = (b + 1) % 2
            dve.wait_ge(scattered[buf], j * 32 + 16 * (b // 2 + 1))
            V.tensor_copy(scur[buf][:, :], smid[buf][:, 0:1])
            V.tensor_copy(wcur[buf][:, :], smid[buf][:, 1:2]).then_inc(w_ready, 1)
            dve.wait_ge(w_ready, j * SETS + (b + 1))
            dve.wait_ge(y_done, j * SETS + (b + 1))
            V.tensor_scalar(ysb[buf][0:BLK, 512:1024], op[1][0:BLK, :], wcur[buf][0:BLK, 0:1], None, ALU.mult).then_inc(y_dve, 1)

        dve.sem_inc(y_dve, 1)
        dve.wait_ge(xgT_done, 1)
        half_T()
        turns_n = dve.value_load(itabi[0:1, ITEMS:ITEMS + 1], min_val=NE // SETS, max_val=MAX_TURNS)
        with dve.Fori(0, turns_n) as j:
            for b in range(SETS):
                e = dve.value_load(itabi[0:1, DS(j * SETS + (b + 2), 1)], min_val=0, max_val=NE - 1)
                dve.wait_ge(idx_ready, j * SETS + (b + 2))
                dve.wait_ge(y_dve, j * SETS + (b + 1))
                V.tensor_copy(smid[b % 2][0:BLK, :], snext[b % 2][0:BLK, :]).then_inc(smid_ready, 1)
                one_hot(DS(e, 1), DS(j * SETS + (b + 2), 1), j * (2 * SETS) + (2 * b + 5))
                dve.wait_ge(h_done, j * SETS + (b + 1))
                dve.wait_ge(egate_ready, j * SETS + (b + 1))
                V.tensor_tensor(eact[0:BLK, :], egate[0:BLK, :], pp[0][0:BLK, FF:2 * FF], ALU.mult).then_inc(eact_ready, 1)
                dve.wait_ge(idx_done, j * SETS + (b + 3))
                dve.wait_ge(gathered[b % 2], j * 32 + 16 * (b // 2 + 1))
                dve.wait_ge(smid_ready, j * SETS + (b + 1))
                row_numbers(b % 2, j * (2 * SETS) + (2 * b + 6), sp_[1])
                dve.wait_ge(xgT_done, j * SETS + (b + 2))
                half_T()
                y_half(b, j)
        y_half(0, turns_n)

        for t in range(TT):
            dve.wait_ge(sum_in[t], 16)
            for n in range(2):
                mark(V.bn_stats(stat[:, n, :], xres[:, t, n * 512:(n + 1) * 512]))
            link()
            norm_rows(2, t, lng3)

    ctx.close()


_INS = ["x", "mem", "positions", "w_in", "cmp_pe_k", "cmp_pe_v", "cmp_w1_k", "cmp_w2_k", "cmp_w1_v", "cmp_w2_v",
        "w_out", "ln1_g", "ln1_b", "w_xq", "w_xkv", "w_xo", "ln2_g", "ln2_b", "w_router", "router_bias",
        "w_gate", "w_up", "w_down", "ws_gate", "ws_up", "ws_down", "ln3_g", "ln3_b"]


def kernel(**inputs):
    import numpy as _np
    import concourse.bacc as _bacc
    from concourse.bass_utils import run_bass_kernel_spmd as _run

    nc = _bacc.Bacc("TRN2", target_bir_lowering=False, num_devices=1)
    arrays = {f"in_{n}": _np.ascontiguousarray(inputs[n])[0] for n in _INS}
    arrays.update({f"in_{n}": a for n, a in constants().items()})
    io = {n[3:]: nc.dram_tensor(n, a.shape, mybir.dt.from_np(a.dtype), kind="ExternalInput").ap()
          for n, a in arrays.items()}
    out = nc.dram_tensor("out_0", (T, D), F32, kind="ExternalOutput").ap()
    build(nc, io, out)
    r = _run(nc, [arrays], core_ids=[0])
    return r.results[0]["out_0"].reshape(1, T, D)
```
